# Optimizing a Trainium2 kernel written in Bass

```python
import math
import jax
import jax.numpy as jnp
from jax import lax
import numpy as np

D_MODEL = 1024
BATCH = 1
SEQ = 256
DEPTH = 2
DEC_BATCH = 8
DEC_SEQ = 8
PAST_LEN = 2048
PAGE_SIZE = 128

N_A_LAYERS = DEPTH // 2
N_B_LAYERS = DEPTH - N_A_LAYERS

SSM_EXPAND = 2
D_INNER = SSM_EXPAND * D_MODEL
SSM_HEAD_DIM = 64
SSM_HEADS = D_INNER // SSM_HEAD_DIM
SSM_GROUPS = 8
SSM_HEADS_PER_GROUP = SSM_HEADS // SSM_GROUPS
D_STATE = 128
CONV_W = 4
CONV_DIM = D_INNER + 2 * SSM_GROUPS * D_STATE
IN_PROJ_DIM = D_INNER + CONV_DIM + SSM_HEADS
SSD_CHUNK = 128

HEAD_DIM = 64
DIL_PATTERNS = ((128, 1), (512, 4), (2048, 16))
N_DIL = len(DIL_PATTERNS)
HEADS_PER_BRANCH = D_MODEL // (2 * HEAD_DIM)
KV_PER_BRANCH = 2
Q_PER_KV = HEADS_PER_BRANCH // KV_PER_BRANCH
N_Q_HEADS = N_DIL * HEADS_PER_BRANCH
N_KV_HEADS = N_DIL * KV_PER_BRANCH
ATTN_OUT_DIM = HEADS_PER_BRANCH * HEAD_DIM
WIN_MAX = max(w for w, _ in DIL_PATTERNS)
WIN_BUF = min(WIN_MAX, PAST_LEN)
ROPE_DIM = HEAD_DIM // 4
ROPE_THETA = 500000.0
Q_BLOCK = 128

PEER_HEADS = 8
PEER_N_KEYS = 128
PEER_N_EXPERTS = PEER_N_KEYS * PEER_N_KEYS
PEER_TOPK = 16
PEER_QUERY_DIM = 256
PEER_HALF = PEER_QUERY_DIM // 2
PEER_TOKEN_BLOCK = 256

PLE_DIM = 256
EPS = 1e-6

kernel_name = 'yoco_ssd_dilated_peer_step'

def rmsnorm(x, g):
    xf = x.astype(jnp.float32)
    y = xf * lax.rsqrt(jnp.mean(xf * xf, axis=-1, keepdims=True) + EPS)
    return (y * g.astype(jnp.float32)).astype(x.dtype)

def rope_partial(x, pos):
    half = ROPE_DIM // 2
    inv = ROPE_THETA ** (-jnp.arange(0, ROPE_DIM, 2, dtype=jnp.float32) / ROPE_DIM)
    ang = pos.astype(jnp.float32)[:, None] * inv[None, :]
    cos = jnp.cos(ang)[None, :, None, :]
    sin = jnp.sin(ang)[None, :, None, :]
    xr = x[..., :ROPE_DIM].astype(jnp.float32)
    x1, x2 = xr[..., :half], xr[..., half:]
    rot = jnp.concatenate([x1 * cos - x2 * sin, x2 * cos + x1 * sin], axis=-1)
    return jnp.concatenate([rot.astype(x.dtype), x[..., ROPE_DIM:]], axis=-1)

def causal_conv(xbc, buf, w, b):
    xp = jnp.concatenate([buf.astype(xbc.dtype), xbc], axis=1)
    y = lax.conv_general_dilated(xp, w[:, None, :].astype(xp.dtype), window_strides=(1,), padding='VALID',
                                 dimension_numbers=('NWC', 'WIO', 'NWC'), feature_group_count=CONV_DIM)
    return y + b.astype(y.dtype), xp[:, -(CONV_W - 1):]

def ssd_scan(xs, dt, a, bm, cm, h0):
    f32 = jnp.float32
    b_, t_ = xs.shape[:2]
    L = SSD_CHUNK if t_ % SSD_CHUNK == 0 else t_
    nc = t_ // L
    G, HG, P, N = SSM_GROUPS, SSM_HEADS_PER_GROUP, SSM_HEAD_DIM, D_STATE

    def chunks(z):
        return jnp.swapaxes(z.reshape((b_, nc, L) + z.shape[2:]), 0, 1)

    xdt = chunks((xs.astype(f32) * dt[..., None]).reshape(b_, t_, G, HG, P))
    da = chunks((dt * a).reshape(b_, t_, G, HG))
    bc = chunks(bm.astype(f32))
    cc = chunks(cm.astype(f32))
    causal = jnp.tril(jnp.ones((L, L), dtype=bool))[None, :, :, None, None]

    def step(h, inp):
        xdt_c, da_c, b_c, c_c = inp
        cum = jnp.cumsum(da_c, axis=1)
        seg = cum[:, :, None] - cum[:, None, :]
        decay = jnp.exp(jnp.where(causal, seg, -jnp.inf))
        cb = jnp.einsum('btgn,bsgn->btsg', c_c, b_c)
        y = jnp.einsum('btsgh,bsghp->btghp', cb[..., None] * decay, xdt_c)
        y = y + jnp.einsum('btgn,bghpn->btghp', c_c, h) * jnp.exp(cum)[..., None]
        tail = jnp.exp(cum[:, -1:] - cum)
        h = h * jnp.exp(cum[:, -1])[..., None, None] + jnp.einsum('bsgn,bsgh,bsghp->bghpn', b_c, tail, xdt_c)
        return h, y

    h_fin, ys = lax.scan(step, h0.astype(f32).reshape(b_, G, HG, P, N), (xdt, da, bc, cc))
    y = jnp.swapaxes(ys, 0, 1).reshape(b_, t_, SSM_HEADS, P)
    return y, h_fin.reshape(b_, SSM_HEADS, P, N)

def mamba_mixer(u, conv_buf, h0, w_in, conv_w, conv_b, dt_bias, a_log, d_skip, norm_g, w_out):
    f32 = jnp.float32
    b_, t_, _ = u.shape
    zxbcdt = u @ w_in
    z = zxbcdt[..., :D_INNER]
    xbc = zxbcdt[..., D_INNER:D_INNER + CONV_DIM]
    dt = zxbcdt[..., D_INNER + CONV_DIM:]
    xbc, new_buf = causal_conv(xbc, conv_buf, conv_w, conv_b)
    xbc = jax.nn.silu(xbc)
    gn = SSM_GROUPS * D_STATE
    xs = xbc[..., :D_INNER].reshape(b_, t_, SSM_HEADS, SSM_HEAD_DIM)
    bm = xbc[..., D_INNER:D_INNER + gn].reshape(b_, t_, SSM_GROUPS, D_STATE)
    cm = xbc[..., D_INNER + gn:].reshape(b_, t_, SSM_GROUPS, D_STATE)
    dt = jax.nn.softplus(dt.astype(f32) + dt_bias.astype(f32))
    a = -jnp.exp(a_log.astype(f32))
    y, h = ssd_scan(xs, dt, a, bm, cm, h0)
    y = y + d_skip.astype(f32)[:, None] * xs.astype(f32)
    y = y.reshape(b_, t_, D_INNER) * jax.nn.silu(z.astype(f32))
    yg = y.reshape(b_, t_, SSM_GROUPS, D_INNER // SSM_GROUPS)
    yg = yg * lax.rsqrt(jnp.mean(yg * yg, axis=-1, keepdims=True) + EPS)
    y = (yg.reshape(b_, t_, D_INNER) * norm_g.astype(f32)).astype(u.dtype)
    return y @ w_out, new_buf, h.astype(h0.dtype)

def peer(u, w_query, sub_keys, expert_u, expert_v):
    f32 = jnp.float32
    b_, t_, d_ = u.shape
    n = b_ * t_
    blk = PEER_TOKEN_BLOCK
    n_pad = -(-n // blk) * blk
    flat = jnp.pad(u.reshape(n, d_), ((0, n_pad - n), (0, 0)))
    kk = PEER_TOPK

    def block(xb):
        q = (xb @ w_query).reshape(blk, PEER_HEADS, 2, PEER_HALF).astype(f32)
        s = jnp.einsum('thcd,ckd->thck', q, sub_keys.astype(f32))
        top_s, top_i = lax.top_k(s, kk)
        cand = top_s[:, :, 0, :, None] + top_s[:, :, 1, None, :]
        cand_idx = top_i[:, :, 0, :, None] * PEER_N_KEYS + top_i[:, :, 1, None, :]
        best_s, best_j = lax.top_k(cand.reshape(blk, PEER_HEADS, kk * kk), kk)
        idx = jnp.take_along_axis(cand_idx.reshape(blk, PEER_HEADS, kk * kk), best_j, axis=-1)
        gate = jax.nn.softmax(best_s, axis=-1)
        ue = expert_u[idx]
        ve = expert_v[idx]
        act = jax.nn.gelu(jnp.einsum('td,thkd->thk', xb, ue).astype(f32))
        coef = (gate * act).astype(xb.dtype)
        return jnp.einsum('thk,thkd->td', coef, ve)

    out = lax.map(block, flat.reshape(n_pad // blk, blk, d_))
    return out.reshape(n_pad, d_)[:n].reshape(b_, t_, d_)

def dilated_attention(q, k, v, q_pos0, k_pos0):
    f32 = jnp.float32
    b_, t_ = q.shape[:2]
    s_len = k.shape[1]
    qb = Q_BLOCK if t_ % Q_BLOCK == 0 else t_
    nb = t_ // qb
    q_blocks = jnp.swapaxes(q.reshape(b_, nb, qb, N_DIL, KV_PER_BRANCH, Q_PER_KV, HEAD_DIM), 0, 1)
    starts = q_pos0 + jnp.arange(nb, dtype=jnp.int32) * qb
    scale = HEAD_DIM ** -0.5
    k_br = [k[:, :, g * KV_PER_BRANCH:(g + 1) * KV_PER_BRANCH] for g in range(N_DIL)]
    v_br = [v[:, :, g * KV_PER_BRANCH:(g + 1) * KV_PER_BRANCH] for g in range(N_DIL)]

    def block(args):
        qblk, p0 = args
        qpos = p0 + jnp.arange(qb, dtype=jnp.int32)
        outs, lses = [], []
        for g, (win, dil) in enumerate(DIL_PATTERNS):
            n_keys = win // dil + 1
            kpos = qpos[:, None] - dil * jnp.arange(n_keys, dtype=jnp.int32)[None, :]
            valid = kpos >= 0
            kidx = jnp.clip(kpos - k_pos0, 0, s_len - 1)
            kg = k_br[g][:, kidx].astype(f32)
            vg = v_br[g][:, kidx].astype(f32)
            s = jnp.einsum('bqkrd,bqnkd->bqkrn', qblk[:, :, g].astype(f32), kg) * scale
            s = jnp.where(valid[None, :, None, None, :], s, -jnp.inf)
            lse = jax.nn.logsumexp(s, axis=-1)
            p = jnp.exp(s - lse[..., None])
            outs.append(jnp.einsum('bqkrn,bqnkd->bqkrd', p, vg))
            lses.append(lse)
        wts = jax.nn.softmax(jnp.stack(lses), axis=0)
        return jnp.sum(wts[..., None] * jnp.stack(outs), axis=0)

    o = lax.map(block, (q_blocks, starts))
    return jnp.swapaxes(o, 0, 1).reshape(b_, t_, ATTN_OUT_DIM).astype(q.dtype)

def shared_kv(h, pos, kv_norm, w_kv, k_norm):
    b_, t_, _ = h.shape
    kv = (rmsnorm(h, kv_norm) @ w_kv).reshape(b_, t_, 2, N_KV_HEADS, HEAD_DIM)
    k = rope_partial(rmsnorm(kv[:, :, 0], k_norm), pos)
    return k, kv[:, :, 1]

def trunk(x, p, conv_state, ssm_state, past_k, past_v, pos0,
          norm_mix, norm_ffn, norm_ple,
          ssm_w_in, ssm_conv_w, ssm_conv_b, ssm_dt_bias, ssm_a_log, ssm_d, ssm_norm, ssm_w_out,
          kv_norm, w_kv, k_norm, w_q, q_norm, w_o,
          peer_w_query, peer_sub_keys, peer_u, peer_v, ple_w_proj, ple_w_gate):
    b_, t_, _ = x.shape
    pos = pos0 + jnp.arange(t_, dtype=jnp.int32)
    h = x
    new_conv, new_ssm = [], []
    k_new = v_new = k_all = v_all = None
    k_pos0 = 0
    for i in range(DEPTH):
        u = rmsnorm(h, norm_mix[i])
        if i < N_A_LAYERS:
            y, cb, st = mamba_mixer(u, conv_state[i], ssm_state[i], ssm_w_in[i], ssm_conv_w[i], ssm_conv_b[i],
                                    ssm_dt_bias[i], ssm_a_log[i], ssm_d[i], ssm_norm[i], ssm_w_out[i])
            new_conv.append(cb)
            new_ssm.append(st)
            h = h + y
        else:
            if k_new is None:
                k_new, v_new = shared_kv(h, pos, kv_norm, w_kv, k_norm)
                if past_k is None:
                    k_all, v_all, k_pos0 = k_new, v_new, pos0
                else:
                    k_all = jnp.concatenate([past_k.astype(k_new.dtype), k_new], axis=1)
                    v_all = jnp.concatenate([past_v.astype(v_new.dtype), v_new], axis=1)
                    k_pos0 = pos0 - past_k.shape[1]
            j = i - N_A_LAYERS
            q = (u @ w_q[j]).reshape(b_, t_, N_Q_HEADS, HEAD_DIM)
            q = rope_partial(rmsnorm(q, q_norm[j]), pos)
            h = h + dilated_attention(q, k_all, v_all, pos0, k_pos0) @ w_o[j]
        h = h + peer(rmsnorm(h, norm_ffn[i]), peer_w_query[i], peer_sub_keys[i], peer_u[i], peer_v[i])
        gate = jax.nn.sigmoid((rmsnorm(h, norm_ple[i]) @ ple_w_gate[i]).astype(jnp.float32))
        h = h + ((p[i] @ ple_w_proj[i]).astype(jnp.float32) * gate).astype(h.dtype)
    return h, jnp.stack(new_conv), jnp.stack(new_ssm), k_new, v_new

def setup_inputs(seed: int = 0) -> dict:
    key = jax.random.key(seed)
    ks = iter(list(jax.random.split(key, 48)))
    f32 = jnp.float32

    def nrm(shape, scale):
        return jax.random.normal(next(ks), shape, f32) * scale

    def gain(shape):
        return 1.0 + nrm(shape, 0.02)

    x_prompt = nrm((BATCH, SEQ, D_MODEL), 1.0)
    x_sample = nrm((DEC_BATCH, DEC_SEQ, D_MODEL), 1.0)
    state_conv = nrm((N_A_LAYERS, DEC_BATCH, CONV_W - 1, CONV_DIM), 1.0)
    state_ssm = nrm((N_A_LAYERS, DEC_BATCH, SSM_HEADS, SSM_HEAD_DIM, D_STATE), 0.1)
    cache_k = nrm((DEC_BATCH, WIN_BUF, N_KV_HEADS, HEAD_DIM), 1.0)
    cache_v = nrm((DEC_BATCH, WIN_BUF, N_KV_HEADS, HEAD_DIM), 1.0)
    p_prompt = nrm((DEPTH, BATCH, SEQ, PLE_DIM), 1.0)
    p_sample = nrm((DEPTH, DEC_BATCH, DEC_SEQ, PLE_DIM), 1.0)
    norm_mix = gain((DEPTH, D_MODEL))
    norm_ffn = gain((DEPTH, D_MODEL))
    norm_ple = gain((DEPTH, D_MODEL))
    ssm_w_in = nrm((N_A_LAYERS, D_MODEL, IN_PROJ_DIM), D_MODEL ** -0.5)
    ssm_conv_w = nrm((N_A_LAYERS, CONV_W, CONV_DIM), CONV_W ** -0.5)
    ssm_conv_b = nrm((N_A_LAYERS, CONV_DIM), 0.02)
    dt0 = jnp.exp(jax.random.uniform(next(ks), (N_A_LAYERS, SSM_HEADS), f32, math.log(1e-3), math.log(1e-1)))
    ssm_dt_bias = dt0 + jnp.log(-jnp.expm1(-dt0))
    ssm_a_log = jnp.log(jax.random.uniform(next(ks), (N_A_LAYERS, SSM_HEADS), f32, 1.0, 16.0))
    ssm_d = gain((N_A_LAYERS, SSM_HEADS))
    ssm_norm = gain((N_A_LAYERS, D_INNER))
    ssm_w_out = nrm((N_A_LAYERS, D_INNER, D_MODEL), D_INNER ** -0.5)
    kv_norm = gain((D_MODEL,))
    w_kv = nrm((D_MODEL, 2 * N_KV_HEADS * HEAD_DIM), D_MODEL ** -0.5)
    k_norm = gain((HEAD_DIM,))
    w_q = nrm((N_B_LAYERS, D_MODEL, N_Q_HEADS * HEAD_DIM), D_MODEL ** -0.5)
    q_norm = gain((N_B_LAYERS, HEAD_DIM))
    w_o = nrm((N_B_LAYERS, ATTN_OUT_DIM, D_MODEL), ATTN_OUT_DIM ** -0.5)
    peer_w_query = nrm((DEPTH, D_MODEL, PEER_HEADS * PEER_QUERY_DIM), D_MODEL ** -0.5)
    peer_sub_keys = nrm((DEPTH, 2, PEER_N_KEYS, PEER_HALF), PEER_HALF ** -0.5)
    peer_u = nrm((DEPTH, PEER_N_EXPERTS, D_MODEL), D_MODEL ** -0.5)
    peer_v = nrm((DEPTH, PEER_N_EXPERTS, D_MODEL), 0.5)
    ple_w_proj = nrm((DEPTH, PLE_DIM, D_MODEL), PLE_DIM ** -0.5)
    ple_w_gate = nrm((DEPTH, D_MODEL, D_MODEL), D_MODEL ** -0.5)
    return {'x_prompt': x_prompt, 'x_sample': x_sample, 'state_conv': state_conv, 'state_ssm': state_ssm,
            'cache_k': cache_k, 'cache_v': cache_v, 'p_prompt': p_prompt, 'p_sample': p_sample,
            'norm_mix': norm_mix, 'norm_ffn': norm_ffn, 'norm_ple': norm_ple,
            'ssm_w_in': ssm_w_in, 'ssm_conv_w': ssm_conv_w, 'ssm_conv_b': ssm_conv_b,
            'ssm_dt_bias': ssm_dt_bias, 'ssm_a_log': ssm_a_log, 'ssm_d': ssm_d, 'ssm_norm': ssm_norm,
            'ssm_w_out': ssm_w_out, 'kv_norm': kv_norm, 'w_kv': w_kv, 'k_norm': k_norm,
            'w_q': w_q, 'q_norm': q_norm, 'w_o': w_o,
            'peer_w_query': peer_w_query, 'peer_sub_keys': peer_sub_keys, 'peer_u': peer_u, 'peer_v': peer_v,
            'ple_w_proj': ple_w_proj, 'ple_w_gate': ple_w_gate}

def reference(x_prompt, x_sample, state_conv, state_ssm, cache_k, cache_v, p_prompt, p_sample,
              norm_mix, norm_ffn, norm_ple,
              ssm_w_in, ssm_conv_w, ssm_conv_b, ssm_dt_bias, ssm_a_log, ssm_d, ssm_norm, ssm_w_out,
              kv_norm, w_kv, k_norm, w_q, q_norm, w_o,
              peer_w_query, peer_sub_keys, peer_u, peer_v, ple_w_proj, ple_w_gate):
    weights = (norm_mix, norm_ffn, norm_ple,
               ssm_w_in, ssm_conv_w, ssm_conv_b, ssm_dt_bias, ssm_a_log, ssm_d, ssm_norm, ssm_w_out,
               kv_norm, w_kv, k_norm, w_q, q_norm, w_o,
               peer_w_query, peer_sub_keys, peer_u, peer_v, ple_w_proj, ple_w_gate)
    b_p = x_prompt.shape[0]
    zero_conv = jnp.zeros((N_A_LAYERS, b_p, CONV_W - 1, CONV_DIM), x_prompt.dtype)
    zero_ssm = jnp.zeros((N_A_LAYERS, b_p, SSM_HEADS, SSM_HEAD_DIM, D_STATE), x_prompt.dtype)
    y_prompt, prompt_conv, prompt_ssm, k_p, v_p = trunk(x_prompt, p_prompt, zero_conv, zero_ssm, None, None, 0, *weights)
    keep = min(WIN_MAX, k_p.shape[1])
    prompt_k = k_p[:, -keep:]
    prompt_v = v_p[:, -keep:]
    y_sample, sample_conv, sample_ssm, sample_k, sample_v = trunk(x_sample, p_sample, state_conv, state_ssm,
                                                                  cache_k, cache_v, PAST_LEN, *weights)
    return (y_prompt, y_sample, prompt_conv, prompt_ssm, prompt_k, prompt_v,
            sample_conv, sample_ssm, sample_k, sample_v)


_drawn_inputs = setup_inputs


def setup_inputs(seed=0):
    import zlib

    import numpy as np

    out = dict(_drawn_inputs(seed))
    spreads = {}
    factors = {'norm_ple': 5.796, 'kv_norm': 2.799, 'k_norm': 3.56, 'q_norm': 7.324}
    for name, (base, spread) in spreads.items():
        noise = np.random.default_rng([zlib.crc32(name.encode()), seed]).standard_normal(out[name].shape)
        drawn = base * np.exp(spread * noise) if base else spread * noise
        out[name] = jnp.asarray(drawn.astype(out[name].dtype))
    for name, factor in factors.items():
        out[name] = (out[name] * factor).astype(out[name].dtype)
    return out
```

```python
import numpy as np
import concourse.bass as bass
import concourse.mybir as mybir
from concourse.alu_op_type import AluOpType as ALU
from contextlib import ExitStack

ACT = mybir.ActivationFunctionType
AX = mybir.AxisListType
F32 = mybir.dt.float32
U32 = mybir.dt.uint32
I32 = mybir.dt.int32

D = 1024
KD = D // 128
NTOK = 320
ROWS = (128, 128, 64)
OFF = (0, 128, 256)
DEC_B, DEC_T, PAST = 8, 8, 2048
D_INNER, CONV_DIM, HEADS, GROUPS, HG, HP, NS = 2048, 4096, 32, 8, 4, 64, 128
XS_BLKS, CONV_BLKS = D_INNER // 128, CONV_DIM // 128
DT_COL = D_INNER + CONV_DIM
PK, PH, TOPK, EXPERTS = 128, 8, 16, 16384
HK = PH * TOPK
PLE = 256
EPS = 1e-6
CONV_W = 4
NB = 8
NW = 4

ARENA = 29696

C_ID, C_TRI, C_STRICT, C_TRIS, C_STRICTS, C_ONES, C_BM, C_ID2, C_IOTA, C_END = 0, 128, 256, 384, 448, 512, 640, 648, 712, 728


def shape_constants():
    c = np.zeros((128, C_END), np.float32)
    k, s = np.arange(128)[:, None], np.arange(128)[None, :]
    c[:, C_ID:C_ID + 128] = k == s
    c[:, C_TRI:C_TRI + 128] = k <= s
    c[:, C_STRICT:C_STRICT + 128] = k > s
    k, s = k[:64], s[:, :64]
    same = k // DEC_T == s // DEC_T
    c[:64, C_TRIS:C_TRIS + 64] = (k <= s) & same
    c[:64, C_STRICTS:C_STRICTS + 64] = (k > s) & same
    c[:, C_ONES:C_ONES + 128] = 1.0
    c[:64, C_BM:C_BM + 8] = k // DEC_T == np.arange(8)[None, :]
    c[:, C_ID2:C_ID2 + 64] = np.arange(128)[:, None] % 64 == np.arange(64)[None, :]
    c[:, C_IOTA:C_IOTA + 16] = np.arange(16)[None, :]
    return c


DILATION = (1, 4, 16)
WINDOW = (128, 512, 2048)
NQH, NKH = 24, 6
SBLK = 13
SCOLS = SBLK * 128 + 48
MASKED = -1.0e30


def attention_masks():
    q = np.arange(128)[:, None]
    parts = []
    for t in range(2):
        k = np.arange(128 * (t + 1))[None, :]
        for d, w in zip(DILATION, WINDOW):
            gap = q + 128 * t - k
            parts.append((gap >= 0) & (gap % d == 0) & (gap <= w))
    row = np.arange(128)[:, None]
    b2, i = row // 64, row % 8
    c = np.arange(512)[None, :]
    parts.append(((c - i) % 4 == 0) & (c >= i))
    residue = (np.arange(1024) // 128)[None, :]
    parts.append(residue == i)
    parts.append(np.arange(128)[None, :] >= i)
    kb, s = (np.arange(16) // 8)[None, :], (np.arange(16) % 8)[None, :]
    for d in DILATION:
        parts.append((kb == b2) & (s <= i) & ((i - s) % d == 0))
    seen = np.concatenate([np.broadcast_to(p, (128, p.shape[1])) for p in parts], axis=1)
    return np.where(seen, 0.0, MASKED).astype(np.float32)


def rotary_angles():
    inv = np.float32(500000.0) ** (-np.arange(0, 16, 2, dtype=np.float32) / np.float32(16))
    pos = np.zeros((3, 128), np.float32)
    pos[0], pos[1] = np.arange(128), np.arange(128) + 128
    pos[2, :64] = PAST + np.arange(64) % DEC_T
    ang = (pos[:, :, None] * inv[None, None, :].astype(np.float32)).astype(np.float32).astype(np.float64)
    return np.stack([np.cos(ang), np.sin(ang)], axis=2).transpose(1, 0, 2, 3).reshape(128, 48).astype(np.float32)


class Signal:

    def __init__(self, sem, counts):
        self.sem, self.n, self.counts = sem, 0, counts

    def mark(self, key=None, by=1):
        self.n += by
        if key is not None:
            self.counts[key] = self.n
        return self.sem, by

    def at(self, key):
        return self.sem, self.counts[key]


class AnyCount(dict):

    def __missing__(self, key):
        return 1


class AnyUser(dict):
    def __missing__(self, key):
        return None


def build(nc, I, O, counts):
    first = counts is None
    counts = {} if first else counts
    ctx = ExitStack()
    with ctx:
        sb = lambda name, shape, dt=F32: ctx.enter_context(nc.sbuf_tensor(name, shape, dt))
        signals = {}

        def signal(name):
            if name not in signals:
                if name not in counts:
                    counts[name] = AnyCount()
                signals[name] = Signal(ctx.enter_context(nc.semaphore(name)), counts[name])
            return signals[name]

        cst = sb("cst", [128, C_END])
        h = sb("h", [128, 3, D])
        u = sb("u", [128, 3, D])
        uT = sb("uT", [128, 16, NTOK])
        wring = sb("wring", [128, NW, 2048])
        gain = sb("gain", [128, 2, D])
        small = sb("small", [128, 1280])
        arena = sb("arena", [128, ARENA])
        banks = ctx.enter_context(nc.psum_tensor("banks", [128, NB, 512], F32))

        ident = cst[:, C_ID:C_ID + 128]
        ones = cst[:, C_ONES:C_ONES + 128]

        def area(base, *shape):
            n = int(np.prod(shape))
            v = arena[:, base:base + n]
            if len(shape) == 2:
                v = v.rearrange("p (a b) -> p a b", a=shape[0])
            if len(shape) == 3:
                v = v.rearrange("p (a b c) -> p a b c", a=shape[0], b=shape[1])
            return v

        job = {}
        order = [0]
        bank_full = [signal(f"bank_full{b}") for b in range(NB)]
        bank_free = [signal(f"bank_free{b}") for b in range(NB)]
        jobs = counts.setdefault("jobs", {})
        last_user = counts.setdefault("last_user", AnyUser())

        def claim(pe, key):
            j = order[0]
            order[0] += 1
            jobs[key] = j
            if j >= NB:
                pe.wait_ge(bank_free[j % NB].sem, j // NB)
            return banks[:, j % NB, :]

        def full(key):
            j = jobs[key]
            return bank_full[j % NB].sem, 1

        def full_at(key):
            j = jobs.get(key, 0)
            return bank_full[j % NB].sem, j // NB + 1

        def filled(eng, key):
            eng.wait_ge(*full_at(key))
            return banks[:, jobs.get(key, 0) % NB, :]

        def free(key):
            return bank_free[jobs.get(key, 0) % NB].sem, 1

        def freed(key):
            j = jobs.get(key, 0)
            return bank_free[j % NB].sem, j // NB + 1

        loads = []
        load_index = {}

        def plan_weight(key, matrix, row0, col0, cols, rows=512):
            load_index[key] = len(loads)
            loads.append((matrix[row0:row0 + rows, col0:col0 + cols].rearrange("(k p) n -> p k n", p=128), rows // 128, cols))

        def plan_project(key, matrix, kchunks, cols):
            for n in range(cols // 512):
                for half in range(kchunks // 4):
                    plan_weight((key, n, half), matrix, half * 512, n * 512, 512)

        plan_project("z", I["w_in"], KD, D_INNER)
        for n in range(CONV_DIM // 512):
            for half in range(2):
                plan_weight(("xbc", n, half), I["w_in"], half * 512, D_INNER + n * 512, 512)
        plan_project("out", I["w_out"], 16, D)

        def plan_ffn(l):
            plan_project(f"query{l}", I["peer_w_query"][l], KD, PH * 256)
            for n in range(2):
                plan_weight((f"pproj{l}", n, 0), I["ple_w_proj"][l], 0, n * 512, 512, rows=256)
                for half in range(2):
                    plan_weight((f"pgate{l}", n, half), I["ple_w_gate"][l], half * 512, n * 512, 512)

        plan_ffn(0)
        for half in range(2):
            plan_weight(("kv", 0, half), I["w_kv"], half * 512, 0, 512)
        for half in range(2):
            plan_weight(("kv", 1, half), I["w_kv"], half * 512, 512, 256)
        plan_project("wq", I["w_q"][0], KD, NQH * 64)
        plan_project("wo", I["w_o"][0], 4, D)
        plan_ffn(1)
        w_ready = [signal(f"w_ready{s}") for s in range(NW)]

        def slot_view(i):
            _, k, cols = loads[i]
            return wring[:, i % NW, 0:k * cols].rearrange("p (k n) -> p k n", k=k)

        def weight(pe, key, user):
            i = load_index[key]
            last_user[i] = user
            pe.wait_ge(w_ready[i % NW].sem, 16 * (i // NW + 1))
            return slot_view(i)

        load_sent = [0]

        def load_weights(sp, upto):
            while load_sent[0] < upto:
                i = load_sent[0]
                if i >= NW:
                    sp.wait_ge(*full_at(last_user[i - NW]))
                sp.dma_start(slot_view(i), loads[i][0]).then_inc(*w_ready[i % NW].mark(by=16))
                load_sent[0] += 1

        ssq, var, rstd, nwt = (small[:, 8 * i:8 * i + 8] for i in range(4))
        gvar, grstd, gnwt = (small[:, 32 + 24 * i:56 + 24 * i].rearrange("p (t g) -> p t g", t=3) for i in range(3))
        dt, da, dtmp, dtmp2, dtmp3 = (small[:, 104 + 96 * i:200 + 96 * i].rearrange("p (t g) -> p t g", t=3) for i in range(5))
        a_bc = small[:, 584:616]
        dtb_bc = small[:, 616:648]
        d_bc = small[:, 648:680]
        ex = small[:, 680:968].rearrange("p (t g) -> p t g", t=3)
        ec = small[:, 968:1096].rearrange("p (k b) -> p k b", k=16)
        ngT = small[:, 1096:1112]

        z = area(0, 3, D_INNER)
        bcT = area(6144, 16, NTOK)
        xs = area(11264, 3, D_INNER)
        btok = area(17408, 3, 1024)
        T0 = 20480
        raw = area(T0, 4, 347)
        xc = area(T0 + 1392, 8, NTOK)
        stT = area(T0 + 3952, 32, 29)
        newT = area(T0 + 4880, 32, 27)
        newst = area(T0 + 5744, 2, 512)
        w_dt = area(T0 + 6768, 8, 32)
        cacc = area(T0 + 7024, 3, NTOK)
        sg = area(T0 + 7984, 3, NTOK)
        conv_rows = arena[0:29, 11264:11264 + 4096]
        ng_rows = arena[0:16, 11264 + 4096:11264 + 4224]
        seg_l = area(T0, 2, 4, 128)
        dec = area(T0 + 1024, 2, 512)
        xdt = area(T0 + 2048, 2, 256)
        xdtt = area(T0 + 2560, 2, 256)
        hT = area(T0 + 3072, 8, 256)
        yt = area(T0 + 5120, 2, 256)
        ctm = area(T0 + 5632, 2, 8, 64)
        bm = area(T0 + 6656, 8, 128)
        hfin = area(T0 + 7680, 2, 256)
        dxs = area(T0 + 8192, 2, 256)
        cbm = area(T0 + 8704, 2, 128)
        assert T0 + 8960 <= ARENA
        h0 = u[:, :, :].rearrange("p s (b n) -> p s b n", b=8)
        h0T = wring[:, 2, :].rearrange("p (s b n) -> p s b n", s=2, b=8)
        hnew = wring[:, 3, :].rearrange("p (s b n) -> p s b n", s=2, b=8)

        PSLOTS = 8
        VPE = (0, 1, 2, 4, 5, 6)
        VDVE = (3, 7)
        qT = area(0, 16, NTOK)
        sk_raw = area(5120, 2, 128)
        skT = area(5376, 2, 128)
        sc = area(5632, 2, 16, 128)
        top_v = area(9728, 16, 16)
        top_i = arena[:, 9984:10240].bitcast(U32).rearrange("p (a b) -> p a b", a=16)
        top_f = area(10240, 16, 16)
        cand = area(10496, 8, 256)
        onehot = area(12544, 128, 16)
        best_v = area(14592, 8, 16)
        best_j = arena[:, 14720:14848].bitcast(U32).rearrange("p (a b) -> p a b", a=8)
        best_a, best_b = area(14848, 8, 16), area(14976, 8, 16)
        pick1, pick2 = area(15104, 128), area(15232, 128)
        expert = arena[:, 15360:15616].bitcast(U32).rearrange("p (s n) -> p s n", s=2)
        pgate = area(15616, 2, 128)
        pact = area(15872, 2, 128)
        ptmp = area(16128, 128)
        ptmp2 = area(16256, 128)
        coef = area(16384, 2, 128)
        rows_buf = area(17152, PSLOTS, D)
        islot = arena[:, 25344:25352].bitcast(U32)
        p_rows = area(25352, 3, PLE)
        pT = area(26120, 2, NTOK)
        sgate = area(26760, 3, 512)
        diag = area(28296, len(VPE), 128)
        assert 28296 + 128 * len(VPE) <= ARENA
        stt2 = small[:, 1112:1136]
        HPT = (8, 8, 4)

        qkT = area(0, 15, NTOK)
        qst = area(4800, 3, 8, 64)
        kvs = area(6336, 3, 768)
        sm = area(8640, 2, 768)
        ssm = area(8640, SCOLS)
        pt = area(10352, 2, 6, 128)
        pts = area(10352, 16, 128)
        kcT = area(12400, 26, 128)
        q_raw = area(10352, 3, 1536)
        sq_buf = area(14960, 30, 64)
        cache = arena[:, 15728:15728 + 4 * 3328].rearrange(
            "p (x w b n) -> p x w b n", x=2, w=2, b=26)
        qkn = arena[:, 22384:22384 + 5760].rearrange("p (t h d) -> p t h d", t=3, h=30)
        vnew = gain[:, :, :].rearrange("p s d -> p (s d)")[:, 0:1536].rearrange("p (c n) -> p c n", c=4)
        osb = gain[:, 1, 512:1024]
        masks = u[:, :, :].rearrange("p t d -> p (t d)")[:, 0:1152 + SCOLS]
        pmask = (masks[:, 0:384], masks[:, 384:1152])
        smask = masks[:, 1152:1152 + SCOLS]
        qvar, qrstd, qtmp = (small[:, 104 + 90 * i:194 + 90 * i].rearrange("p (t h) -> p t h", t=3) for i in range(3))
        so = small[:, 680:808]
        gq, gk = small[:, 808:872], small[:, 872:936]
        negmax, zsum, rz = (small[:, 936 + 2 * i:938 + 2 * i] for i in range(3))
        angles = small[:, 1136:1184].rearrange("p (t c f) -> p t c f", t=3, c=2)

        h_in = [signal(f"h_loaded{t}") for t in range(3)]
        gain_in = [signal(f"gain_loaded{i}") for i in range(2)]
        cst_in = signal("constants_loaded")
        rows_in = signal("conv_rows_loaded")
        dtw_in = signal("dt_weights_loaded")
        vec_in = signal("head_vectors_loaded")
        h0_in = [signal(f"state_loaded{i}") for i in range(3)]
        hnew_out = [signal(f"state_stored{i}") for i in range(2)]
        hfin_out = [signal(f"final_state_stored{i}") for i in range(2)]
        newst_out = [signal(f"conv_rows_stored{i}") for i in range(2)]
        squares = signal("squares_summed")
        u_ready = signal("u_normalised")
        sk_in = signal("sub_keys_loaded")
        prow_in = signal("ple_rows_loaded")
        gathered = [signal(f"rows_gathered{k}") for k in range(PSLOTS)]
        slot_free = [signal(f"row_slot_free{k}") for k in range(PSLOTS)]
        index_copied = signal("index_copied")
        diag_made = signal("diagonals_made")
        angles_in = signal("angles_loaded")
        masks_in = signal("masks_loaded")
        qk_gain_in = signal("head_gains_loaded")
        cache_in = [signal(f"cache_loaded{i}") for i in range(2)]
        vnew_in = signal("new_values_moved")
        stored = signal("outputs_stored")
        act_order, dve_order, pool_order = signal("scalar_step"), signal("vector_step"), signal("pool_step")
        act_done, dve_done, pool_done = signal("scalar_result"), signal("vector_result"), signal("pool_result")

        def stepper(eng, order):
            def s(ins, sig=None, key=None):
                sig = sig or order
                ins.then_inc(*sig.mark(key))
                eng.wait_ge(sig.sem, sig.n)

            def freeing(ins, key):
                ins.then_inc(*free(key))
                eng.wait_ge(*freed(key))
            return s, freeing

        def step_of(t, g):
            return t * GROUPS + g

        def tri_of(t):
            return cst[:, C_TRI:C_TRI + 128] if t < 2 else cst[0:64, C_TRIS:C_TRIS + 64]

        def strict_of(t):
            return cst[:, C_STRICT:C_STRICT + 128] if t < 2 else cst[0:64, C_STRICTS:C_STRICTS + 64]

        def spread(ap, n):
            return ap.unsqueeze(2).to_broadcast([ap.shape[0], ap.shape[1], n])

        def repeat(ap, n):
            return ap.unsqueeze(1).to_broadcast([ap.shape[0], n, ap.shape[1]])

        def heads(ap):
            return ap.rearrange("p (h d) -> p h d", d=64)

        def peer_rounds(t):
            return HPT[t] * TOPK // PSLOTS

        def u_base(l, t):
            return 2 * (l * sum(map(peer_rounds, range(3))) + sum(map(peer_rounds, range(t))))

        def v_base(l, t):
            return u_base(l, t) + peer_rounds(t)

        block = ctx.enter_context(nc.Block())

        @block.tensor
        def _(pe):
            def transposes(key, pieces):
                bank = claim(pe, key)
                for col, src in pieces:
                    r, c = src.shape[0], src.shape[-1]
                    mm = pe.transpose(bank[0:c, col:col + r], src, ident[0:r, 0:r])
                mm.then_inc(*full(key))

            def norm_transposes(key):
                for t in range(3):
                    pe.wait_ge(*u_ready.at((key, t)))
                    for half in range(2):
                        transposes(("uT", key, t, half),
                                   [(j * 128, u[0:ROWS[t], t, (4 * half + j) * 128:(4 * half + j + 1) * 128])
                                    for j in range(4)])
                for t in range(3):
                    for half in range(2):
                        pe.wait_ge(*freed(("uT", key, t, half)))

            def project_block(key, n, kchunks):
                acc = [claim(pe, (key, n, t)) for t in range(3)]
                for half in range(kchunks // 4):
                    w = weight(pe, (key, n, half), (key, n, 2))
                    for t in range(3):
                        for k in range(4):
                            kk = half * 4 + k
                            mm = pe.matmul(acc[t][0:ROWS[t], 0:w.shape[2]], uT[:, kk, OFF[t]:OFF[t] + ROWS[t]], w[:, k, :],
                                           start=(kk == 0), stop=(kk == kchunks - 1))
                        if kk == kchunks - 1:
                            mm.then_inc(*full((key, n, t)))

            def project(key, nblocks, kchunks):
                for n in range(nblocks):
                    project_block(key, n, kchunks)

            pe.wait_ge(*cst_in.at("cst"))
            pe.wait_ge(rows_in.sem, 64)
            for half in range(2):
                transposes(("rows", half), [(j * 29, conv_rows[:, (16 * half + j) * 128:(16 * half + j + 1) * 128])
                                            for j in range(16)])
            transposes("ng", [(0, ng_rows)])
            norm_transposes("mix0")
            pe.wait_ge(dtw_in.sem, 16)
            for t in range(3):
                acc = claim(pe, ("dt", t))
                for k in range(KD):
                    mm = pe.matmul(acc[0:ROWS[t], 0:32], uT[:, k, OFF[t]:OFF[t] + ROWS[t]], w_dt[:, k, :],
                                   start=(k == 0), stop=(k == KD - 1))
                mm.then_inc(*full(("dt", t)))
            project("z", 4, KD)

            def to_tokens(n):
                for j in range(4):
                    pe.wait_ge(*dve_done.at(("silu", 4 * n + j)))
                src = [xc[:, (4 * n + j) % 8, :] if n < 4 else bcT[:, 4 * n + j - 16, :] for j in range(4)]
                for t in range(3):
                    transposes(("tok", n, t), [(j * 128, src[j][:, OFF[t]:OFF[t] + ROWS[t]]) for j in range(4)])

            for n in range(8):
                w = [weight(pe, ("xbc", n, half), ("xbc", 4 * n + 3)) for half in range(2)]
                for j in range(4):
                    acc = claim(pe, ("xbc", 4 * n + j))
                    for k in range(KD):
                        mm = pe.matmul(acc[:, 0:NTOK], w[k // 4][:, k % 4, j * 128:(j + 1) * 128], uT[:, k, :],
                                       start=(k == 0), stop=(k == KD - 1))
                    mm.then_inc(*full(("xbc", 4 * n + j)))
                if 1 <= n <= 6:
                    to_tokens(n - 1)
            for q in range(8):
                for j in range(4):
                    pe.wait_ge(*pool_done.at(("newrow", 4 * q + j)))
                transposes(("newst", q), [(j * 128, newT[:, 4 * q + j, :]) for j in range(4)])

            def sample_states(g):
                x = step_of(2, g) % 2
                for i in range(2):
                    blk = 2 * g + i
                    pe.wait_ge(*h0_in[blk % 3].at(blk))
                    for q in range(2):
                        transposes(("h0T", blk, q), [(b * 128, h0[:, blk % 3, 4 * q + b, :]) for b in range(4)])
                pe.wait_ge(*pool_done.at(("ctm", g)))
                for i in range(2):
                    for q in range(2):
                        pe.wait_ge(*freed(("h0T", 2 * g + i, q)))
                bank = claim(pe, ("inter", 2, g))
                for i in range(2):
                    for b in range(8):
                        mm = pe.matmul(bank[0:64, i * 128:(i + 1) * 128], ctm[:, g % 2, b, :], h0T[:, i, b, :],
                                       start=(b == 0), stop=(b == 7))
                mm.then_inc(*full(("inter", 2, g)))
                pe.wait_ge(*dve_done.at(("bm", g)))
                pe.wait_ge(*pool_done.at(("xdt", 2, g)))
                for i in range(2):
                    for q in range(2):
                        bank = claim(pe, ("hupd", 2 * g + i, q))
                        mm = pe.matmul(bank[:, :], xdtt[0:64, x, i * 128:(i + 1) * 128],
                                       bm[0:64, 4 * q:4 * q + 4, :], start=True, stop=True)
                        mm.then_inc(*full(("hupd", 2 * g + i, q)))

            def scan_group(t, g):
                R, x = ROWS[t], step_of(t, g) % 2
                tok = slice(OFF[t], OFF[t] + R)
                pe.wait_ge(*dve_done.at(("seg", t, g)))
                bank = claim(pe, ("seg", t, g))
                for j in range(4):
                    mm = pe.matmul(bank[0:R, j * R:(j + 1) * R], seg_l[0:R, x, j, 0:R], tri_of(t), start=True, stop=True)
                mm.then_inc(*full(("seg", t, g)))
                bank = claim(pe, ("cb", t, g))
                pe.matmul(bank[0:R, 0:R], bcT[:, g, tok], bcT[:, 8 + g, tok], start=True, stop=True)\
                  .then_inc(*full(("cb", t, g)))
                if t == 1:
                    pe.wait_ge(*freed(("state", 0, g)))
                    bank = claim(pe, ("inter", t, g))
                    pe.matmul(bank[:, 0:256], bcT[:, 8 + g, tok], hT[:, g, :], start=True, stop=True)\
                      .then_inc(*full(("inter", t, g)))
                if t == 2:
                    sample_states(g)
                pe.wait_ge(*dve_done.at(("m", t, g)))
                pe.wait_ge(*pool_done.at(("xdt", t, g)))
                bank = claim(pe, ("y", t, g))
                for j in range(4):
                    mm = pe.matmul(bank[0:R, j * 64:(j + 1) * 64], dec[0:R, x, j * R:(j + 1) * R],
                                   xdt[0:R, x, j * 64:(j + 1) * 64], start=True, stop=True)
                mm.then_inc(*full(("y", t, g)))
                if t < 2:
                    bank = claim(pe, ("state", t, g))
                    pe.matmul(bank[:, 0:256], btok[:, t, g * 128:(g + 1) * 128], xdtt[:, x, :], start=True, stop=True)\
                      .then_inc(*full(("state", t, g)))
                if t == 1:
                    pe.wait_ge(*freed(("state", 1, g)))
                    transposes(("hfin", g), [(i * 128, hT[:, g, i * 128:(i + 1) * 128]) for i in range(2)])

            for q in range(6):
                for t in range(3):
                    pe.wait_ge(*freed(("tok", q, t)))
            pe.wait_ge(*dve_done.at("da"))
            for b in (16 + 15,):
                pe.wait_ge(*dve_done.at(("silu", b)))
            for t in range(3):
                R = ROWS[t]
                bank = claim(pe, ("cum", t))
                pe.matmul(bank[0:R, 0:32], tri_of(t), da[0:R, t, :], start=True, stop=True)
                pe.matmul(bank[0:R, 32:64], strict_of(t), da[0:R, t, :], start=True, stop=True)
                pe.matmul(bank[0:R, 64:96], ones[0:R, 0:R], da[0:R, t, :], start=True, stop=True)\
                  .then_inc(*full(("cum", t)))
                if t == 2:
                    bank = claim(pe, "ec")
                    for hd in range(HEADS):
                        rows, k = slice(64 * (hd % 2), 64 * (hd % 2) + 64), hd // 2
                        mm = pe.matmul(bank[rows, k * 8:(k + 1) * 8], da[0:64, 2, hd:hd + 1].to_broadcast([64, 64]),
                                       cst[0:64, C_BM:C_BM + 8], start=True, stop=True)
                    mm.then_inc(*full("ec"))
                for g in range(GROUPS):
                    scan_group(t, g)
                pe.wait_ge(*dve_done.at(("ynorm", t)))
                for q in range(4):
                    transposes(("yT", t, q), [(j * 128, z[0:R, t, (4 * q + j) * 128:(4 * q + j + 1) * 128]) for j in range(4)])
            for t in range(3):
                for q in range(4):
                    pe.wait_ge(*freed(("yT", t, q)))
            project("out", 2, 16)

            def select(l, t, quads=range(4)):
                for q in quads:
                    bank = claim(pe, ("score", l, t, q))
                    if t < 2:
                        for j in range(4):
                            mm = pe.matmul(bank[:, j * 128:(j + 1) * 128], qT[:, 4 * q + j, OFF[t]:OFF[t] + 128],
                                           skT[:, j % 2, :], start=True, stop=True)
                    elif q < 2:
                        for hf in range(2):
                            for j in range(4):
                                mm = pe.matmul(bank[64 * hf:64 * hf + 64, j * 128:(j + 1) * 128],
                                               qT[:, 8 * hf + 4 * q + j, 256:320], skT[:, j % 2, :], start=True, stop=True)
                    else:
                        mm = pe.matmul(bank[0:64, 0:1], ident[:, 0:64], ident[:, 0:1], start=True, stop=True)
                    mm.then_inc(*full(("score", l, t, q)))

            def combine(l, t):
                R, base = ROWS[t], v_base(l, t)
                acc = [claim(pe, ("peer", l, t, n)) for n in range(2)]
                for n in range(2):
                    pe.matmul(acc[n][0:R, :], ident[0:R, 0:R], h[0:R, t, n * 512:(n + 1) * 512], start=True, stop=False)
                made = u_base(l, t) // 2 * len(VPE)
                with pe.Fori(0, peer_rounds(t), 1) as i:
                    for d, k in enumerate(VPE):
                        pe.wait_ge(diag_made.sem, i * len(VPE) + (made + d + 1))
                        pe.wait_ge(gathered[k].sem, i * 16 + (base * 16 + 16))
                        for n in range(2):
                            mm = pe.matmul(acc[n][0:R, :], diag[:, d, 0:R], rows_buf[:, k, n * 512:(n + 1) * 512],
                                           start=False, stop=False, skip_group_check=True)
                        mm.then_inc(slot_free[k].sem, 1)
                pe.wait_ge(*dve_done.at(("vsum", l, t)))
                for n in range(2):
                    pe.matmul(acc[n][0:R, :], ident if t < 2 else cst[:, C_ID2:C_ID2 + 64], u[:, t, n * 512:(n + 1) * 512],
                              start=False, stop=True).then_inc(*full(("peer", l, t, n)))

            def ffn(l):
                pe.wait_ge(*sk_in.at(l))
                transposes(("sk", l), [(c * 128, sk_raw[:, c, :]) for c in range(2)])
                norm_transposes(f"ffn{l}")
                for n in range(4):
                    w = [weight(pe, (f"query{l}", n, half), ("q", l, 4 * n + 3)) for half in range(2)]
                    for j in range(4):
                        acc = claim(pe, ("q", l, 4 * n + j))
                        for k in range(KD):
                            mm = pe.matmul(acc[:, 0:NTOK], w[k // 4][:, k % 4, j * 128:(j + 1) * 128], uT[:, k, :],
                                           start=(k == 0), stop=(k == KD - 1))
                        mm.then_inc(*full(("q", l, 4 * n + j)))
                    if n == 0:
                        pe.wait_ge(*freed(("sk", l)))
                    else:
                        for b in range(4 * n - 4, 4 * n):
                            pe.wait_ge(*freed(("q", l, b)))
                        select(l, 0, [n - 1])
                for b in range(12, 16):
                    pe.wait_ge(*freed(("q", l, b)))
                select(l, 0, [3])
                select(l, 1)
                select(l, 2)
                combine(l, 0)
                combine(l, 1)
                combine(l, 2)
                pe.wait_ge(*prow_in.at(l))
                for t in range(3):
                    transposes(("pT", l, t), [(c * 128, p_rows[0:ROWS[t], t, c * 128:(c + 1) * 128]) for c in range(2)])
                norm_transposes(f"ple{l}")
                for t in range(3):
                    pe.wait_ge(*freed(("pT", l, t)))
                for n in range(2):
                    w = weight(pe, (f"pproj{l}", n, 0), (f"pproj{l}", n, 2))
                    for t in range(3):
                        acc = claim(pe, (f"pproj{l}", n, t))
                        for k in range(2):
                            mm = pe.matmul(acc[0:ROWS[t], :], pT[:, k, OFF[t]:OFF[t] + ROWS[t]], w[:, k, :],
                                           start=(k == 0), stop=(k == 1))
                        mm.then_inc(*full((f"pproj{l}", n, t)))
                    project_block(f"pgate{l}", n, KD)

            ffn(0)

            norm_transposes("kv")
            project("kv", 2, KD)
            norm_transposes("mix1")
            project("wq", 3, KD)
            for t in range(3):
                R = ROWS[t]
                pe.wait_ge(*dve_done.at(("rope", t)))
                for g in range(4):
                    heads_of = [2 * (4 * g + j) for j in range(4 if g < 3 else 3)]
                    transposes(("qk", t, g), [(j * 128, qkn[0:R, t, hd:hd + 2, :].rearrange("p h d -> p (h d)"))
                                              for j, hd in enumerate(heads_of)])
            for t in range(3):
                for g in range(4):
                    pe.wait_ge(*freed(("qk", t, g)))

            def prompt_scores(t, hd):
                r, j = divmod(hd, 4)
                rows, K = slice(64 * r, 64 * r + 64), 128 * (t + 1)
                per = 3 if t == 0 else 2
                for c in range(t + 1):
                    bank = claim(pe, ("s", t, hd, c))
                    for g in range(c * per, min(3, (c + 1) * per)):
                        mm = pe.matmul(bank[:, (g - c * per) * K:(g - c * per + 1) * K], qkT[rows, 4 * g + j, OFF[t]:OFF[t] + 128],
                                       qkT[rows, 12 + g, 0:K], start=True, stop=True)
                    mm.then_inc(*full(("s", t, hd, c)))

            def prompt_values(t, hd):
                r, x, n = hd // 4, hd % 2, 3 * (t + 1)
                pe.wait_ge(*act_done.at(("p", t, hd)))
                for c in range(t + 1):
                    transposes(("pt", t, hd, c), [((b - 4 * c) * 128, sm[:, x, b * 128:(b + 1) * 128])
                                                  for b in range(4 * c, min(n, 4 * c + 4))])
                for c in range(t + 1):
                    pe.wait_ge(*freed(("pt", t, hd, c)))
                bank = claim(pe, ("o", t, hd))
                for b in range(n):
                    g, kb = divmod(b, t + 1)
                    mm = pe.matmul(bank[:, 0:64], pt[:, x, b, :], kvs[:, kb, 384 + (2 * g + r) * 64:448 + (2 * g + r) * 64],
                                   start=(b == 0), stop=(b == n - 1))
                mm.then_inc(*full(("o", t, hd)))

            for t in range(2):
                for hd in range(9):
                    if hd < 8:
                        prompt_scores(t, hd)
                    if hd >= 1:
                        prompt_values(t, hd - 1)
                pe.wait_ge(*dve_done.at(("osb", t)))
                transposes(("oT", t), [(c * 128, osb[:, c * 128:(c + 1) * 128]) for c in range(4)])

            def sample_keys(p):
                pe.wait_ge(*cache_in[p % 2].at(p))
                for c in range(7):
                    transposes(("kc", p, c), [((b - 4 * c) * 128, cache[:, p % 2, 0, b, :]) for b in range(4 * c, min(26, 4 * c + 4))])

            def sample_scores(p):
                for c in range(7):
                    pe.wait_ge(*freed(("kc", p, c)))
                for c in range(4):
                    bank = claim(pe, ("ss", p, c))
                    for b2 in range(2):
                        rows, q = slice(64 * b2, 64 * b2 + 64), qst[:, :, 2 * p + b2, :]
                        keys = kcT[:, 13 * b2 + 4 * c:13 * b2 + 4 * c + (4 if c < 3 else 1), :]
                        g = (1, 2, 2, 0)[c]
                        mm = pe.matmul(bank[rows, 0:128 * keys.shape[1]], q[:, g, :], keys, start=True, stop=True)
                        if c == 3:
                            for g in range(3):
                                mm = pe.matmul(bank[rows, 128 + 16 * g:144 + 16 * g], q[:, g, :],
                                               qkT[:, 12 + g, 256 + 16 * p:272 + 16 * p], start=True, stop=True)
                    mm.then_inc(*full(("ss", p, c)))

            def sample_values(p):
                pe.wait_ge(*act_done.at(("sp", p)))
                for c in range(4):
                    pieces = [((b - 4 * c) * 128, ssm[:, b * 128:(b + 1) * 128]) for b in range(4 * c, min(13, 4 * c + 4))]
                    if c == 3:
                        pieces += [((1 + g) * 128, ssm[:, SBLK * 128 + 16 * g:SBLK * 128 + 16 * g + 16]) for g in range(3)]
                    transposes(("spt", p, c), pieces)
                for c in range(4):
                    pe.wait_ge(*freed(("spt", p, c)))
                if p == 0:
                    pe.wait_ge(vnew_in.sem, 64)
                bank = claim(pe, ("so", p))
                for b2 in range(2):
                    rows = slice(64 * b2, 64 * b2 + 64)
                    for b in range(13):
                        pe.matmul(bank[rows, 0:128], pts[:, b, rows], cache[:, p % 2, 1, 13 * b2 + b, :], start=(b == 0), stop=False)
                    for g in range(3):
                        mm = pe.matmul(bank[rows, 0:128], pts[0:16, 13 + g, rows], vnew[0:16, p, 128 * g:128 * g + 128],
                                       start=False, stop=(g == 2))
                mm.then_inc(*full(("so", p)))

            def sample_turn(p):
                pe.wait_ge(*dve_done.at(("so", p)))
                transposes(("soT", p), [(0, so)])

            sample_keys(0)
            sample_scores(0)
            for p in range(4):
                if p + 1 < 4:
                    sample_keys(p + 1)
                sample_values(p)
                if p + 1 < 4:
                    sample_scores(p + 1)
                sample_turn(p)
            for t in range(2):
                pe.wait_ge(*freed(("oT", t)))
            pe.wait_ge(*dve_done.at(("oT", 3)))
            project("wo", 2, 4)
            ffn(1)

        @block.sync
        def _(sp):
            def load_gain(i, name, row):
                sp.dma_start(gain[:, i, :], row.to_broadcast([128, D])).then_inc(*gain_in[i].mark(name, 16))

            sp.dma_start(cst[:, :], I["constants"]).then_inc(*cst_in.mark("cst", 16))
            for t in range(3):
                src = I["x_prompt"][0, OFF[t]:OFF[t] + 128, :] if t < 2 else I["x_sample"].rearrange("b s d -> (b s) d")
                sp.dma_start(h[0:ROWS[t], t, :], src).then_inc(*h_in[t].mark("x", 16))
            load_gain(0, "mix0", I["norm_mix"][0:1, :])
            sp.dma_start(conv_rows[0:24, :], I["state_conv"][0].rearrange("b w c -> (b w) c")).then_inc(rows_in.sem, 16)
            sp.dma_start(conv_rows[24:28, :], I["ssm_conv_w"][0]).then_inc(rows_in.sem, 16)
            sp.dma_start(conv_rows[28:29, :], I["ssm_conv_b"]).then_inc(rows_in.sem, 16)
            sp.dma_start(ng_rows, I["ssm_norm"][0].rearrange("(c p) -> c p", p=128)).then_inc(rows_in.sem, 16)
            sp.dma_start(w_dt, I["w_in"][:, DT_COL:DT_COL + 32].rearrange("(k p) n -> p k n", p=128)).then_inc(dtw_in.sem, 16)
            sp.wait_ge(*dve_done.at("small"))
            sp.dma_start(small[:, 1136:1184], I["angles"]).then_inc(angles_in.sem, 16)
            sp.dma_start(a_bc, I["ssm_a_log"].to_broadcast([128, 32])).then_inc(vec_in.sem, 16)
            sp.dma_start(dtb_bc, I["ssm_dt_bias"].to_broadcast([128, 32])).then_inc(vec_in.sem, 16)
            sp.dma_start(d_bc, I["ssm_d"].to_broadcast([128, 32])).then_inc(vec_in.sem, 16)
            load_weights(sp, load_index[("out", 0, 0)])
            for q in range(8):
                sp.wait_ge(*freed(("newst", q)))
                cols = slice(q * 512, (q + 1) * 512)
                sp.dma_start(O["prompt_conv"][0, 0, :, cols], newst[0:3, q % 2, :]).then_inc(*newst_out[q % 2].mark(by=16))
                sp.dma_start(O["sample_conv"][0, :, :, cols].rearrange("b w c -> (b w) c"), newst[3:27, q % 2, :])\
                  .then_inc(*newst_out[q % 2].mark(q, 16))
            load_weights(sp, load_index[("out", 0, 0)] + 2)

            def store_state(blk):
                sp.wait_ge(*dve_done.at(("hnew", blk)))
                sp.dma_start(O["sample_ssm"][0, :, 2 * blk:2 * blk + 2, :, :].rearrange("b h p n -> (h p) b n"),
                             hnew[:, blk % 2, :, :]).then_inc(*hnew_out[blk % 2].mark(blk, 16))

            for t in range(3):
                for half in range(2):
                    sp.wait_ge(*full_at(("uT", "mix0", t, half)))
            for blk in range(16):
                if blk >= 3:
                    sp.wait_ge(*dve_done.at(("hnew", blk - 3)))
                sp.dma_start(h0[:, blk % 3, :, :],
                             I["state_ssm"][0, :, 2 * blk:2 * blk + 2, :, :].rearrange("b h p n -> (h p) b n"))\
                  .then_inc(*h0_in[blk % 3].mark(blk, 16))
                if blk == 2:
                    for g in range(8):
                        sp.wait_ge(*freed(("hfin", g)))
                        sp.dma_start(O["prompt_ssm"][0, 0, 4 * g:4 * g + 4, :, :].rearrange("(i h) p n -> (h p) i n", i=2),
                                     hfin[:, g % 2, :].rearrange("p (i n) -> p i n", i=2)).then_inc(*hfin_out[g % 2].mark(g, 16))
                if blk >= 3:
                    store_state(blk - 3)
            for blk in (13, 14, 15):
                store_state(blk)
            for blk in (14, 15):
                sp.wait_ge(*hnew_out[blk % 2].at(blk))
            load_weights(sp, load_index[("query0", 0, 0)])

            def ffn(l):
                sp.dma_start(sk_raw, I["peer_sub_keys"][l].rearrange("c k d -> k c d")).then_inc(*sk_in.mark(l, 16))
                load_gain(1, f"ffn{l}", I["norm_ffn"][l:l + 1, :])
                load_gain(0, f"ple{l}", I["norm_ple"][l:l + 1, :])
                for t in range(3):
                    src = I["p_prompt"][l, 0, OFF[t]:OFF[t] + 128, :] if t < 2 else I["p_sample"][l].rearrange("b s d -> (b s) d")
                    sp.dma_start(p_rows[0:ROWS[t], t, :], src).then_inc(*prow_in.mark(l, 16))
                load_weights(sp, load_index[(f"pgate{l}", 1, 1)] + 1)

            sp.wait_ge(*freed(("yT", 2, 3)))
            ffn(0)
            load_gain(1, "kv", I["kv_norm"].rearrange("(a d) -> a d", a=1))
            load_gain(0, "mix1", I["norm_mix"][1:2, :])
            sp.dma_start(gq, I["q_norm"].to_broadcast([128, 64])).then_inc(qk_gain_in.sem, 16)
            sp.dma_start(gk, I["k_norm"].rearrange("(a d) -> a d", a=1).to_broadcast([128, 64])).then_inc(qk_gain_in.sem, 16)
            load_weights(sp, load_index[("wo", 0, 0)])
            for t in range(3):
                for half in range(2):
                    sp.wait_ge(*full_at(("uT", "mix1", t, half)))
            sp.dma_start(masks, I["masks"]).then_inc(masks_in.sem, 16)
            for t in range(3):
                sp.wait_ge(*dve_done.at(("rope", t)))
                for name, src in (("k", qkn[:, t, NQH:, :].rearrange("p h d -> p (h d)")), ("v", kvs[:, t, 384:768])):
                    dst = O["prompt_" + name][0, OFF[t]:OFF[t] + 128] if t < 2 else O["sample_" + name].rearrange("b s h d -> (b s) h d")
                    sp.dma_start(dst.rearrange("t h d -> t (h d)"), src[0:ROWS[t], :]).then_inc(stored.sem, 16)
            for p in range(4):
                sp.dma_start(vnew[0:16, p, :], kvs[16 * p:16 * p + 16, 2, 384:768]).then_inc(vnew_in.sem, 16)
            for p in range(4):
                if p == 1:
                    for g in range(4):
                        sp.wait_ge(*full_at(("qk", 2, g)))
                    sp.wait_ge(stored.sem, 96)
                if p >= 2:
                    sp.wait_ge(*full_at(("so", p - 2)))
                for w, name in enumerate(("cache_k", "cache_v")):
                    for b2 in range(2):
                        rows, dst = I[name][2 * p + b2], cache[:, p % 2, w, 13 * b2:13 * b2 + 13, :]
                        cut = lambda r, g: r[:, :, 2 * g:2 * g + 2, :].rearrange("b m h d -> m b (h d)")
                        sp.dma_start(dst[:, 0:4, :], cut(rows[PAST - 512:, :, :].rearrange("(b m) h d -> b m h d", m=128), 1))\
                          .then_inc(*cache_in[p % 2].mark(by=16))
                        sp.dma_start(dst[:, 4:12, :], cut(rows.rearrange("(m b) h d -> b m h d", b=16)[0:8], 2))\
                          .then_inc(*cache_in[p % 2].mark(by=16))
                        sp.dma_start(dst[:, 12, :], rows[PAST - 128:, 0:2, :].rearrange("m h d -> m (h d)"))\
                          .then_inc(*cache_in[p % 2].mark(p, by=16))
            load_weights(sp, load_index[("query1", 0, 0)])
            sp.wait_ge(*full_at(("wo", 0, 0)))
            ffn(1)
            for t in range(3):
                sp.wait_ge(*dve_done.at(("ple", 1, 1, t)))
                dst = O["y_prompt"][0, OFF[t]:OFF[t] + 128, :] if t < 2 else O["y_sample"].rearrange("b s d -> (b s) d")
                sp.dma_start(dst, h[0:ROWS[t], t, :]).then_inc(stored.sem, 16)
            sp.wait_ge(stored.sem, 144)
            for g in (6, 7):
                sp.wait_ge(*hfin_out[g % 2].at(g))
                sp.wait_ge(*newst_out[g % 2].at(g))

        @block.scalar
        def _(act):
            s, freeing = stepper(act, act_order)

            def norm(key, ready):
                act.wait_ge(*dve_done.at("small"))
                for t in range(3):
                    act.wait_ge(*ready(t))
                    s(act.activation(u[0:ROWS[t], t, :], h[0:ROWS[t], t, :], ACT.Square,
                                     accum_out=ssq[0:ROWS[t], t:t + 1]), squares, (key, t))
                for t in range(3):
                    for half in range(2):
                        bank = filled(act, ("uT", key, t, half))
                        freeing(act.activation(uT[:, 4 * half:4 * half + 4, OFF[t]:OFF[t] + ROWS[t]],
                                               bank.rearrange("p (j r) -> p j r", j=4)[:, :, 0:ROWS[t]], ACT.Copy),
                                ("uT", key, t, half))

            for half in range(2):
                bank = filled(act, ("rows", half))
                freeing(act.activation(stT[:, 16 * half:16 * half + 16, :],
                                       bank[:, 0:464].rearrange("p (j r) -> p j r", j=16), ACT.Copy), ("rows", half))
            act.wait_ge(*dve_done.at("small"))
            bank = filled(act, "ng")
            freeing(act.activation(ngT, bank[:, 0:16], ACT.Copy), "ng")
            norm("mix0", lambda t: h_in[t].at("x"))
            act.wait_ge(vec_in.sem, 48)
            s(act.activation(a_bc, a_bc, ACT.Exp), act_done, "a")
            act.wait_ge(*dve_done.at("dt_abs"))
            s(act.activation(dtmp, dtmp, ACT.Exp, scale=-1.0))
            s(act.activation(dtmp2, dtmp, ACT.Ln, bias=1.0), act_done, "dt_ln")
            for n in range(4):
                for t in range(3):
                    bank = filled(act, ("z", n, t))
                    s(act.activation(z[0:ROWS[t], t, n * 512:(n + 1) * 512], bank[0:ROWS[t], :], ACT.Tanh, scale=0.5),
                      act_done, ("ztanh", n, t))

            def conv_tanh(b):
                act.wait_ge(*dve_done.at(("conv", b)))
                s(act.activation(sg[:, b % 3, :], cacc[:, b % 3, :], ACT.Tanh, scale=0.5), act_done, ("ctanh", b))

            def take_tokens(n):
                for t in range(3):
                    bank = filled(act, ("tok", n, t))
                    dst = xs[0:ROWS[t], t, n * 512:(n + 1) * 512] if n < 4 else btok[0:ROWS[t], t, (n - 4) * 512:(n - 3) * 512]
                    freeing(act.activation(dst, bank[0:ROWS[t], :], ACT.Copy), ("tok", n, t))

            for b in range(CONV_BLKS):
                bank = filled(act, ("xbc", b))
                act.wait_ge(*pool_done.at(("rawstate", b)))
                s(act.activation(raw[:, b % 4, 3:259], bank[:, 0:256], ACT.Copy))
                freeing(act.activation(raw[:, b % 4, 259:347].rearrange("p (b w) -> p b w", b=8)[:, :, 3:11],
                                       bank[:, 256:320].rearrange("p (b w) -> p b w", b=8), ACT.Copy), ("xbc", b))
                if b >= 1:
                    conv_tanh(b - 1)
                if 7 <= b <= 27 and b % 4 == 3:
                    take_tokens(b // 4 - 1)
            conv_tanh(CONV_BLKS - 1)
            for q in range(8):
                bank = filled(act, ("newst", q))
                if q >= 2:
                    act.wait_ge(*newst_out[q % 2].at(q - 2))
                freeing(act.activation(newst[0:27, q % 2, :], bank[0:27, :], ACT.Copy), ("newst", q))

            for t in range(3):
                R = ROWS[t]
                bank = filled(act, ("cum", t))
                freeing(act.activation(ex[0:R, t, :], bank[0:R, 0:96], ACT.Exp), ("cum", t))
                if t == 2:
                    bank = filled(act, "ec")
                    freeing(act.activation(ec, bank[:, 0:128].rearrange("p (k b) -> p k b", k=16), ACT.Exp), "ec")
                for g in range(GROUPS):
                    x, n = step_of(t, g) % 2, step_of(t, g)
                    if n >= 2:
                        act.wait_ge(*full_at(("y", (n - 2) // 8, (n - 2) % 8)))
                    bank = filled(act, ("seg", t, g))
                    freeing(act.activation(dec[0:R, x, 0:4 * R], bank[0:R, 0:4 * R], ACT.Exp), ("seg", t, g))
                    if t == 2:
                        for i in range(2):
                            for q in range(2):
                                bank = filled(act, ("h0T", 2 * g + i, q))
                                if g >= 1:
                                    act.wait_ge(*full_at(("inter", 2, g - 1)))
                                freeing(act.activation(h0T[:, i, 4 * q:4 * q + 4, :],
                                                       bank.rearrange("p (b n) -> p b n", b=4), ACT.Copy),
                                        ("h0T", 2 * g + i, q))
                    if t == 1:
                        bank = filled(act, ("hfin", g))
                        if g >= 2:
                            act.wait_ge(*hfin_out[g % 2].at(g - 2))
                        freeing(act.activation(hfin[:, g % 2, :], bank[:, 0:256], ACT.Copy), ("hfin", g))
                    act.wait_ge(*dve_done.at(("gated", t, g)))
                    s(act.activation(yt[0:R, x, :], z[0:R, t, g * 256:(g + 1) * 256], ACT.Square,
                                     accum_out=gvar[0:R, t, g:g + 1]), act_done, ("gsq", t, g))

            def take_scores(l, t, quads=range(4)):
                for q in quads:
                    bank = filled(act, ("score", l, t, q))
                    if t == 2 and q == 0:
                        act.wait_ge(*dve_done.at(("picked", l, 0)))
                    if t < 2 or q < 2:
                        freeing(act.activation(sc[:, t % 2, 4 * q:4 * q + 4, :], bank.rearrange("p (j r) -> p j r", j=4), ACT.Copy),
                                ("score", l, t, q))
                    else:
                        freeing(act.activation(small[0:64, 1201:1202], bank[0:64, 0:1], ACT.Copy), ("score", l, t, q))

            def gate_exp(l, t):
                x, n = t % 2, HPT[t] * TOPK
                act.wait_ge(*dve_done.at(("gate_in", l, t)))
                s(act.activation(pgate[:, x, 0:n], pgate[:, x, 0:n], ACT.Exp), act_done, ("gate_exp", l, t))

            def coefficients(l, t):
                x, n = t % 2, HPT[t] * TOPK
                act.wait_ge(*dve_done.at(("gelu_in", l, t)))
                s(act.activation(ptmp[:, 0:n], ptmp[:, 0:n], ACT.Tanh, scale=0.7978845608028654), act_done, ("gelu_tanh", l, t))
                act.wait_ge(*dve_done.at(("coef", l, t)))
                R, base = ROWS[t], v_base(l, t)
                cols = coef[:, x, :].rearrange("p (n k) -> p n k", k=PSLOTS)
                unit = ident if t < 2 else cst[:, C_ID2:C_ID2 + 64]
                with act.Fori(0, peer_rounds(t), 1) as i:
                    for d, k in enumerate(VPE):
                        act.wait_ge(slot_free[k].sem, i + (base + 1))
                        act.activation(diag[:, d, 0:R], unit, ACT.Copy, scale=cols[:, bass.ds(i, 1), k])\
                           .then_inc(diag_made.sem, 1)

            def ffn(l):
                bank = filled(act, ("sk", l))
                freeing(act.activation(skT, bank[:, 0:256].rearrange("p (c k) -> p c k", c=2), ACT.Copy), ("sk", l))
                norm(f"ffn{l}", lambda t: dve_done.at(("h", "mix", l, t)))
                for n in range(5):
                    for b in range(4 * n, 4 * n + 4 if n < 4 else 16):
                        bank = filled(act, ("q", l, b))
                        freeing(act.activation(qT[:, b, :], bank[:, 0:NTOK], ACT.Copy), ("q", l, b))
                    if n >= 1:
                        take_scores(l, 0, [n - 1])
                take_scores(l, 1)
                gate_exp(l, 0)
                take_scores(l, 2)
                gate_exp(l, 1)
                coefficients(l, 0)
                gate_exp(l, 2)
                coefficients(l, 1)
                coefficients(l, 2)
                for t in range(3):
                    bank = filled(act, ("pT", l, t))
                    freeing(act.activation(pT[:, :, OFF[t]:OFF[t] + ROWS[t]],
                                           bank[:, 0:256].rearrange("p (c r) -> p c r", c=2)[:, :, 0:ROWS[t]], ACT.Copy), ("pT", l, t))
                norm(f"ple{l}", lambda t: dve_done.at(("h", "peer", l, t)))
                for n in range(2):
                    for t in range(3):
                        bank = filled(act, (f"pgate{l}", n, t))
                        if n == 1:
                            act.wait_ge(*dve_done.at(("ple", l, 0, t)))
                        freeing(act.activation(sgate[0:ROWS[t], t, :], bank[0:ROWS[t], :], ACT.Tanh, scale=0.5), (f"pgate{l}", n, t))

            ffn(0)

            norm("kv", lambda t: dve_done.at(("ple", 0, 1, t)))
            for n in range(2):
                for t in range(3):
                    bank = filled(act, ("kv", n, t))
                    freeing(act.activation(kvs[0:ROWS[t], t, n * 512:n * 512 + (512 if n == 0 else 256)],
                                           bank[0:ROWS[t], 0:(512 if n == 0 else 256)], ACT.Copy), ("kv", n, t))
            norm("mix1", lambda t: dve_done.at(("ple", 0, 1, t)))
            for n in range(3):
                for t in range(3):
                    bank = filled(act, ("wq", n, t))
                    freeing(act.activation(q_raw[0:ROWS[t], t, n * 512:(n + 1) * 512], bank[0:ROWS[t], :], ACT.Copy), ("wq", n, t))
            for t in range(3):
                R = ROWS[t]
                if t >= 1:
                    act.wait_ge(*dve_done.at(("qsum", t - 1)))
                s(act.activation(sq_buf[0:R, 0:NQH, :].rearrange("p h d -> p (h d)"), q_raw[0:R, t, :], ACT.Square))
                s(act.activation(sq_buf[0:R, NQH:, :].rearrange("p h d -> p (h d)"), kvs[0:R, t, 0:384], ACT.Square),
                  act_done, ("qsq", t))
            for t in range(3):
                for g in range(4):
                    bank = filled(act, ("qk", t, g)).rearrange("p (j r) -> p j r", j=4)
                    if t < 2 or g == 3:
                        n = 4 if g < 3 else 3
                        freeing(act.activation(qkT[:, 4 * g:4 * g + n, OFF[t]:OFF[t] + ROWS[t]], bank[:, 0:n, 0:ROWS[t]], ACT.Copy),
                                ("qk", t, g))
                    else:
                        act.wait_ge(*dve_done.at("qst_zero"))
                        for r in range(2):
                            rows = slice(64 * r, 64 * r + 64)
                            dst = qst[rows, g, :, 32 * r:32 * r + 32].rearrange("p b (j i) -> p b j i", j=4)
                            src = bank[rows, :, 0:64].rearrange("p j (b i) -> p b j i", i=8)
                            for j in range(4):
                                ins = act.activation(dst[:, :, j, :], src[:, :, j, :], ACT.Copy)
                                if r == 1 and j == 3:
                                    freeing(ins, ("qk", t, g))
                                else:
                                    s(ins)

            def prompt_exp(t, hd):
                x, n = hd % 2, 384 * (t + 1)
                act.wait_ge(*dve_done.at(("max", t, hd)))
                s(act.activation(sm[:, x, 0:n], sm[:, x, 0:n], ACT.Exp, bias=negmax[:, x:x + 1], accum_out=zsum[:, x:x + 1]),
                  act_done, ("p", t, hd))

            def prompt_turn(t, hd):
                x, n = hd % 2, 3 * (t + 1)
                for c in range(t + 1):
                    bank = filled(act, ("pt", t, hd, c))
                    m = min(n, 4 * c + 4) - 4 * c
                    freeing(act.activation(pt[:, x, 4 * c:4 * c + m, :], bank.rearrange("p (b r) -> p b r", b=4)[:, 0:m, :], ACT.Copy),
                            ("pt", t, hd, c))

            for t in range(2):
                for hd in range(8):
                    prompt_exp(t, hd)
                    prompt_turn(t, hd)
                bank = filled(act, ("oT", t))
                freeing(act.activation(uT[:, 0:4, OFF[t]:OFF[t] + 128], bank.rearrange("p (c r) -> p c r", c=4), ACT.Copy), ("oT", t))

            def sample_keys(p):
                for c in range(7):
                    bank = filled(act, ("kc", p, c))
                    n = min(26, 4 * c + 4) - 4 * c
                    if p >= 1:
                        act.wait_ge(*full_at(("ss", p - 1, 3)))
                    freeing(act.activation(kcT[:, 4 * c:4 * c + n, :], bank.rearrange("p (b r) -> p b r", b=4)[:, 0:n, :], ACT.Copy),
                            ("kc", p, c))

            def sample_exp(p):
                act.wait_ge(*dve_done.at(("smax", p)))
                s(act.activation(ssm, ssm, ACT.Exp, bias=negmax[:, 0:1], accum_out=zsum[:, 0:1]), act_done, ("sp", p))

            def sample_turn(p):
                for c in range(4):
                    bank = filled(act, ("spt", p, c)).rearrange("p (b r) -> p b r", b=4)
                    if p >= 1:
                        act.wait_ge(*full_at(("so", p - 1)))
                    if c < 3:
                        freeing(act.activation(pts[:, 4 * c:4 * c + 4, :], bank, ACT.Copy), ("spt", p, c))
                    else:
                        s(act.activation(pts[:, 12, :], bank[:, 0, :], ACT.Copy))
                        freeing(act.activation(pts[0:16, 13:16, :], bank[0:16, 1:4, :], ACT.Copy), ("spt", p, c))

            sample_keys(0)
            for p in range(4):
                sample_exp(p)
                if p + 1 < 4:
                    sample_keys(p + 1)
                sample_turn(p)
            ffn(1)

        @block.vector
        def _(dve):
            s, freeing = stepper(dve, dve_order)

            def rsqrt(r, v, tmp):
                s(dve.tensor_scalar(tmp.bitcast(U32), v.bitcast(U32), 1, None, ALU.logical_shift_right))
                s(dve.tensor_scalar(r.bitcast(I32), tmp.bitcast(I32), -1.0, float(0x5F3759DF), ALU.mult, ALU.add))
                for _ in range(4):
                    s(dve.tensor_tensor(tmp, r, r, ALU.mult))
                    s(dve.tensor_tensor(tmp, tmp, v, ALU.mult))
                    s(dve.tensor_scalar(tmp, tmp, -0.5, 1.5, ALU.mult, ALU.add))
                    s(dve.tensor_tensor(r, r, tmp, ALU.mult))

            def norm(key, i):
                dve.wait_ge(*squares.at((key, 2)))
                s(dve.tensor_scalar(var[:, 0:3], ssq[:, 0:3], 1.0 / D, EPS, ALU.mult, ALU.add))
                rsqrt(rstd[:, 0:3], var[:, 0:3], nwt[:, 0:3])
                dve.wait_ge(*gain_in[i].at(key))
                for t in range(3):
                    R = ROWS[t]
                    s(dve.scalar_tensor_tensor(u[0:R, t, :], h[0:R, t, :], rstd[0:R, t:t + 1], gain[0:R, i, :],
                                               ALU.mult, ALU.mult), u_ready, (key, t))

            s(dve.memset(small[:, :], 0.0), dve_done, "small")
            norm("mix0", 0)
            dve.wait_ge(vec_in.sem, 48)
            for t in range(3):
                bank = filled(dve, ("dt", t))
                freeing(dve.tensor_tensor(dt[0:ROWS[t], t, :], bank[0:ROWS[t], 0:32], dtb_bc[0:ROWS[t], :], ALU.add), ("dt", t))
            s(dve.scalar_tensor_tensor(dtmp, dt, -1.0, dt, ALU.mult, ALU.max), dve_done, "dt_abs")
            dve.wait_ge(*act_done.at("dt_ln"))
            s(dve.tensor_scalar(dtmp3, dtmp, 1.0, -1.0, ALU.add, ALU.add))
            s(dve.tensor_scalar(da, dtmp3, 0.0, None, ALU.is_equal))
            s(dve.tensor_tensor(dtmp3, dtmp3, da, ALU.add))
            s(dve.tensor_tensor(dtmp2, dtmp2, da, ALU.add))
            s(dve.reciprocal(dtmp3, dtmp3))
            s(dve.tensor_tensor(dtmp2, dtmp2, dtmp3, ALU.mult))
            s(dve.tensor_tensor(dtmp2, dtmp2, dtmp, ALU.mult))
            s(dve.scalar_tensor_tensor(dt, dt, 0.0, dtmp2, ALU.max, ALU.add))
            s(dve.scalar_tensor_tensor(da, dt, -1.0, repeat(a_bc, 3), ALU.mult, ALU.mult), dve_done, "da")
            for n in range(4):
                for t in range(3):
                    zz = z[0:ROWS[t], t, n * 512:(n + 1) * 512]
                    dve.wait_ge(*act_done.at(("ztanh", n, t)))
                    s(dve.tensor_scalar(zz, zz, 0.5, 0.5, ALU.mult, ALU.add))
                    bank = filled(dve, ("z", n, t))
                    freeing(dve.tensor_tensor(zz, zz, bank[0:ROWS[t], :], ALU.mult), ("z", n, t))

            def conv(b):
                dve.wait_ge(*freed(("xbc", b)))
                if b >= 3:
                    dve.wait_ge(*act_done.at(("ctanh", b - 3)))
                p = raw[:, b % 4, 0:259]
                q = raw[:, b % 4, 259:347].rearrange("p (b w) -> p b w", b=8)
                outs = cacc[:, b % 3, 0:256], cacc[:, b % 3, 256:320].rearrange("p (b w) -> p b w", b=8)
                tap = lambda w: stT[:, b, 24 + w:25 + w]
                s(dve.tensor_scalar(outs[0], p[:, 0:256], tap(0), tap(4), ALU.mult, ALU.add))
                s(dve.tensor_scalar(outs[1], q[:, :, 0:8], tap(0), tap(4), ALU.mult, ALU.add))
                for w in range(1, CONV_W):
                    s(dve.scalar_tensor_tensor(outs[0], p[:, w:w + 256], tap(w), outs[0], ALU.mult, ALU.add))
                    s(dve.scalar_tensor_tensor(outs[1], q[:, :, w:w + 8], tap(w), outs[1], ALU.mult, ALU.add),
                      *((dve_done, ("conv", b)) if w == CONV_W - 1 else ()))

            def silu(b):
                dve.wait_ge(*act_done.at(("ctanh", b)))
                e = sg[:, b % 3, :]
                s(dve.tensor_scalar(e, e, 0.5, 0.5, ALU.mult, ALU.add))
                if 8 <= b < 16:
                    for t in range(3):
                        dve.wait_ge(*full_at(("tok", b // 4 - 2, t)))
                dst = xc[:, b % 8, :] if b < 16 else bcT[:, b - 16, :]
                s(dve.tensor_tensor(dst, e, cacc[:, b % 3, :], ALU.mult), dve_done, ("silu", b))

            for b in range(CONV_BLKS):
                conv(b)
                if b >= 1:
                    silu(b - 1)
            silu(CONV_BLKS - 1)

            def decays(n):
                t, g = divmod(n, GROUPS)
                R, x = ROWS[t], n % 2
                if n >= 2:
                    dve.wait_ge(*full_at(("seg", (n - 2) // 8, (n - 2) % 8)))
                s(dve.tensor_tensor(seg_l[0:R, x, :, 0:R], repeat(strict_of(t), 4), spread(da[0:R, t, 4 * g:4 * g + 4], R),
                                    ALU.mult), dve_done, ("seg", t, g))

            for q in range(8):
                dve.wait_ge(*full_at(("newst", q)))
            for q in (6, 7):
                dve.wait_ge(*newst_out[q % 2].at(q))
            s(dve.memset(ctm[:, :, :, :], 0.0), dve_done, "scan_area")
            decays(0)
            for n in range(3 * GROUPS):
                t, g = divmod(n, GROUPS)
                R, x = ROWS[t], n % 2
                if n + 1 < 3 * GROUPS:
                    decays(n + 1)
                bank = filled(dve, ("cb", t, g))
                freeing(dve.tensor_tensor(cbm[0:R, x, 0:R], bank[0:R, 0:R], tri_of(t), ALU.mult), ("cb", t, g))
                dve.wait_ge(*freed(("seg", t, g)))
                d = dec[0:R, x, 0:4 * R].rearrange("p (j r) -> p j r", j=4)
                s(dve.tensor_tensor(d, d, repeat(cbm[0:R, x, 0:R], 4), ALU.mult), dve_done, ("m", t, g))
                if t == 2:
                    if g >= 1:
                        dve.wait_ge(*full_at(("hupd", 2 * g - 1, 1)))
                    s(dve.tensor_tensor(bm[0:64, :, :], repeat(btok[0:64, 2, g * 128:(g + 1) * 128], 8),
                                        spread(cst[0:64, C_BM:C_BM + 8], 128), ALU.mult), dve_done, ("bm", g))
                    for i in range(2):
                        blk = 2 * g + i
                        dve.wait_ge(*pool_done.at(("h0s", blk)))
                        if blk >= 2:
                            dve.wait_ge(*hnew_out[blk % 2].at(blk - 2))
                        for q in range(2):
                            bank = filled(dve, ("hupd", blk, q))
                            freeing(dve.tensor_tensor(hnew[:, i, 4 * q:4 * q + 4, :], h0[:, blk % 3, 4 * q:4 * q + 4, :],
                                                      bank.rearrange("p (b n) -> p b n", b=4), ALU.add), ("hupd", blk, q))
                        s(dve.tensor_copy(small[:, 1200:1201], cst[:, 0:1]), dve_done, ("hnew", blk))
                y = yt[0:R, x, :]
                if n >= 2:
                    dve.wait_ge(*act_done.at(("gsq", (n - 2) // 8, (n - 2) % 8)))
                dve.wait_ge(*pool_done.at(("dxs", t, g)))
                if t == 0:
                    bank = filled(dve, ("y", t, g))
                    freeing(dve.tensor_tensor(y, bank[0:R, 0:256], dxs[0:R, x, :], ALU.add), ("y", t, g))
                else:
                    bank = filled(dve, ("inter", t, g))
                    freeing(dve.tensor_tensor(heads(y), heads(bank[0:R, 0:256]), spread(ex[0:R, t, 4 * g:4 * g + 4], 64),
                                              ALU.mult), ("inter", t, g))
                    s(dve.tensor_tensor(y, y, dxs[0:R, x, :], ALU.add))
                    bank = filled(dve, ("y", t, g))
                    freeing(dve.tensor_tensor(y, y, bank[0:R, 0:256], ALU.add), ("y", t, g))
                zz = z[0:R, t, g * 256:(g + 1) * 256]
                s(dve.tensor_tensor(zz, zz, y, ALU.mult), dve_done, ("gated", t, g))
                if t == 0:
                    bank = filled(dve, ("state", t, g))
                    freeing(dve.tensor_copy(hT[:, g, :], bank[:, 0:256]), ("state", t, g))
                if t == 1:
                    s(dve.tensor_tensor(heads(hT[:, g, :]), heads(hT[:, g, :]), spread(ex[:, t, 64 + 4 * g:68 + 4 * g], 64), ALU.mult))
                    bank = filled(dve, ("state", t, g))
                    freeing(dve.tensor_tensor(hT[:, g, :], hT[:, g, :], bank[:, 0:256], ALU.add), ("state", t, g))
                if g == GROUPS - 1:
                    dve.wait_ge(*act_done.at(("gsq", t, g)))
                    s(dve.tensor_scalar(gvar[0:R, t, :], gvar[0:R, t, :], 1.0 / 256, EPS, ALU.mult, ALU.add))
                    rsqrt(grstd[0:R, t, :], gvar[0:R, t, :], gnwt[0:R, t, :])
                    zg = z[0:R, t, :].rearrange("p (g d) -> p g d", g=GROUPS)
                    s(dve.tensor_tensor(zg, zg, spread(grstd[0:R, t, :], 256), ALU.mult), dve_done, ("ynorm", t))
                    for q in range(4):
                        bank = filled(dve, ("yT", t, q))
                        freeing(dve.tensor_tensor(uT[:, 4 * q:4 * q + 4, OFF[t]:OFF[t] + R],
                                                  bank.rearrange("p (j r) -> p j r", j=4)[:, :, 0:R],
                                                  spread(ngT[:, 4 * q:4 * q + 4], R), ALU.mult), ("yT", t, q))

            def add_to_h(key, l):
                for n in range(2):
                    for t in range(3):
                        hh = h[0:ROWS[t], t, n * 512:(n + 1) * 512]
                        bank = filled(dve, (key, n, t))
                        freeing(dve.tensor_tensor(hh, hh, bank[0:ROWS[t], :], ALU.add), (key, n, t))
                        if n == 1:
                            dve_done.counts[("h", "mix", l, t)] = dve_done.n + 1
                            s(dve.tensor_copy(small[:, 1200:1201], cst[:, 0:1]), dve_done, ("h", "mix", l, t))

            def top16(values, out_v, out_i):
                for half in range(2):
                    o = slice(8 * half, 8 * half + 8)
                    s(dve.max(out_v[:, o], values))
                    s(dve.max_index(out_i[:, o], out_v[:, o], values))
                    if half == 0:
                        s(dve.match_replace(values, out_v[:, o], values, -3.0e38))

            def pick(l, t):
                H, x = HPT[t], t % 2
                n = H * TOPK
                for q in range(H // 2):
                    dve.wait_ge(*freed(("score", l, t, q)))
                    for hc in range(4 * q, 4 * q + 4):
                        top16(sc[:, x, hc, :], top_v[:, hc, :], top_i[:, hc, :])
                        yield
                pair = top_v[:, 0:2 * H, :].rearrange("p (h c) k -> p h c k", c=2)
                grid = cand[:, 0:H, :].rearrange("p h (a b) -> p h a b", a=TOPK)
                s(dve.tensor_tensor(grid, pair[:, :, 0, :].unsqueeze(3).to_broadcast([128, H, TOPK, TOPK]),
                                    pair[:, :, 1, :].unsqueeze(2).to_broadcast([128, H, TOPK, TOPK]), ALU.add))
                yield
                for hd in range(H):
                    top16(cand[:, hd, :], best_v[:, hd, :], best_j[:, hd, :])
                    yield
                s(dve.tensor_copy(top_f[:, 0:2 * H, :], top_i[:, 0:2 * H, :]))
                for shift, dst in ((True, best_a), (False, best_b)):
                    j32 = ptmp.bitcast(U32)[:, 0:n].rearrange("p (h k) -> p h k", h=H)
                    s(dve.tensor_scalar(j32, best_j[:, 0:H, :], 4 if shift else 15, None,
                                        ALU.logical_shift_right if shift else ALU.bitwise_and))
                    s(dve.tensor_copy(dst[:, 0:H, :], j32))
                yield
                keys = top_f[:, 0:2 * H, :].rearrange("p (h c) k -> p h c k", c=2)
                for c, (pos, dst) in enumerate(((best_a, pick1), (best_b, pick2))):
                    hot = onehot[:, 0:n, :]
                    s(dve.tensor_tensor(hot, pos[:, 0:H, :].rearrange("p h k -> p (h k)").unsqueeze(2).to_broadcast([128, n, 16]),
                                        cst[:, C_IOTA:C_IOTA + 16].unsqueeze(1).to_broadcast([128, n, 16]), ALU.is_equal))
                    yield
                    hot4 = hot.rearrange("p (h k) a -> p h k a", h=H)
                    s(dve.tensor_tensor(hot4, hot4, keys[:, :, c, :].unsqueeze(2).to_broadcast([128, H, TOPK, 16]), ALU.mult))
                    yield
                    s(dve.tensor_reduce(dst[:, 0:n], hot, AX.X, ALU.add))
                    yield
                s(dve.scalar_tensor_tensor(pick1[:, 0:n], pick1[:, 0:n], float(PK), pick2[:, 0:n], ALU.mult, ALU.add))
                s(dve.tensor_scalar(expert[:, x, 0:n], pick1[:, 0:n], float(l * EXPERTS), None, ALU.add), dve_done, ("expert", l, t))
                g = pgate[:, x, 0:n].rearrange("p (h k) -> p h k", h=H)
                s(dve.tensor_tensor(g, best_v[:, 0:H, :], best_v[:, 0:H, 0:1].to_broadcast([128, H, TOPK]), ALU.subtract),
                  dve_done, ("gate_in", l, t))
                dve_done.counts[("picked", l, t)] = dve_done.n
                yield
                dve.wait_ge(*act_done.at(("gate_exp", l, t)))
                s(dve.tensor_reduce(stt2[:, 0:H], g, AX.X, ALU.add))
                s(dve.reciprocal(stt2[:, 8:8 + H], stt2[:, 0:H]))
                s(dve.tensor_tensor(g, g, spread(stt2[:, 8:8 + H], TOPK), ALU.mult))

            def dots(l, t, beside=()):
                x, n, base = t % 2, HPT[t] * TOPK, u_base(l, t)
                cols = pact[:, x, :].rearrange("p (n k) -> p n k", k=PSLOTS)
                rounds = peer_rounds(t)

                def slots(first, last):
                    with dve.Fori(first, last, 1) as i:
                        for k in range(PSLOTS):
                            dve.wait_ge(gathered[k].sem, i * 16 + (base * 16 + 16))
                            dve.scalar_tensor_tensor(rows_buf[:, k, :], rows_buf[:, k, :], 1.0, u[:, t, :], ALU.mult, ALU.mult,
                                                     accum_out=cols[:, bass.ds(i, 1), k]).then_inc(slot_free[k].sem, 1)

                at = 0
                for step, _ in enumerate(beside):
                    if step % 2 == 0 and at < rounds:
                        slots(at, at + 1)
                        at += 1
                if at < rounds:
                    slots(at, rounds)
                for k in range(PSLOTS):
                    dve.wait_ge(slot_free[k].sem, base + rounds + 1)
                a, q = pact[:, x, 0:n], ptmp[:, 0:n]
                s(dve.tensor_tensor(q, a, a, ALU.mult))
                s(dve.tensor_scalar(q, q, 0.044715, 1.0, ALU.mult, ALU.add))
                s(dve.tensor_tensor(q, q, a, ALU.mult), dve_done, ("gelu_in", l, t))
                s(dve.tensor_scalar(ptmp2[:, 0:n], a, 0.5, None, ALU.mult))
                s(dve.tensor_tensor(ptmp2[:, 0:n], ptmp2[:, 0:n], pgate[:, x, 0:n], ALU.mult))
                dve.wait_ge(*act_done.at(("gelu_tanh", l, t)))
                s(dve.scalar_tensor_tensor(coef[:, x, 0:n], q, 1.0, ptmp2[:, 0:n], ALU.add, ALU.mult), dve_done, ("coef", l, t))

            def sum_rows(l, t):
                x, base, rounds = t % 2, v_base(l, t), peer_rounds(t)
                cols = coef[:, x, :].rearrange("p (n k) -> p n k", k=PSLOTS)
                s(dve.memset(u[:, t, :], 0.0))
                with dve.Fori(0, rounds, 1) as i:
                    for k, before, ahead in ((VDVE[0], VDVE[1], 1), (VDVE[1], VDVE[0], 2)):
                        dve.wait_ge(slot_free[before].sem, i + (base + ahead))
                        dve.wait_ge(gathered[k].sem, i * 16 + (base * 16 + 16))
                        dve.scalar_tensor_tensor(u[:, t, :], rows_buf[:, k, :], cols[:, bass.ds(i, 1), k], u[:, t, :],
                                                 ALU.mult, ALU.add).then_inc(slot_free[k].sem, 1)
                dve.wait_ge(slot_free[VDVE[1]].sem, base + rounds + 1)
                s(dve.tensor_copy(small[:, 1200:1201], cst[:, 0:1]), dve_done, ("vsum", l, t))

            def take_peer(l, t):
                for n in range(2):
                    bank = filled(dve, ("peer", l, t, n))
                    freeing(dve.tensor_copy(h[0:ROWS[t], t, n * 512:(n + 1) * 512], bank[0:ROWS[t], :]), ("peer", l, t, n))
                s(dve.tensor_copy(small[:, 1200:1201], cst[:, 0:1]), dve_done, ("h", "peer", l, t))

            def ffn(l):
                norm(f"ffn{l}", 1)
                s(dve.tensor_copy(u[64:128, 2, :], u[0:64, 2, :]))
                for _ in pick(l, 0):
                    pass
                for t in range(3):
                    dots(l, t, pick(l, t + 1) if t < 2 else ())
                    sum_rows(l, t)
                    take_peer(l, t)
                norm(f"ple{l}", 0)
                for n in range(2):
                    for t in range(3):
                        R = ROWS[t]
                        gt = sgate[0:R, t, :]
                        dve.wait_ge(*freed((f"pgate{l}", n, t)))
                        s(dve.tensor_scalar(gt, gt, 0.5, 0.5, ALU.mult, ALU.add))
                        bank = filled(dve, (f"pproj{l}", n, t))
                        freeing(dve.tensor_tensor(gt, gt, bank[0:R, :], ALU.mult), (f"pproj{l}", n, t))
                        hh = h[0:R, t, n * 512:(n + 1) * 512]
                        s(dve.tensor_tensor(hh, hh, gt, ALU.add), dve_done, ("ple", l, n, t))

            for k in range(PSLOTS):
                dve.sem_inc(slot_free[k].sem, 1)
            add_to_h("out", 0)
            ffn(0)

            norm("kv", 1)
            norm("mix1", 0)
            dve.wait_ge(qk_gain_in.sem, 32)
            s(dve.tensor_scalar(gq, gq, 0.125, None, ALU.mult))
            for t in range(3):
                dve.wait_ge(*act_done.at(("qsq", t)))
                R = ROWS[t]
                s(dve.tensor_reduce(qvar[0:R, t, :], sq_buf[0:R, :, :], AX.X, ALU.add), dve_done, ("qsum", t))
            for t in range(3):
                R = ROWS[t]
                v = qvar[0:R, t, :]
                s(dve.tensor_scalar(v, v, 1.0 / 64, EPS, ALU.mult, ALU.add))
                rsqrt(qrstd[0:R, t, :], v, qtmp[0:R, t, :])
                for g in range(3):
                    src = q_raw[0:R, t, g * 512:(g + 1) * 512].rearrange("p (r j d) -> p r j d", r=2, j=4)
                    dst = qkn[0:R, t, 8 * g:8 * g + 8, :].rearrange("p (j r) d -> p r j d", r=2)
                    by = qrstd[0:R, t, 8 * g:8 * g + 8].rearrange("p (r j) -> p r j", r=2).unsqueeze(3).to_broadcast([R, 2, 4, 64])
                    s(dve.tensor_tensor(dst, src, by, ALU.mult))
                kk, qq = qkn[0:R, t, NQH:, :], qkn[0:R, t, 0:NQH, :]
                s(dve.tensor_tensor(kk, heads(kvs[0:R, t, 0:384]), spread(qrstd[0:R, t, NQH:], 64), ALU.mult))
                s(dve.tensor_tensor(qq, qq, repeat(gq[0:R, :], NQH), ALU.mult))
                s(dve.tensor_tensor(kk, kk, repeat(gk[0:R, :], NKH), ALU.mult))
                dve.wait_ge(angles_in.sem, 16)
                x1, x2 = qkn[0:R, t, :, 0:8], qkn[0:R, t, :, 8:16]
                cos, sin = repeat(angles[0:R, t, 0, :], 30), repeat(angles[0:R, t, 1, :], 30)
                r4 = [arena[0:R, 16880 + 240 * i:17120 + 240 * i].rearrange("p (h f) -> p h f", h=30)
                      for i in range(4)]
                s(dve.tensor_tensor(r4[0], x1, cos, ALU.mult))
                s(dve.tensor_tensor(r4[1], x2, sin, ALU.mult))
                s(dve.tensor_tensor(r4[2], x2, cos, ALU.mult))
                s(dve.tensor_tensor(r4[3], x1, sin, ALU.mult))
                s(dve.tensor_tensor(x1, r4[0], r4[1], ALU.subtract))
                s(dve.tensor_tensor(x2, r4[2], r4[3], ALU.add), dve_done, ("rope", t))
                if t == 0:
                    s(dve.memset(qst, 0.0), dve_done, "qst_zero")

            def prompt_max(t, hd):
                x, n = hd % 2, 384 * (t + 1)
                dve.wait_ge(masks_in.sem, 16)
                if hd >= 2:
                    dve.wait_ge(*full_at(("o", t, hd - 2)))
                at = 0
                for c in range(t + 1):
                    m = 384 if t == 0 else (512, 256)[c]
                    bank = filled(dve, ("s", t, hd, c))
                    freeing(dve.tensor_tensor(sm[:, x, at:at + m], bank[:, 0:m], pmask[t][:, at:at + m], ALU.add), ("s", t, hd, c))
                    at += m
                s(dve.tensor_reduce(negmax[:, x:x + 1], sm[:, x, 0:n], AX.X, ALU.max, negate=True), dve_done, ("max", t, hd))

            def prompt_out(t, hd):
                x = hd % 2
                dve.wait_ge(*act_done.at(("p", t, hd)))
                s(dve.reciprocal(rz[:, x:x + 1], zsum[:, x:x + 1]))
                bank = filled(dve, ("o", t, hd))
                freeing(dve.tensor_scalar(osb[:, hd * 64:(hd + 1) * 64], bank[:, 0:64], rz[:, x:x + 1], None, ALU.mult), ("o", t, hd))

            for t in range(2):
                if t == 1:
                    dve.wait_ge(*full_at(("oT", 0)))
                for hd in range(9):
                    if hd < 8:
                        prompt_max(t, hd)
                    if hd >= 1:
                        prompt_out(t, hd - 1)
                s(dve.tensor_copy(small[:, 1200:1201], cst[:, 0:1]), dve_done, ("osb", t))

            def sample_max(p):
                if p >= 1:
                    for c in range(4):
                        dve.wait_ge(*full_at(("spt", p - 1, c)))
                for c in range(4):
                    at, m = 512 * c, 512 if c < 3 else SCOLS - 1536
                    bank = filled(dve, ("ss", p, c))
                    freeing(dve.tensor_tensor(ssm[:, at:at + m], bank[:, 0:m], smask[:, at:at + m], ALU.add), ("ss", p, c))
                s(dve.tensor_reduce(negmax[:, 0:1], ssm, AX.X, ALU.max, negate=True), dve_done, ("smax", p))

            def sample_out(p):
                dve.wait_ge(*act_done.at(("sp", p)))
                s(dve.reciprocal(rz[:, 0:1], zsum[:, 0:1]))
                bank = filled(dve, ("so", p))
                if p >= 1:
                    dve.wait_ge(*full_at(("soT", p - 1)))
                freeing(dve.tensor_scalar(so, bank[:, 0:128], rz[:, 0:1], None, ALU.mult), ("so", p))
                s(dve.tensor_copy(small[:, 1200:1201], cst[:, 0:1]), dve_done, ("so", p))

            def sample_back(p):
                bank = filled(dve, ("soT", p))[:, 0:128].rearrange("p (b r c f i) -> p b r c f i", b=2, r=2, c=2, f=2)
                for r in range(2):
                    for f in range(2):
                        for c in range(2):
                            src = bank[64 * r:64 * r + 64, :, r, c, f, :]
                            dst = uT[64 * f:64 * f + 64, 2 * r + c, 256 + 16 * p:272 + 16 * p].rearrange("p (b i) -> p b i", b=2)
                            ins = dve.tensor_copy(dst, src)
                            if (r, f, c) == (1, 1, 1):
                                freeing(ins, ("soT", p))
                            else:
                                s(ins)
                s(dve.tensor_copy(small[:, 1200:1201], cst[:, 0:1]), dve_done, ("oT", p))

            for p in range(4):
                sample_max(p)
                sample_out(p)
                sample_back(p)
            add_to_h("wo", 1)
            ffn(1)

        @block.gpsimd
        def _(pool):
            s, freeing = stepper(pool, pool_order)
            for slot in range(4):
                s(pool.memset(raw[:, slot, 0:3], 0.0))
            for half in range(2):
                pool.wait_ge(*freed(("rows", half)))
            for b in range(CONV_BLKS):
                if b >= 4:
                    pool.wait_ge(*dve_done.at(("conv", b - 4)))
                q = raw[:, b % 4, 259:347].rearrange("p (b w) -> p b w", b=8)
                s(pool.tensor_copy(q[:, :, 0:3], stT[:, b, 0:24].rearrange("p (b w) -> p b w", b=8)), pool_done, ("rawstate", b))
                pool.wait_ge(*freed(("xbc", b)))
                s(pool.tensor_copy(newT[:, b, 0:3], raw[:, b % 4, 256:259]))
                s(pool.tensor_copy(newT[:, b, 3:27].rearrange("p (b w) -> p b w", b=8), q[:, :, 8:11]), pool_done, ("newrow", b))
            pool.wait_ge(*dve_done.at("scan_area"))
            pool.wait_ge(vec_in.sem, 48)
            for n in range(3 * GROUPS):
                t, g = divmod(n, GROUPS)
                R, x = ROWS[t], n % 2
                pool.wait_ge(*freed(("cum", t)))
                pool.wait_ge(*freed(("tok", g // 2, t)))
                if n >= 2:
                    tp, gp = divmod(n - 2, GROUPS)
                    pool.wait_ge(*full_at(("y", tp, gp)))
                    pool.wait_ge(*full_at(("state", tp, gp) if tp < 2 else ("hupd", 2 * gp + 1, 1)))
                    pool.wait_ge(*dve_done.at(("gated", tp, gp)))
                xg = heads(xs[0:R, t, g * 256:(g + 1) * 256])
                s(pool.tensor_tensor(heads(xdt[0:R, x, :]), xg, spread(dt[0:R, t, 4 * g:4 * g + 4], 64), ALU.mult))
                s(pool.tensor_tensor(heads(xdtt[0:R, x, :]), heads(xdt[0:R, x, :]),
                                     spread(ex[0:R, t, 32 + 4 * g:36 + 4 * g], 64), ALU.mult), pool_done, ("xdt", t, g))
                s(pool.tensor_tensor(heads(dxs[0:R, x, :]), xg, spread(d_bc[0:R, 4 * g:4 * g + 4], 64), ALU.mult),
                  pool_done, ("dxs", t, g))
                if t == 2:
                    if g >= 2:
                        pool.wait_ge(*full_at(("inter", 2, g - 2)))
                    c = ctm[:, g % 2, :, :]
                    diag = bass.AP(c.tensor, c.offset, [list(c.ap[0]), [72, 8], [1, 8]])
                    s(pool.tensor_copy(diag, bcT[:, 8 + g, 256:320].rearrange("p (b w) -> p b w", b=8)), pool_done, ("ctm", g))
                    pool.wait_ge(*freed("ec"))
                    for i in range(2):
                        blk = 2 * g + i
                        for q in range(2):
                            pool.wait_ge(*full_at(("h0T", blk, q)))
                        hh = h0[:, blk % 3, :, :]
                        s(pool.tensor_tensor(hh, hh, spread(ec[:, blk, :], 128), ALU.mult), pool_done, ("h0s", blk))

            tables = {which: I["peer_" + which].rearrange("l e d -> (l e) d") for which in "uv"}

            def gather(l, t, which):
                base = (u_base if which == "u" else v_base)(l, t)
                cols = expert[:, t % 2, :].rearrange("p (n k) -> p n k", k=PSLOTS)
                with pool.Fori(0, peer_rounds(t), 1) as i:
                    for k in range(PSLOTS):
                        pool.wait_ge(slot_free[k].sem, i + (base + 1))
                        pool.tensor_copy(islot[:, k:k + 1], cols[:, bass.ds(i, 1), k]).then_inc(index_copied.sem, 1)
                        pool.wait_ge(index_copied.sem, i * PSLOTS + (base * PSLOTS + k + 1))
                        pool.nop(nofuse=True)
                        pool.indirect_dma_start(rows_buf[:, k, :], None, tables[which],
                                                bass.IndirectOffsetOnAxis(ap=islot[:, k:k + 1], axis=0))\
                            .then_inc(gathered[k].sem, 16)

            def ffn(l):
                for t in range(3):
                    pool.wait_ge(*dve_done.at(("expert", l, t)))
                    gather(l, t, "u")
                    gather(l, t, "v")

            ffn(0)
            ffn(1)
    return counts


INPUTS = ["x_prompt", "x_sample", "state_conv", "state_ssm", "cache_k", "cache_v", "p_prompt", "p_sample",
          "norm_mix", "norm_ffn", "norm_ple", "ssm_w_in", "ssm_conv_w", "ssm_conv_b", "ssm_dt_bias", "ssm_a_log",
          "ssm_d", "ssm_norm", "ssm_w_out", "kv_norm", "w_kv", "k_norm", "w_q", "q_norm", "w_o",
          "peer_w_query", "peer_sub_keys", "peer_u", "peer_v", "ple_w_proj", "ple_w_gate"]
OUTPUTS = [("y_prompt", (1, 256, 1024)), ("y_sample", (8, 8, 1024)), ("prompt_conv", (1, 1, 3, 4096)),
           ("prompt_ssm", (1, 1, 32, 64, 128)), ("prompt_k", (1, 256, 6, 64)), ("prompt_v", (1, 256, 6, 64)),
           ("sample_conv", (1, 8, 3, 4096)), ("sample_ssm", (1, 8, 32, 64, 128)),
           ("sample_k", (8, 8, 6, 64)), ("sample_v", (8, 8, 6, 64))]


def kernel(**inputs):
    import concourse.bacc as bacc
    from concourse.bass_utils import run_bass_kernel_spmd

    arrays = {name: np.ascontiguousarray(inputs[name]) for name in INPUTS}
    arrays["constants"] = shape_constants()
    arrays["masks"] = attention_masks()
    arrays["angles"] = rotary_angles()

    def program(counts):
        nc = bacc.Bacc("TRN2", target_bir_lowering=False, num_devices=1)
        I = {n: nc.dram_tensor(n, a.shape, F32, kind="ExternalInput").ap() for n, a in arrays.items()}
        O = {n: nc.dram_tensor("out_" + n, shape, F32, kind="ExternalOutput").ap() for n, shape in OUTPUTS}
        I["w_in"], I["w_out"] = I["ssm_w_in"][0], I["ssm_w_out"][0]
        return nc, build(nc, I, O, counts)

    counts = program(None)[1]
    nc = program({k: dict(v) for k, v in counts.items()})[0]
    r = run_bass_kernel_spmd(nc, [arrays], core_ids=[0]).results[0]
    return tuple(r["out_" + n] for n, _ in OUTPUTS)
```

```python
import numpy as np
import concourse.bass as bass
import concourse.mybir as mybir
from concourse.alu_op_type import AluOpType as ALU
from contextlib import ExitStack

ACT = mybir.ActivationFunctionType
AX = mybir.AxisListType
F32 = mybir.dt.float32
U32 = mybir.dt.uint32
I32 = mybir.dt.int32

D = 1024
KD = D // 128
NTOK = 320
ROWS = (128, 128, 64)
OFF = (0, 128, 256)
GROUP_TILES = {"P": (0, 1), "S": (2,)}
ALL = (0, 1, 2)
DEC_B, DEC_T, PAST = 8, 8, 2048
D_INNER, CONV_DIM, HEADS, GROUPS, HG, HP, NS = 2048, 4096, 32, 8, 4, 64, 128
XS_BLKS, CONV_BLKS = D_INNER // 128, CONV_DIM // 128
DT_COL = D_INNER + CONV_DIM
PK, PH, TOPK, EXPERTS = 128, 8, 16, 16384
HK = PH * TOPK
PLE = 256
EPS = 1e-6
CONV_W = 4
NB = 8
NW = 4

ARENA = 29696

C_ID, C_TRI, C_STRICT, C_TRIS, C_STRICTS, C_ONES, C_BM, C_ID2, C_IOTA, C_END = 0, 128, 256, 384, 448, 512, 640, 648, 712, 728


def shape_constants():
    c = np.zeros((128, C_END), np.float32)
    k, s = np.arange(128)[:, None], np.arange(128)[None, :]
    c[:, C_ID:C_ID + 128] = k == s
    c[:, C_TRI:C_TRI + 128] = k <= s
    c[:, C_STRICT:C_STRICT + 128] = k > s
    k, s = k[:64], s[:, :64]
    same = k // DEC_T == s // DEC_T
    c[:64, C_TRIS:C_TRIS + 64] = (k <= s) & same
    c[:64, C_STRICTS:C_STRICTS + 64] = (k > s) & same
    c[:, C_ONES:C_ONES + 128] = 1.0
    c[:64, C_BM:C_BM + 8] = k // DEC_T == np.arange(8)[None, :]
    c[:, C_ID2:C_ID2 + 64] = np.arange(128)[:, None] % 64 == np.arange(64)[None, :]
    c[:, C_IOTA:C_IOTA + 16] = np.arange(16)[None, :]
    return c


DILATION = (1, 4, 16)
WINDOW = (128, 512, 2048)
NQH, NKH = 24, 6
SBLK = 13
SCOLS = SBLK * 128 + 48
MASKED = -1.0e30


def attention_masks():
    q = np.arange(128)[:, None]
    parts = []
    for t in range(2):
        k = np.arange(128 * (t + 1))[None, :]
        for d, w in zip(DILATION, WINDOW):
            gap = q + 128 * t - k
            parts.append((gap >= 0) & (gap % d == 0) & (gap <= w))
    row = np.arange(128)[:, None]
    b2, i = row // 64, row % 8
    c = np.arange(512)[None, :]
    parts.append(((c - i) % 4 == 0) & (c >= i))
    residue = (np.arange(1024) // 128)[None, :]
    parts.append(residue == i)
    parts.append(np.arange(128)[None, :] >= i)
    kb, s = (np.arange(16) // 8)[None, :], (np.arange(16) % 8)[None, :]
    for d in DILATION:
        parts.append((kb == b2) & (s <= i) & ((i - s) % d == 0))
    seen = np.concatenate([np.broadcast_to(p, (128, p.shape[1])) for p in parts], axis=1)
    return np.where(seen, 0.0, MASKED).astype(np.float32)


def rotary_angles():
    inv = np.float32(500000.0) ** (-np.arange(0, 16, 2, dtype=np.float32) / np.float32(16))
    pos = np.zeros((3, 128), np.float32)
    pos[0], pos[1] = np.arange(128), np.arange(128) + 128
    pos[2, :64] = PAST + np.arange(64) % DEC_T
    ang = (pos[:, :, None] * inv[None, None, :].astype(np.float32)).astype(np.float32).astype(np.float64)
    return np.stack([np.cos(ang), np.sin(ang)], axis=2).transpose(1, 0, 2, 3).reshape(128, 48).astype(np.float32)


class Signal:

    def __init__(self, sem, counts):
        self.sem, self.n, self.counts = sem, 0, counts

    def mark(self, key=None, by=1):
        self.n += by
        if key is not None:
            self.counts[key] = self.n
        return self.sem, by

    def at(self, key):
        return self.sem, self.counts[key]


class AnyCount(dict):

    def __missing__(self, key):
        return 1


class AnyUser(dict):
    def __missing__(self, key):
        return None


def build(nc, I, O, counts):
    first = counts is None
    counts = {} if first else counts
    ctx = ExitStack()
    with ctx:
        sb = lambda name, shape, dt=F32: ctx.enter_context(nc.sbuf_tensor(name, shape, dt))
        signals = {}

        def signal(name):
            if name not in signals:
                if name not in counts:
                    counts[name] = AnyCount()
                signals[name] = Signal(ctx.enter_context(nc.semaphore(name)), counts[name])
            return signals[name]

        cst = sb("cst", [128, C_END])
        h = sb("h", [128, 3, D])
        u = sb("u", [128, 3, D])
        uT = sb("uT", [128, 16, NTOK])
        wring = sb("wring", [128, NW, 2048])
        gain = sb("gain", [128, 2, D])
        small = sb("small", [128, 1280])
        arena = sb("arena", [128, ARENA])
        banks = ctx.enter_context(nc.psum_tensor("banks", [128, NB, 512], F32))

        ident = cst[:, C_ID:C_ID + 128]
        ones = cst[:, C_ONES:C_ONES + 128]

        def area(base, *shape):
            n = int(np.prod(shape))
            v = arena[:, base:base + n]
            if len(shape) == 2:
                v = v.rearrange("p (a b) -> p a b", a=shape[0])
            if len(shape) == 3:
                v = v.rearrange("p (a b c) -> p a b c", a=shape[0], b=shape[1])
            return v

        bank_full = [signal(f"bank_full{b}") for b in range(NB)]
        bank_free = [signal(f"bank_free{b}") for b in range(NB)]
        jobs = counts.setdefault("jobs", {})
        last_user = counts.setdefault("last_user", AnyUser())
        bank_uses, held, turn = [0] * NB, set(), [0]

        def claim(pe, key, hold=False):
            while turn[0] % NB in held:
                turn[0] += 1
            b = turn[0] % NB
            turn[0] += 1
            if hold:
                held.add(b)
            bank_uses[b] += 1
            jobs[key] = b, bank_uses[b]
            if bank_uses[b] > 1:
                pe.wait_ge(bank_free[b].sem, bank_uses[b] - 1)
            return banks[:, b, :]

        def full(key):
            return bank_full[jobs[key][0]].sem, 1

        def full_at(key):
            b, n = jobs.get(key, (0, 1))
            return bank_full[b].sem, n

        def filled(eng, key):
            eng.wait_ge(*full_at(key))
            return banks[:, jobs.get(key, (0, 1))[0], :]

        def free(key):
            return bank_free[jobs.get(key, (0, 1))[0]].sem, 1

        def freed(key):
            b, n = jobs.get(key, (0, 1))
            return bank_free[b].sem, n

        def advance(steps, n=None):
            for _ in steps if n is None else range(n):
                if n is not None:
                    next(steps, None)

        loads = []
        load_index = {}

        def plan_weight(key, matrix, row0, col0, cols, rows=512):
            load_index[key] = len(loads)
            loads.append((matrix[row0:row0 + rows, col0:col0 + cols].rearrange("(k p) n -> p k n", p=128), rows // 128, cols))

        def plan_project(key, matrix, kchunks, cols):
            for n in range(cols // 512):
                for half in range(kchunks // 4):
                    plan_weight((key, n, half), matrix, half * 512, n * 512, 512)

        plan_project("z", I["w_in"], KD, D_INNER)
        for n in range(CONV_DIM // 512):
            for half in range(2):
                plan_weight(("xbc", n, half), I["w_in"], half * 512, D_INNER + n * 512, 512)
        plan_project("out", I["w_out"], 16, D)

        def plan_ple(l, group):
            for n in range(2):
                plan_weight((f"pproj{l}{group}", n, 0), I["ple_w_proj"][l], 0, n * 512, 512, rows=256)
                for half in range(2):
                    plan_weight((f"pgate{l}{group}", n, half), I["ple_w_gate"][l], half * 512, n * 512, 512)

        plan_project("query0", I["peer_w_query"][0], KD, PH * 256)
        for group in GROUP_TILES:
            plan_ple(0, group)
            for n, cols in ((0, 512), (1, 256)):
                for half in range(2):
                    plan_weight((f"kv{group}", n, half), I["w_kv"], half * 512, n * 512, cols)
            plan_project(f"wq{group}", I["w_q"][0], KD, NQH * 64)
        plan_project("wo", I["w_o"][0], 4, D)
        plan_project("query1", I["peer_w_query"][1], KD, PH * 256)
        for group in GROUP_TILES:
            plan_ple(1, group)
        w_ready = [signal(f"w_ready{s}") for s in range(NW)]

        def slot_view(i):
            _, k, cols = loads[i]
            return wring[:, i % NW, 0:k * cols].rearrange("p (k n) -> p k n", k=k)

        def weight(pe, key, user):
            i = load_index[key]
            last_user[i] = user
            pe.wait_ge(w_ready[i % NW].sem, 16 * (i // NW + 1))
            return slot_view(i)

        load_sent = [0]

        def load_weights(sp, upto):
            while load_sent[0] < upto:
                i = load_sent[0]
                if i >= NW:
                    sp.wait_ge(*full_at(last_user[i - NW]))
                sp.dma_start(slot_view(i), loads[i][0]).then_inc(*w_ready[i % NW].mark(by=16))
                load_sent[0] += 1

        ssq, var, rstd, nwt = (small[:, 8 * i:8 * i + 8] for i in range(4))
        gvar, grstd, gnwt = (small[:, 32 + 24 * i:56 + 24 * i].rearrange("p (t g) -> p t g", t=3) for i in range(3))
        dt, da, dtmp, dtmp2, dtmp3 = (small[:, 104 + 96 * i:200 + 96 * i].rearrange("p (t g) -> p t g", t=3) for i in range(5))
        a_bc = small[:, 584:616]
        dtb_bc = small[:, 616:648]
        d_bc = small[:, 648:680]
        ex = small[:, 680:968].rearrange("p (t g) -> p t g", t=3)
        ec = small[:, 968:1096].rearrange("p (k b) -> p k b", k=16)
        ngT = small[:, 1096:1112]

        z = area(0, 3, D_INNER)
        bcT = area(6144, 16, NTOK)
        xs = area(11264, 3, D_INNER)
        btok = area(17408, 3, 1024)
        T0 = 20480
        raw = area(T0, 4, 347)
        xc = area(T0 + 1392, 8, NTOK)
        stT = area(T0 + 3952, 32, 29)
        newT = area(T0 + 4880, 32, 27)
        newst = uT[:, :, :].rearrange("p k t -> p (k t)")[:, 0:CONV_DIM].rearrange("p (q c) -> p q c", q=8)
        w_dt = area(T0 + 6768, 8, 32)
        cacc = area(T0 + 7024, 3, NTOK)
        sg = area(T0 + 7984, 3, NTOK)
        conv_rows = arena[0:29, 11264:11264 + 4096]
        ng_rows = arena[0:16, 11264 + 4096:11264 + 4224]
        seg_l = area(T0, 2, 4, 128)
        dec = area(T0 + 1024, 2, 512)
        xdt = area(T0 + 2048, 2, 256)
        xdtt = area(T0 + 2560, 2, 256)
        hT = area(T0 + 3072, 8, 256)
        yt = area(T0 + 5120, 2, 256)
        ctm = area(T0 + 5632, 2, 8, 64)
        bm = area(T0 + 6656, 8, 128)
        hfin = area(T0 + 7680, 2, 256)
        dxs = area(T0 + 8192, 2, 256)
        cbm = area(T0 + 8704, 2, 128)
        assert T0 + 8960 <= ARENA
        h0 = u[:, :, :].rearrange("p s (b n) -> p s b n", b=8)
        h0T = wring[:, 2, :].rearrange("p (s b n) -> p s b n", s=2, b=8)
        hnew = wring[:, 3, :].rearrange("p (s b n) -> p s b n", s=2, b=8)

        PSLOTS = 8
        VPE = ((0, 1, 2, 4, 5, 6),) * 2 + ((0, 2, 4, 6),)
        VDVE = ((3, 7),) * 2 + ((1, 3, 5, 7),)
        qT = area(0, 16, NTOK)
        sk_raw = area(5120, 2, 128)
        skT = area(5376, 2, 128)
        sc = area(5632, 2, 16, 128)
        top_v = area(9728, 16, 16)
        top_i = arena[:, 9984:10240].bitcast(U32).rearrange("p (a b) -> p a b", a=16)
        top_f = area(10240, 16, 16)
        cand = area(10496, 8, 256)
        onehot = area(12544, 128, 16)
        best_v = area(14592, 8, 16)
        best_j = arena[:, 14720:14848].bitcast(U32).rearrange("p (a b) -> p a b", a=8)
        best_a, best_b = area(14848, 8, 16), area(14976, 8, 16)
        pick1, pick2 = area(15104, 128), area(15232, 128)
        expert = arena[:, 15360:15616].bitcast(U32).rearrange("p (s n) -> p s n", s=2)
        pgate = area(15616, 2, 128)
        pact = area(15872, 2, 128)
        ptmp = area(16128, 128)
        ptmp2 = area(16256, 128)
        coef = area(16384, 2, 128)
        rows_buf = area(17152, PSLOTS, D)
        islot = arena[:, 25344:25352].bitcast(U32)
        p_rows = area(25352, 3, PLE)
        pT = area(26120, 2, NTOK)
        sgate = area(26760, 3, 512)
        diag = area(28296, len(VPE[0]), 128)
        assert 28296 + 128 * len(VPE[0]) <= ARENA
        stt2 = small[:, 1112:1136]
        BESIDE_U = 9
        HPT = (8, 8, 4)

        qkT = area(0, 15, NTOK)
        qst = area(4800, 3, 8, 64)
        kvs = area(6336, 3, 768)
        qkn_p = area(8640, 2, 30, 64)
        qkn_s = area(23920, 30, 64)
        q_raw_p = area(0, 2, 1536)
        q_raw_s = area(22384, 1536)
        q_raw = (q_raw_p[:, 0, :], q_raw_p[:, 1, :], q_raw_s)
        sq_q = {"P": area(3072, NQH, 64), "S": area(14016, NQH, 64)}
        sq_k = {"P": area(4608, NKH, 64), "S": area(26760, NKH, 64)}
        rotary = {"P": 3072, "S": 14016}
        qkn = (qkn_p[:, 0], qkn_p[:, 1], qkn_s)
        sm = area(12480, 2, 768)
        pt = area(8640, 2, 6, 128)
        osb = area(27144, 512)
        ssm = area(8640, SCOLS)
        pts = area(10352, 16, 128)
        kcT = area(12400, 26, 128)
        cache = arena[:, 15728:15728 + 4 * 3328].rearrange(
            "p (x w b n) -> p x w b n", x=2, w=2, b=26)
        vnew = gain[:, :, :].rearrange("p s d -> p (s d)")[:, 0:1536].rearrange("p (c n) -> p c n", c=4)
        masks = u[:, :, :].rearrange("p t d -> p (t d)")[:, 0:1152 + SCOLS]
        pmask = (masks[:, 0:384], masks[:, 384:1152])
        smask = masks[:, 1152:1152 + SCOLS]
        qvar, qrstd, qtmp = (small[:, 104 + 90 * i:194 + 90 * i].rearrange("p (t h) -> p t h", t=3) for i in range(3))
        so = small[:, 680:808]
        gq, gk = small[:, 808:872], small[:, 872:936]
        negmax, zsum, rz = (small[:, 936 + 4 * i:940 + 4 * i] for i in range(3))
        angles = small[:, 1136:1184].rearrange("p (t c f) -> p t c f", t=3, c=2)

        FFN_GAIN, PLE_GAIN = 1, {(0, "P"): 0, (0, "S"): 1, (1, "P"): 0, (1, "S"): 0}
        KV_GAIN, MIX1_GAIN = {"P": 1, "S": 0}, {"P": 0, "S": 1}

        h_in = [signal(f"h_loaded{t}") for t in range(3)]
        gain_in = [signal(f"gain_loaded{i}") for i in range(2)]
        cst_in = signal("constants_loaded")
        rows_in = signal("conv_rows_loaded")
        dtw_in = signal("dt_weights_loaded")
        vec_in = signal("head_vectors_loaded")
        h0_in = [signal(f"state_loaded{i}") for i in range(3)]
        hnew_out = [signal(f"state_stored{i}") for i in range(2)]
        hfin_out = [signal(f"final_state_stored{i}") for i in range(2)]
        newst_out = signal("conv_rows_stored")
        squares = signal("squares_summed")
        u_ready = signal("u_normalised")
        sk_in = signal("sub_keys_loaded")
        prow_in = signal("ple_rows_loaded")
        gathered = [signal(f"rows_gathered{k}") for k in range(PSLOTS)]
        slot_free = [signal(f"row_slot_free{k}") for k in range(PSLOTS)]
        index_copied = signal("index_copied")
        diag_made = signal("diagonals_made")
        angles_in = signal("angles_loaded")
        masks_in = signal("masks_loaded")
        qk_gain_in = signal("head_gains_loaded")
        cache_in = [[signal(f"cached_{w}_loaded{i}") for i in range(2)] for w in ("keys", "values")]
        vnew_in = signal("new_values_moved")
        stored = signal("outputs_stored")
        act_order, dve_order, pool_order = signal("scalar_step"), signal("vector_step"), signal("pool_step")
        act_done, dve_done, pool_done = signal("scalar_result"), signal("vector_result"), signal("pool_result")

        def stepper(eng, order):
            def s(ins, sig=None, key=None):
                sig = sig or order
                ins.then_inc(*sig.mark(key))
                eng.wait_ge(sig.sem, sig.n)

            def freeing(ins, key):
                ins.then_inc(*free(key))
                eng.wait_ge(*freed(key))
            return s, freeing

        def step_of(t, g):
            return t * GROUPS + g

        def tri_of(t):
            return cst[:, C_TRI:C_TRI + 128] if t < 2 else cst[0:64, C_TRIS:C_TRIS + 64]

        def strict_of(t):
            return cst[:, C_STRICT:C_STRICT + 128] if t < 2 else cst[0:64, C_STRICTS:C_STRICTS + 64]

        def spread(ap, n):
            return ap.unsqueeze(2).to_broadcast([ap.shape[0], ap.shape[1], n])

        def repeat(ap, n):
            return ap.unsqueeze(1).to_broadcast([ap.shape[0], n, ap.shape[1]])

        def heads(ap):
            return ap.rearrange("p (h d) -> p h d", d=64)

        def peer_rounds(t):
            return HPT[t] * TOPK // PSLOTS

        def u_base(l, t):
            return 2 * (l * sum(map(peer_rounds, range(3))) + sum(map(peer_rounds, range(t))))

        def v_base(l, t):
            return u_base(l, t) + peer_rounds(t)

        def diagonals_before(l, t):
            each = [peer_rounds(i) * len(VPE[i]) for i in range(3)]
            return l * sum(each) + sum(each[:t])

        def in_rounds(t, rounds, beside=None, pace=1):
            if beside is None:
                rounds(0, peer_rounds(t))
            else:
                for r in range(peer_rounds(t)):
                    rounds(r, r + 1)
                    advance(beside, pace)

        block = ctx.enter_context(nc.Block())

        @block.tensor
        def _(pe):
            def transposes(key, pieces):
                bank = claim(pe, key)
                for col, src in pieces:
                    r, c = src.shape[0], src.shape[-1]
                    mm = pe.transpose(bank[0:c, col:col + r], src, ident[0:r, 0:r])
                mm.then_inc(*full(key))

            def norm_transposes(key, tiles=ALL):
                for t in tiles:
                    pe.wait_ge(*u_ready.at((key, t)))
                    for half in range(2):
                        transposes(("uT", key, t, half),
                                   [(j * 128, u[0:ROWS[t], t, (4 * half + j) * 128:(4 * half + j + 1) * 128])
                                    for j in range(4)])
                for t in tiles:
                    for half in range(2):
                        pe.wait_ge(*freed(("uT", key, t, half)))

            def project_block(key, n, kchunks, tiles=ALL):
                acc = {t: claim(pe, (key, n, t)) for t in tiles}
                for half in range(kchunks // 4):
                    w = weight(pe, (key, n, half), (key, n, tiles[-1]))
                    for t in tiles:
                        for k in range(4):
                            kk = half * 4 + k
                            mm = pe.matmul(acc[t][0:ROWS[t], 0:w.shape[2]], uT[:, kk, OFF[t]:OFF[t] + ROWS[t]], w[:, k, :],
                                           start=(kk == 0), stop=(kk == kchunks - 1))
                        if kk == kchunks - 1:
                            mm.then_inc(*full((key, n, t)))

            def project(key, nblocks, kchunks):
                for n in range(nblocks):
                    project_block(key, n, kchunks)

            pe.wait_ge(*cst_in.at("cst"))
            norm_transposes("mix0")
            pe.wait_ge(dtw_in.sem, 16)
            for t in range(3):
                acc = claim(pe, ("dt", t))
                for k in range(KD):
                    mm = pe.matmul(acc[0:ROWS[t], 0:32], uT[:, k, OFF[t]:OFF[t] + ROWS[t]], w_dt[:, k, :],
                                   start=(k == 0), stop=(k == KD - 1))
                mm.then_inc(*full(("dt", t)))
            project_block("z", 0, KD)
            pe.wait_ge(rows_in.sem, 64)
            for half in range(2):
                transposes(("rows", half), [(j * 29, conv_rows[:, (16 * half + j) * 128:(16 * half + j + 1) * 128])
                                            for j in range(16)])
            transposes("ng", [(0, ng_rows)])
            for n in range(1, 4):
                project_block("z", n, KD)

            def to_tokens(n):
                for j in range(4):
                    pe.wait_ge(*dve_done.at(("silu", 4 * n + j)))
                src = [xc[:, (4 * n + j) % 8, :] if n < 4 else bcT[:, 4 * n + j - 16, :] for j in range(4)]
                for t in range(3):
                    transposes(("tok", n, t), [(j * 128, src[j][:, OFF[t]:OFF[t] + ROWS[t]]) for j in range(4)])

            for n in range(8):
                w = [weight(pe, ("xbc", n, half), ("xbc", 4 * n + 3)) for half in range(2)]
                for j in range(4):
                    acc = claim(pe, ("xbc", 4 * n + j))
                    for k in range(KD):
                        mm = pe.matmul(acc[:, 0:NTOK], w[k // 4][:, k % 4, j * 128:(j + 1) * 128], uT[:, k, :],
                                       start=(k == 0), stop=(k == KD - 1))
                    mm.then_inc(*full(("xbc", 4 * n + j)))
                if 1 <= n <= 6:
                    to_tokens(n - 1)
            for q in range(8):
                for j in range(4):
                    pe.wait_ge(*pool_done.at(("newrow", 4 * q + j)))
                transposes(("newst", q), [(j * 128, newT[:, 4 * q + j, :]) for j in range(4)])

            def sample_turn(g):
                for i in range(2):
                    blk = 2 * g + i
                    pe.wait_ge(*h0_in[blk % 3].at(blk))
                    for q in range(2):
                        transposes(("h0T", blk, q), [(b * 128, h0[:, blk % 3, 4 * q + b, :]) for b in range(4)])

            def sample_states(g):
                x = step_of(2, g) % 2
                pe.wait_ge(*pool_done.at(("ctm", g)))
                for i in range(2):
                    for q in range(2):
                        pe.wait_ge(*freed(("h0T", 2 * g + i, q)))
                bank = claim(pe, ("inter", 2, g))
                for i in range(2):
                    for b in range(8):
                        mm = pe.matmul(bank[0:64, i * 128:(i + 1) * 128], ctm[:, g % 2, b, :], h0T[:, i, b, :],
                                       start=(b == 0), stop=(b == 7))
                mm.then_inc(*full(("inter", 2, g)))
                pe.wait_ge(*dve_done.at(("bm", g)))
                for i in range(2):
                    for q in range(2):
                        bank = claim(pe, ("hupd", 2 * g + i, q))
                        mm = pe.matmul(bank[:, :], xdtt[0:64, x, i * 128:(i + 1) * 128],
                                       bm[0:64, 4 * q:4 * q + 4, :], start=True, stop=True)
                        mm.then_inc(*full(("hupd", 2 * g + i, q)))

            def scan_front(t, g):
                R, x = ROWS[t], step_of(t, g) % 2
                tok = slice(OFF[t], OFF[t] + R)
                pe.wait_ge(*dve_done.at(("seg", t, g)))
                bank = claim(pe, ("seg", t, g))
                for j in range(4):
                    mm = pe.matmul(bank[0:R, j * R:(j + 1) * R], seg_l[0:R, x, j, 0:R], tri_of(t), start=True, stop=True)
                mm.then_inc(*full(("seg", t, g)))
                bank = claim(pe, ("cb", t, g))
                pe.matmul(bank[0:R, 0:R], bcT[:, g, tok], bcT[:, 8 + g, tok], start=True, stop=True)\
                  .then_inc(*full(("cb", t, g)))

            def final_state(g):
                pe.wait_ge(*freed(("state", 1, g)))
                transposes(("hfin", g), [(i * 128, hT[:, g, i * 128:(i + 1) * 128]) for i in range(2)])

            def scan_back(t, g):
                R, x = ROWS[t], step_of(t, g) % 2
                if t == 1:
                    pe.wait_ge(*freed(("state", 0, g)))
                    bank = claim(pe, ("inter", t, g))
                    pe.matmul(bank[:, 0:256], bcT[:, 8 + g, OFF[t]:OFF[t] + R], hT[:, g, :], start=True, stop=True)\
                      .then_inc(*full(("inter", t, g)))
                pe.wait_ge(*dve_done.at(("m", t, g)))
                pe.wait_ge(*pool_done.at(("xdt", t, g)))
                bank = claim(pe, ("y", t, g))
                for j in range(4):
                    mm = pe.matmul(bank[0:R, j * 64:(j + 1) * 64], dec[0:R, x, j * R:(j + 1) * R],
                                   xdt[0:R, x, j * 64:(j + 1) * 64], start=True, stop=True)
                mm.then_inc(*full(("y", t, g)))
                if t == 2:
                    sample_states(g)
                if t < 2:
                    bank = claim(pe, ("state", t, g))
                    pe.matmul(bank[:, 0:256], btok[:, t, g * 128:(g + 1) * 128], xdtt[:, x, :], start=True, stop=True)\
                      .then_inc(*full(("state", t, g)))
                if GROUPS < step_of(t, g) <= 2 * GROUPS:
                    final_state(step_of(t, g) - 1 - GROUPS)

            def turn_rows(t):
                pe.wait_ge(*dve_done.at(("ynorm", t)))
                for q in range(4):
                    transposes(("yT", t, q), [(j * 128, z[0:ROWS[t], t, (4 * q + j) * 128:(4 * q + j + 1) * 128])
                                              for j in range(4)])

            for q in range(6):
                for t in range(3):
                    pe.wait_ge(*freed(("tok", q, t)))
            pe.wait_ge(*dve_done.at("da"))
            pe.wait_ge(*dve_done.at(("silu", CONV_BLKS - 1)))
            for t in range(3):
                R = ROWS[t]
                bank = claim(pe, ("cum", t))
                pe.matmul(bank[0:R, 0:32], tri_of(t), da[0:R, t, :], start=True, stop=True)
                pe.matmul(bank[0:R, 32:64], strict_of(t), da[0:R, t, :], start=True, stop=True)
                pe.matmul(bank[0:R, 64:96], ones[0:R, 0:R], da[0:R, t, :], start=True, stop=True)\
                  .then_inc(*full(("cum", t)))
            bank = claim(pe, "ec")
            for hd in range(HEADS):
                rows, k = slice(64 * (hd % 2), 64 * (hd % 2) + 64), hd // 2
                mm = pe.matmul(bank[rows, k * 8:(k + 1) * 8], da[0:64, 2, hd:hd + 1].to_broadcast([64, 64]),
                               cst[0:64, C_BM:C_BM + 8], start=True, stop=True)
            mm.then_inc(*full("ec"))
            scan_front(0, 0)
            for n in range(3 * GROUPS):
                if n >= 2 * GROUPS:
                    sample_turn(n - 2 * GROUPS)
                if n + 1 < 3 * GROUPS:
                    scan_front(*divmod(n + 1, GROUPS))
                scan_back(*divmod(n, GROUPS))
                if n % GROUPS == 0 and n > 0:
                    turn_rows(n // GROUPS - 1)
            turn_rows(2)
            for t in range(3):
                for q in range(4):
                    pe.wait_ge(*freed(("yT", t, q)))
            project("out", 2, 16)

            def select(l, t, quads=range(4)):
                for q in quads:
                    if q >= HPT[t] // 2:
                        break
                    bank = claim(pe, ("score", l, t, q))
                    if t < 2:
                        for j in range(4):
                            mm = pe.matmul(bank[:, j * 128:(j + 1) * 128], qT[:, 4 * q + j, OFF[t]:OFF[t] + 128],
                                           skT[:, j % 2, :], start=True, stop=True)
                    else:
                        for hf in range(2):
                            for j in range(4):
                                mm = pe.matmul(bank[64 * hf:64 * hf + 64, j * 128:(j + 1) * 128],
                                               qT[:, 8 * hf + 4 * q + j, 256:320], skT[:, j % 2, :], start=True, stop=True)
                    mm.then_inc(*full(("score", l, t, q)))

            def combine(l, t, beside=None):
                R, base = ROWS[t], v_base(l, t)
                acc = [claim(pe, ("peer", l, t, n), hold=True) for n in range(2)]
                for n in range(2):
                    pe.matmul(acc[n][0:R, :], ident[0:R, 0:R], h[0:R, t, n * 512:(n + 1) * 512], start=True, stop=False)
                made = diagonals_before(l, t)

                def rounds(first, last):
                    with pe.Fori(first, last, 1) as i:
                        for d, k in enumerate(VPE[t]):
                            pe.wait_ge(diag_made.sem, i * len(VPE[t]) + (made + d + 1))
                            pe.wait_ge(gathered[k].sem, i * 16 + (base * 16 + 16))
                            for n in range(2):
                                mm = pe.matmul(acc[n][0:R, :], diag[:, d, 0:R], rows_buf[:, k, n * 512:(n + 1) * 512],
                                               start=False, stop=False, skip_group_check=True)
                            mm.then_inc(slot_free[k].sem, 1)

                in_rounds(t, rounds, beside)
                pe.wait_ge(*dve_done.at(("vsum", l, t)))
                for n in range(2):
                    pe.matmul(acc[n][0:R, :], ident if t < 2 else cst[:, C_ID2:C_ID2 + 64], u[:, t, n * 512:(n + 1) * 512],
                              start=False, stop=True).then_inc(*full(("peer", l, t, n)))
                held.clear()

            def ffn(l):
                pe.wait_ge(*sk_in.at(l))
                transposes(("sk", l), [(c * 128, sk_raw[:, c, :]) for c in range(2)])
                norm_transposes(f"ffn{l}")
                for n in range(4):
                    w = [weight(pe, (f"query{l}", n, half), ("q", l, 4 * n + 3)) for half in range(2)]
                    for j in range(4):
                        acc = claim(pe, ("q", l, 4 * n + j))
                        for k in range(KD):
                            mm = pe.matmul(acc[:, 0:NTOK], w[k // 4][:, k % 4, j * 128:(j + 1) * 128], uT[:, k, :],
                                           start=(k == 0), stop=(k == KD - 1))
                        mm.then_inc(*full(("q", l, 4 * n + j)))
                    if n == 0:
                        pe.wait_ge(*freed(("sk", l)))
                    else:
                        for b in range(4 * n - 4, 4 * n):
                            pe.wait_ge(*freed(("q", l, b)))
                        select(l, 0, [n - 1])
                for b in range(12, 16):
                    pe.wait_ge(*freed(("q", l, b)))
                select(l, 0, [3])
                select(l, 1)
                select(l, 2)
                combine(l, 0)
                combine(l, 1)
                if l == 0:
                    prompt = middle("P")
                    advance(prompt, BESIDE_U)
                    combine(l, 2, prompt)
                    advance(prompt)
                else:
                    prompt = embed(1, "P")
                    advance(prompt, BESIDE_U)
                    combine(l, 2)
                    advance(embed(1, "S"))

            def embed(l, group):
                tiles = GROUP_TILES[group]
                pe.wait_ge(*prow_in.at(l))
                for t in tiles:
                    transposes(("pT", l, t), [(c * 128, p_rows[0:ROWS[t], t, c * 128:(c + 1) * 128]) for c in range(2)])
                norm_transposes(f"ple{l}{group}", tiles)
                for t in tiles:
                    pe.wait_ge(*freed(("pT", l, t)))
                yield
                for n in range(2):
                    w = weight(pe, (f"pproj{l}{group}", n, 0), (f"pproj{l}", n, tiles[-1]))
                    for t in tiles:
                        acc = claim(pe, (f"pproj{l}", n, t))
                        for k in range(2):
                            mm = pe.matmul(acc[0:ROWS[t], :], pT[:, k, OFF[t]:OFF[t] + ROWS[t]], w[:, k, :],
                                           start=(k == 0), stop=(k == 1))
                        mm.then_inc(*full((f"pproj{l}", n, t)))
                    project_block(f"pgate{l}{group}", n, KD, tiles)
                    yield

            def middle(group):
                tiles = GROUP_TILES[group]
                yield from embed(0, group)
                norm_transposes(f"kv{group}", tiles)
                yield
                for n in range(2):
                    project_block(f"kv{group}", n, KD, tiles)
                    yield
                norm_transposes(f"mix1{group}", tiles)
                yield
                for n in range(3):
                    project_block(f"wq{group}", n, KD, tiles)
                    yield
                for _ in range(1 + 2 * len(tiles)):
                    yield
                pe.wait_ge(*dve_done.at(("rope", tiles[-1])))
                for t in tiles:
                    R = ROWS[t]
                    for g in range(4):
                        heads_of = [2 * (4 * g + j) for j in range(4 if g < 3 else 3)]
                        transposes(("qk", t, g), [(j * 128, qkn[t][0:R, hd:hd + 2, :].rearrange("p h d -> p (h d)"))
                                                  for j, hd in enumerate(heads_of)])
                    for g in range(4):
                        pe.wait_ge(*freed(("qk", t, g)))

            ffn(0)

            def prompt_scores(t, hd):
                r, j = divmod(hd, 4)
                rows, K = slice(64 * r, 64 * r + 64), 128 * (t + 1)
                per = 3 if t == 0 else 2
                for c in range(t + 1):
                    bank = claim(pe, ("s", t, hd, c))
                    for g in range(c * per, min(3, (c + 1) * per)):
                        mm = pe.matmul(bank[:, (g - c * per) * K:(g - c * per + 1) * K], qkT[rows, 4 * g + j, OFF[t]:OFF[t] + 128],
                                       qkT[rows, 12 + g, 0:K], start=True, stop=True)
                    mm.then_inc(*full(("s", t, hd, c)))

            def prompt_turn(t, hd):
                x, n = hd % 2, 3 * (t + 1)
                pe.wait_ge(*act_done.at(("p", t, hd)))
                for c in range(t + 1):
                    transposes(("pt", t, hd, c), [((b - 4 * c) * 128, sm[:, x, b * 128:(b + 1) * 128])
                                                  for b in range(4 * c, min(n, 4 * c + 4))])

            def prompt_values(t, hd):
                r, x, n = hd // 4, hd % 2, 3 * (t + 1)
                for c in range(t + 1):
                    pe.wait_ge(*freed(("pt", t, hd, c)))
                bank = claim(pe, ("o", t, hd))
                for b in range(n):
                    g, kb = divmod(b, t + 1)
                    mm = pe.matmul(bank[:, 0:64], pt[:, x, b, :], kvs[:, kb, 384 + (2 * g + r) * 64:448 + (2 * g + r) * 64],
                                   start=(b == 0), stop=(b == n - 1))
                mm.then_inc(*full(("o", t, hd)))

            samples = middle("S")
            for t in range(2):
                for hd in range(10):
                    if hd < 8:
                        prompt_scores(t, hd)
                    if 1 <= hd < 9:
                        prompt_turn(t, hd - 1)
                    if hd >= 2:
                        prompt_values(t, hd - 2)
                    advance(samples, 1)
                pe.wait_ge(*dve_done.at(("osb", t)))
                transposes(("oT", t), [(c * 128, osb[:, c * 128:(c + 1) * 128]) for c in range(4)])
            advance(samples)

            def sample_keys(p):
                pe.wait_ge(*cache_in[0][p % 2].at(p))
                for c in range(7):
                    transposes(("kc", p, c), [((b - 4 * c) * 128, cache[:, p % 2, 0, b, :]) for b in range(4 * c, min(26, 4 * c + 4))])

            def sample_scores(p):
                for c in range(7):
                    pe.wait_ge(*freed(("kc", p, c)))
                for c in range(4):
                    bank = claim(pe, ("ss", p, c))
                    for b2 in range(2):
                        rows, q = slice(64 * b2, 64 * b2 + 64), qst[:, :, 2 * p + b2, :]
                        keys = kcT[:, 13 * b2 + 4 * c:13 * b2 + 4 * c + (4 if c < 3 else 1), :]
                        g = (1, 2, 2, 0)[c]
                        mm = pe.matmul(bank[rows, 0:128 * keys.shape[1]], q[:, g, :], keys, start=True, stop=True)
                        if c == 3:
                            for g in range(3):
                                mm = pe.matmul(bank[rows, 128 + 16 * g:144 + 16 * g], q[:, g, :],
                                               qkT[:, 12 + g, 256 + 16 * p:272 + 16 * p], start=True, stop=True)
                    mm.then_inc(*full(("ss", p, c)))

            def sample_values(p):
                pe.wait_ge(*act_done.at(("sp", p)))
                for c in range(4):
                    pieces = [((b - 4 * c) * 128, ssm[:, b * 128:(b + 1) * 128]) for b in range(4 * c, min(13, 4 * c + 4))]
                    if c == 3:
                        pieces += [((1 + g) * 128, ssm[:, SBLK * 128 + 16 * g:SBLK * 128 + 16 * g + 16]) for g in range(3)]
                    transposes(("spt", p, c), pieces)
                for c in range(4):
                    pe.wait_ge(*freed(("spt", p, c)))
                if p == 0:
                    pe.wait_ge(vnew_in.sem, 64)
                pe.wait_ge(*cache_in[1][p % 2].at(p))
                bank = claim(pe, ("so", p))
                for b2 in range(2):
                    rows = slice(64 * b2, 64 * b2 + 64)
                    for b in range(13):
                        pe.matmul(bank[rows, 0:128], pts[:, b, rows], cache[:, p % 2, 1, 13 * b2 + b, :], start=(b == 0), stop=False)
                    for g in range(3):
                        mm = pe.matmul(bank[rows, 0:128], pts[0:16, 13 + g, rows], vnew[0:16, p, 128 * g:128 * g + 128],
                                       start=False, stop=(g == 2))
                mm.then_inc(*full(("so", p)))

            def sample_turn(p):
                pe.wait_ge(*dve_done.at(("so", p)))
                transposes(("soT", p), [(0, so)])

            sample_keys(0)
            sample_scores(0)
            for p in range(4):
                if p + 1 < 4:
                    sample_keys(p + 1)
                sample_values(p)
                if p + 1 < 4:
                    sample_scores(p + 1)
                sample_turn(p)
            for t in range(2):
                pe.wait_ge(*freed(("oT", t)))
            pe.wait_ge(*dve_done.at(("oT", 3)))
            project("wo", 2, 4)
            ffn(1)

        @block.sync
        def _(sp):
            def load_gain(i, name, row, last=None):
                if last is not None:
                    sp.wait_ge(*u_ready.at(last))
                sp.dma_start(gain[:, i, :], row.to_broadcast([128, D])).then_inc(*gain_in[i].mark(name, 16))

            for t in range(3):
                src = I["x_prompt"][0, OFF[t]:OFF[t] + 128, :] if t < 2 else I["x_sample"].rearrange("b s d -> (b s) d")
                sp.dma_start(h[0:ROWS[t], t, :], src).then_inc(*h_in[t].mark("x", 16))
            load_gain(0, "mix0", I["norm_mix"][0:1, :])
            sp.dma_start(cst[:, :], I["constants"]).then_inc(*cst_in.mark("cst", 16))
            sp.dma_start(w_dt, I["w_in"][:, DT_COL:DT_COL + 32].rearrange("(k p) n -> p k n", p=128)).then_inc(dtw_in.sem, 16)
            load_weights(sp, 2)
            sp.dma_start(conv_rows[0:24, :], I["state_conv"][0].rearrange("b w c -> (b w) c")).then_inc(rows_in.sem, 16)
            sp.dma_start(conv_rows[24:28, :], I["ssm_conv_w"][0]).then_inc(rows_in.sem, 16)
            sp.dma_start(conv_rows[28:29, :], I["ssm_conv_b"]).then_inc(rows_in.sem, 16)
            sp.dma_start(ng_rows, I["ssm_norm"][0].rearrange("(c p) -> c p", p=128)).then_inc(rows_in.sem, 16)
            sp.wait_ge(*dve_done.at("small"))
            sp.dma_start(small[:, 1136:1184], I["angles"]).then_inc(angles_in.sem, 16)
            sp.dma_start(a_bc, I["ssm_a_log"].to_broadcast([128, 32])).then_inc(vec_in.sem, 16)
            sp.dma_start(dtb_bc, I["ssm_dt_bias"].to_broadcast([128, 32])).then_inc(vec_in.sem, 16)
            sp.dma_start(d_bc, I["ssm_d"].to_broadcast([128, 32])).then_inc(vec_in.sem, 16)
            load_weights(sp, load_index[("out", 0, 0)])
            for q in range(8):
                sp.wait_ge(*freed(("newst", q)))
                cols = slice(q * 512, (q + 1) * 512)
                sp.dma_start(O["prompt_conv"][0, 0, :, cols], newst[0:3, q, :]).then_inc(*newst_out.mark(by=16))
                sp.dma_start(O["sample_conv"][0, :, :, cols].rearrange("b w c -> (b w) c"), newst[3:27, q, :])\
                  .then_inc(*newst_out.mark("all", 16))
            load_weights(sp, load_index[("out", 0, 0)] + 2)

            def store_state(blk):
                sp.wait_ge(*dve_done.at(("hnew", blk)))
                sp.dma_start(O["sample_ssm"][0, :, 2 * blk:2 * blk + 2, :, :].rearrange("b h p n -> (h p) b n"),
                             hnew[:, blk % 2, :, :]).then_inc(*hnew_out[blk % 2].mark(blk, 16))

            for t in range(3):
                for half in range(2):
                    sp.wait_ge(*full_at(("uT", "mix0", t, half)))
            for blk in range(16):
                if blk >= 3:
                    sp.wait_ge(*dve_done.at(("hnew", blk - 3)))
                sp.dma_start(h0[:, blk % 3, :, :],
                             I["state_ssm"][0, :, 2 * blk:2 * blk + 2, :, :].rearrange("b h p n -> (h p) b n"))\
                  .then_inc(*h0_in[blk % 3].mark(blk, 16))
                if blk == 2:
                    for g in range(8):
                        sp.wait_ge(*freed(("hfin", g)))
                        sp.dma_start(O["prompt_ssm"][0, 0, 4 * g:4 * g + 4, :, :].rearrange("(i h) p n -> (h p) i n", i=2),
                                     hfin[:, g % 2, :].rearrange("p (i n) -> p i n", i=2)).then_inc(*hfin_out[g % 2].mark(g, 16))
                if blk >= 3:
                    store_state(blk - 3)
            for blk in (13, 14, 15):
                store_state(blk)
            for blk in (14, 15):
                sp.wait_ge(*hnew_out[blk % 2].at(blk))
            load_weights(sp, load_index[("query0", 0, 0)])

            def ffn(l):
                sp.dma_start(sk_raw, I["peer_sub_keys"][l].rearrange("c k d -> k c d")).then_inc(*sk_in.mark(l, 16))
                load_gain(FFN_GAIN, f"ffn{l}", I["norm_ffn"][l:l + 1, :])
                load_gain(PLE_GAIN[l, "P"], f"ple{l}P", I["norm_ple"][l:l + 1, :])
                if l == 1:
                    gain_in[0].counts["ple1S"] = gain_in[0].n
                for t in range(3):
                    src = I["p_prompt"][l, 0, OFF[t]:OFF[t] + 128, :] if t < 2 else I["p_sample"][l].rearrange("b s d -> (b s) d")
                    sp.dma_start(p_rows[0:ROWS[t], t, :], src).then_inc(*prow_in.mark(l, 16))

            def store_heads(t):
                sp.wait_ge(*dve_done.at(("rope", t)))
                for name, src in (("k", qkn[t][:, NQH:, :].rearrange("p h d -> p (h d)")), ("v", kvs[:, t, 384:768])):
                    dst = O["prompt_" + name][0, OFF[t]:OFF[t] + 128] if t < 2 else O["sample_" + name].rearrange("b s h d -> (b s) h d")
                    sp.dma_start(dst.rearrange("t h d -> t (h d)"), src[0:ROWS[t], :]).then_inc(*stored.mark(("heads", t), 16))

            def load_cache(p, w):
                name, landed = ("cache_k", "cache_v")[w], cache_in[w][p % 2]
                for b2 in range(2):
                    rows, dst = I[name][2 * p + b2], cache[:, p % 2, w, 13 * b2:13 * b2 + 13, :]
                    cut = lambda r, g: r[:, :, 2 * g:2 * g + 2, :].rearrange("b m h d -> m b (h d)")
                    sp.dma_start(dst[:, 0:4, :], cut(rows[PAST - 512:, :, :].rearrange("(b m) h d -> b m h d", m=128), 1))\
                      .then_inc(*landed.mark(by=16))
                    sp.dma_start(dst[:, 4:12, :], cut(rows.rearrange("(m b) h d -> b m h d", b=16)[0:8], 2))\
                      .then_inc(*landed.mark(by=16))
                    sp.dma_start(dst[:, 12, :], rows[PAST - 128:, 0:2, :].rearrange("m h d -> m (h d)"))\
                      .then_inc(*landed.mark(p, by=16))

            sp.wait_ge(*freed(("yT", 2, 3)))
            ffn(0)
            kv_norm, mix1, ple0 = I["kv_norm"].rearrange("(a d) -> a d", a=1), I["norm_mix"][1:2, :], I["norm_ple"][0:1, :]
            load_weights(sp, load_index[("query0", 1, 0)])
            load_gain(KV_GAIN["P"], "kvP", kv_norm, ("ffn0", 2))
            sp.dma_start(gq, I["q_norm"].to_broadcast([128, 64])).then_inc(qk_gain_in.sem, 16)
            sp.dma_start(gk, I["k_norm"].rearrange("(a d) -> a d", a=1).to_broadcast([128, 64])).then_inc(qk_gain_in.sem, 16)
            load_weights(sp, load_index[("pproj0P", 1, 0)])
            load_gain(MIX1_GAIN["P"], "mix1P", mix1, ("ple0P", 1))
            load_weights(sp, load_index[("wqP", 0, 0)])
            load_gain(PLE_GAIN[0, "S"], "ple0S", ple0, ("kvP", 1))
            load_weights(sp, load_index[("wqP", 2, 0)])
            load_gain(KV_GAIN["S"], "kvS", kv_norm, ("mix1P", 1))
            for t in range(2):
                for half in range(2):
                    sp.wait_ge(*full_at(("uT", "mix1P", t, half)))
            sp.dma_start(masks[:, 0:1152], I["masks"][:, 0:1152]).then_inc(*masks_in.mark("P", 16))
            load_weights(sp, load_index[("pproj0S", 0, 0)] + 2)
            store_heads(0)
            store_heads(1)
            sp.wait_ge(*dve_done.at(("h", "peer", 0, 2)))
            load_weights(sp, load_index[("pproj0S", 1, 0)])
            load_gain(MIX1_GAIN["S"], "mix1S", mix1, ("ple0S", 2))
            load_weights(sp, load_index[("wqS", 0, 0)])
            load_cache(0, 0)
            load_weights(sp, load_index[("wqS", 2, 0)])
            load_cache(0, 1)
            load_weights(sp, load_index[("wo", 0, 0)])
            store_heads(2)
            sp.wait_ge(*full_at(("uT", "mix1S", 2, 1)))
            sp.wait_ge(*dve_done.at(("osb", 1)))
            sp.wait_ge(*full_at(("oT", 1)))
            sp.dma_start(masks[:, 1152:], I["masks"][:, 1152:]).then_inc(*masks_in.mark("S", 16))
            for p in range(4):
                sp.dma_start(vnew[0:16, p, :], kvs[16 * p:16 * p + 16, 2, 384:768]).then_inc(vnew_in.sem, 16)
            for g in range(4):
                sp.wait_ge(*full_at(("qk", 2, g)))
            sp.wait_ge(stored.sem, 96)
            load_cache(1, 0)
            load_cache(1, 1)
            for p in (2, 3):
                sp.wait_ge(*full_at(("kc", p - 2, 6)))
                load_cache(p, 0)
                sp.wait_ge(*full_at(("so", p - 2)))
                load_cache(p, 1)
            load_weights(sp, load_index[("query1", 0, 0)])
            sp.wait_ge(*full_at(("wo", 0, 0)))
            ffn(1)
            load_weights(sp, len(loads))
            for t in range(3):
                sp.wait_ge(*dve_done.at(("ple", 1, 1, t)))
                dst = O["y_prompt"][0, OFF[t]:OFF[t] + 128, :] if t < 2 else O["y_sample"].rearrange("b s d -> (b s) d")
                sp.dma_start(dst, h[0:ROWS[t], t, :]).then_inc(stored.sem, 16)
            sp.wait_ge(stored.sem, 144)
            sp.wait_ge(*newst_out.at("all"))
            for g in (6, 7):
                sp.wait_ge(*hfin_out[g % 2].at(g))

        @block.scalar
        def _(act):
            s, freeing = stepper(act, act_order)

            def norm(key, ready, tiles=ALL):
                act.wait_ge(*dve_done.at("small"))
                for t in tiles:
                    act.wait_ge(*ready(t))
                    s(act.activation(u[0:ROWS[t], t, :], h[0:ROWS[t], t, :], ACT.Square,
                                     accum_out=ssq[0:ROWS[t], t:t + 1]), squares, (key, t))
                for t in tiles:
                    for half in range(2):
                        bank = filled(act, ("uT", key, t, half))
                        freeing(act.activation(uT[:, 4 * half:4 * half + 4, OFF[t]:OFF[t] + ROWS[t]],
                                               bank.rearrange("p (j r) -> p j r", j=4)[:, :, 0:ROWS[t]], ACT.Copy),
                                ("uT", key, t, half))

            norm("mix0", lambda t: h_in[t].at("x"))
            act.wait_ge(vec_in.sem, 48)
            s(act.activation(a_bc, a_bc, ACT.Exp), act_done, "a")
            act.wait_ge(*dve_done.at("dt_abs"))
            s(act.activation(dtmp, dtmp, ACT.Exp, scale=-1.0))
            s(act.activation(dtmp2, dtmp, ACT.Ln, bias=1.0), act_done, "dt_ln")
            for n in range(4):
                for t in range(3):
                    bank = filled(act, ("z", n, t))
                    s(act.activation(z[0:ROWS[t], t, n * 512:(n + 1) * 512], bank[0:ROWS[t], :], ACT.Tanh, scale=0.5),
                      act_done, ("ztanh", n, t))
                if n == 0:
                    for half in range(2):
                        bank = filled(act, ("rows", half))
                        freeing(act.activation(stT[:, 16 * half:16 * half + 16, :],
                                               bank[:, 0:464].rearrange("p (j r) -> p j r", j=16), ACT.Copy), ("rows", half))
                    bank = filled(act, "ng")
                    freeing(act.activation(ngT, bank[:, 0:16], ACT.Copy), "ng")

            def conv_tanh(b):
                act.wait_ge(*dve_done.at(("conv", b)))
                s(act.activation(sg[:, b % 3, :], cacc[:, b % 3, :], ACT.Tanh, scale=0.5), act_done, ("ctanh", b))

            def take_tokens(n):
                for t in range(3):
                    bank = filled(act, ("tok", n, t))
                    dst = xs[0:ROWS[t], t, n * 512:(n + 1) * 512] if n < 4 else btok[0:ROWS[t], t, (n - 4) * 512:(n - 3) * 512]
                    freeing(act.activation(dst, bank[0:ROWS[t], :], ACT.Copy), ("tok", n, t))

            for b in range(CONV_BLKS):
                bank = filled(act, ("xbc", b))
                act.wait_ge(*pool_done.at(("rawstate", b)))
                s(act.activation(raw[:, b % 4, 3:259], bank[:, 0:256], ACT.Copy))
                freeing(act.activation(raw[:, b % 4, 259:347].rearrange("p (b w) -> p b w", b=8)[:, :, 3:11],
                                       bank[:, 256:320].rearrange("p (b w) -> p b w", b=8), ACT.Copy), ("xbc", b))
                if b >= 1:
                    conv_tanh(b - 1)
                if 7 <= b <= 27 and b % 4 == 3:
                    take_tokens(b // 4 - 1)
            conv_tanh(CONV_BLKS - 1)
            for q in range(8):
                bank = filled(act, ("newst", q))
                freeing(act.activation(newst[0:27, q, :], bank[0:27, :], ACT.Copy), ("newst", q))

            for t in range(3):
                R = ROWS[t]
                bank = filled(act, ("cum", t))
                freeing(act.activation(ex[0:R, t, :], bank[0:R, 0:96], ACT.Exp), ("cum", t))
            bank = filled(act, "ec")
            freeing(act.activation(ec, bank[:, 0:128].rearrange("p (k b) -> p k b", k=16), ACT.Exp), "ec")

            def decay_exp(n):
                (t, g), x = divmod(n, GROUPS), n % 2
                R = ROWS[t]
                if n >= 2:
                    act.wait_ge(*full_at(("y", (n - 2) // 8, (n - 2) % 8)))
                bank = filled(act, ("seg", t, g))
                freeing(act.activation(dec[0:R, x, 0:4 * R], bank[0:R, 0:4 * R], ACT.Exp), ("seg", t, g))

            decay_exp(0)
            for n in range(3 * GROUPS):
                (t, g), x = divmod(n, GROUPS), n % 2
                R = ROWS[t]
                if t == 2:
                    for i in range(2):
                        for q in range(2):
                            bank = filled(act, ("h0T", 2 * g + i, q))
                            if g >= 1:
                                act.wait_ge(*full_at(("inter", 2, g - 1)))
                            freeing(act.activation(h0T[:, i, 4 * q:4 * q + 4, :],
                                                   bank.rearrange("p (b n) -> p b n", b=4), ACT.Copy),
                                    ("h0T", 2 * g + i, q))
                if n + 1 < 3 * GROUPS:
                    decay_exp(n + 1)
                if GROUPS < n <= 2 * GROUPS:
                    gf = n - 1 - GROUPS
                    bank = filled(act, ("hfin", gf))
                    if gf >= 2:
                        act.wait_ge(*hfin_out[gf % 2].at(gf - 2))
                    freeing(act.activation(hfin[:, gf % 2, :], bank[:, 0:256], ACT.Copy), ("hfin", gf))
                act.wait_ge(*dve_done.at(("gated", t, g)))
                s(act.activation(yt[0:R, x, :], z[0:R, t, g * 256:(g + 1) * 256], ACT.Square,
                                 accum_out=gvar[0:R, t, g:g + 1]), act_done, ("gsq", t, g))

            def take_scores(l, t, quads=range(4)):
                for q in quads:
                    if q >= HPT[t] // 2:
                        break
                    bank = filled(act, ("score", l, t, q))
                    if t == 2 and q == 0:
                        act.wait_ge(*dve_done.at(("gate_in", l, 0, 3)))
                    freeing(act.activation(sc[:, t % 2, 4 * q:4 * q + 4, :], bank.rearrange("p (j r) -> p j r", j=4), ACT.Copy),
                            ("score", l, t, q))

            def gate_exp(l, t):
                x, n = t % 2, HPT[t] * TOPK
                act.wait_ge(*dve_done.at(("gate_in", l, t, HPT[t] // 2 - 1)))
                s(act.activation(pgate[:, x, 0:n], pgate[:, x, 0:n], ACT.Exp), act_done, ("gate_exp", l, t))

            def coefficients(l, t, beside=None):
                x, n = t % 2, HPT[t] * TOPK
                act.wait_ge(*dve_done.at(("gelu_in", l, t)))
                s(act.activation(ptmp[:, 0:n], ptmp[:, 0:n], ACT.Tanh, scale=0.7978845608028654), act_done, ("gelu_tanh", l, t))
                act.wait_ge(*dve_done.at(("coef", l, t)))
                R, base = ROWS[t], v_base(l, t)
                cols = coef[:, x, :].rearrange("p (n k) -> p n k", k=PSLOTS)
                unit = ident if t < 2 else cst[:, C_ID2:C_ID2 + 64]

                def rounds(first, last):
                    with act.Fori(first, last, 1) as i:
                        for d, k in enumerate(VPE[t]):
                            act.wait_ge(slot_free[k].sem, i + (base + 1))
                            act.activation(diag[:, d, 0:R], unit, ACT.Copy, scale=cols[:, bass.ds(i, 1), k])\
                               .then_inc(diag_made.sem, 1)

                in_rounds(t, rounds, beside)

            def ffn(l):
                bank = filled(act, ("sk", l))
                freeing(act.activation(skT, bank[:, 0:256].rearrange("p (c k) -> p c k", c=2), ACT.Copy), ("sk", l))
                norm(f"ffn{l}", lambda t: dve_done.at(("h", "mix", l, t)))
                for n in range(5):
                    for b in range(4 * n, 4 * n + 4 if n < 4 else 16):
                        bank = filled(act, ("q", l, b))
                        freeing(act.activation(qT[:, b, :], bank[:, 0:NTOK], ACT.Copy), ("q", l, b))
                    if n >= 1:
                        take_scores(l, 0, [n - 1])
                take_scores(l, 1)
                gate_exp(l, 0)
                take_scores(l, 2)
                coefficients(l, 0)
                gate_exp(l, 1)
                coefficients(l, 1)
                gate_exp(l, 2)
                prompt = middle("P") if l == 0 else embed(1, "P")
                advance(prompt, BESIDE_U)
                coefficients(l, 2, prompt)
                advance(prompt)
                if l == 1:
                    advance(embed(1, "S"))

            def embed(l, group):
                tiles = GROUP_TILES[group]
                for t in tiles:
                    bank = filled(act, ("pT", l, t))
                    freeing(act.activation(pT[:, :, OFF[t]:OFF[t] + ROWS[t]],
                                           bank[:, 0:256].rearrange("p (c r) -> p c r", c=2)[:, :, 0:ROWS[t]], ACT.Copy), ("pT", l, t))
                norm(f"ple{l}{group}", lambda t: dve_done.at(("h", "peer", l, t)), tiles)
                yield
                for n in range(2):
                    for t in tiles:
                        bank = filled(act, (f"pgate{l}{group}", n, t))
                        if n == 1:
                            act.wait_ge(*dve_done.at(("ple", l, 0, t)))
                        freeing(act.activation(sgate[0:ROWS[t], t, :], bank[0:ROWS[t], :], ACT.Tanh, scale=0.5),
                                (f"pgate{l}{group}", n, t))
                    yield

            def middle(group):
                tiles = GROUP_TILES[group]
                yield from embed(0, group)
                norm(f"kv{group}", lambda t: dve_done.at(("ple", 0, 1, t)), tiles)
                yield
                for n, m in ((0, 512), (1, 256)):
                    for t in tiles:
                        bank = filled(act, (f"kv{group}", n, t))
                        freeing(act.activation(kvs[0:ROWS[t], t, n * 512:n * 512 + m], bank[0:ROWS[t], 0:m], ACT.Copy),
                                (f"kv{group}", n, t))
                    yield
                norm(f"mix1{group}", lambda t: dve_done.at(("ple", 0, 1, t)), tiles)
                yield
                for n in range(3):
                    for t in tiles:
                        bank = filled(act, (f"wq{group}", n, t))
                        freeing(act.activation(q_raw[t][0:ROWS[t], n * 512:(n + 1) * 512], bank[0:ROWS[t], :], ACT.Copy),
                                (f"wq{group}", n, t))
                    yield
                for t in tiles:
                    R = ROWS[t]
                    if t == 1:
                        act.wait_ge(*dve_done.at(("qsum", 0)))
                    s(act.activation(sq_q[group][0:R].rearrange("p h d -> p (h d)"), q_raw[t][0:R, :], ACT.Square))
                    s(act.activation(sq_k[group][0:R].rearrange("p h d -> p (h d)"), kvs[0:R, t, 0:384], ACT.Square),
                      act_done, ("qsq", t))
                for _ in range(1 + 2 * len(tiles)):
                    yield
                for t in tiles:
                    for g in range(4):
                        bank = filled(act, ("qk", t, g)).rearrange("p (j r) -> p j r", j=4)
                        if t < 2 or g == 3:
                            n = 4 if g < 3 else 3
                            freeing(act.activation(qkT[:, 4 * g:4 * g + n, OFF[t]:OFF[t] + ROWS[t]], bank[:, 0:n, 0:ROWS[t]], ACT.Copy),
                                    ("qk", t, g))
                        else:
                            act.wait_ge(*dve_done.at("qst_zero"))
                            for r in range(2):
                                rows = slice(64 * r, 64 * r + 64)
                                dst = qst[rows, g, :, 32 * r:32 * r + 32].rearrange("p b (j i) -> p b j i", j=4)
                                src = bank[rows, :, 0:64].rearrange("p j (b i) -> p b j i", i=8)
                                for j in range(4):
                                    ins = act.activation(dst[:, :, j, :], src[:, :, j, :], ACT.Copy)
                                    if r == 1 and j == 3:
                                        freeing(ins, ("qk", t, g))
                                    else:
                                        s(ins)

            ffn(0)

            def prompt_exp(t, hd):
                x, n = hd % 2, 384 * (t + 1)
                act.wait_ge(*dve_done.at(("max", t, hd)))
                s(act.activation(sm[:, x, 0:n], sm[:, x, 0:n], ACT.Exp, bias=negmax[:, x:x + 1], accum_out=zsum[:, hd % 4:hd % 4 + 1]),
                  act_done, ("p", t, hd))

            def prompt_turn(t, hd):
                x, n = hd % 2, 3 * (t + 1)
                if hd >= 2:
                    act.wait_ge(*full_at(("o", t, hd - 2)))
                for c in range(t + 1):
                    bank = filled(act, ("pt", t, hd, c))
                    m = min(n, 4 * c + 4) - 4 * c
                    freeing(act.activation(pt[:, x, 4 * c:4 * c + m, :], bank.rearrange("p (b r) -> p b r", b=4)[:, 0:m, :], ACT.Copy),
                            ("pt", t, hd, c))

            samples = middle("S")
            act.wait_ge(*stored.at(("heads", 1)))
            for t in range(2):
                for hd in range(10):
                    if 1 <= hd < 9:
                        prompt_exp(t, hd - 1)
                        prompt_turn(t, hd - 1)
                    advance(samples, 1)
                bank = filled(act, ("oT", t))
                freeing(act.activation(uT[:, 0:4, OFF[t]:OFF[t] + 128], bank.rearrange("p (c r) -> p c r", c=4), ACT.Copy), ("oT", t))

            advance(samples)

            def sample_keys(p):
                for c in range(7):
                    bank = filled(act, ("kc", p, c))
                    n = min(26, 4 * c + 4) - 4 * c
                    if p >= 1:
                        act.wait_ge(*full_at(("ss", p - 1, 3)))
                    freeing(act.activation(kcT[:, 4 * c:4 * c + n, :], bank.rearrange("p (b r) -> p b r", b=4)[:, 0:n, :], ACT.Copy),
                            ("kc", p, c))

            def sample_exp(p):
                act.wait_ge(*dve_done.at(("smax", p)))
                s(act.activation(ssm, ssm, ACT.Exp, bias=negmax[:, 0:1], accum_out=zsum[:, p % 4:p % 4 + 1]), act_done, ("sp", p))

            def sample_turn(p):
                for c in range(4):
                    bank = filled(act, ("spt", p, c)).rearrange("p (b r) -> p b r", b=4)
                    if p >= 1:
                        act.wait_ge(*full_at(("so", p - 1)))
                    if c < 3:
                        freeing(act.activation(pts[:, 4 * c:4 * c + 4, :], bank, ACT.Copy), ("spt", p, c))
                    else:
                        s(act.activation(pts[:, 12, :], bank[:, 0, :], ACT.Copy))
                        freeing(act.activation(pts[0:16, 13:16, :], bank[0:16, 1:4, :], ACT.Copy), ("spt", p, c))

            sample_keys(0)
            for p in range(4):
                if p + 1 < 4:
                    sample_keys(p + 1)
                sample_exp(p)
                sample_turn(p)
            ffn(1)

        @block.vector
        def _(dve):
            s, freeing = stepper(dve, dve_order)

            def tell(key):
                s(dve.tensor_copy(small[:, 1200:1201], cst[:, 0:1]), dve_done, key)

            def rsqrt(r, v, tmp):
                s(dve.tensor_scalar(tmp.bitcast(U32), v.bitcast(U32), 1, None, ALU.logical_shift_right))
                s(dve.tensor_scalar(r.bitcast(I32), tmp.bitcast(I32), -1.0, float(0x5F3759DF), ALU.mult, ALU.add))
                for _ in range(4):
                    s(dve.tensor_tensor(tmp, r, r, ALU.mult))
                    s(dve.tensor_tensor(tmp, tmp, v, ALU.mult))
                    s(dve.tensor_scalar(tmp, tmp, -0.5, 1.5, ALU.mult, ALU.add))
                    s(dve.tensor_tensor(r, r, tmp, ALU.mult))

            def norm(key, i, tiles=ALL):
                c = slice(tiles[0], tiles[-1] + 1)
                dve.wait_ge(*squares.at((key, tiles[-1])))
                s(dve.tensor_scalar(var[:, c], ssq[:, c], 1.0 / D, EPS, ALU.mult, ALU.add))
                rsqrt(rstd[:, c], var[:, c], nwt[:, c])
                dve.wait_ge(*gain_in[i].at(key))
                for t in tiles:
                    R = ROWS[t]
                    s(dve.scalar_tensor_tensor(u[0:R, t, :], h[0:R, t, :], rstd[0:R, t:t + 1], gain[0:R, i, :],
                                               ALU.mult, ALU.mult), u_ready, (key, t))

            s(dve.memset(small[:, :], 0.0), dve_done, "small")
            norm("mix0", 0)
            dve.wait_ge(vec_in.sem, 48)
            for t in range(3):
                bank = filled(dve, ("dt", t))
                freeing(dve.tensor_tensor(dt[0:ROWS[t], t, :], bank[0:ROWS[t], 0:32], dtb_bc[0:ROWS[t], :], ALU.add), ("dt", t))
            s(dve.scalar_tensor_tensor(dtmp, dt, -1.0, dt, ALU.mult, ALU.max), dve_done, "dt_abs")
            dve.wait_ge(*act_done.at("dt_ln"))
            s(dve.tensor_scalar(dtmp3, dtmp, 1.0, -1.0, ALU.add, ALU.add))
            s(dve.tensor_scalar(da, dtmp3, 0.0, None, ALU.is_equal))
            s(dve.tensor_tensor(dtmp3, dtmp3, da, ALU.add))
            s(dve.tensor_tensor(dtmp2, dtmp2, da, ALU.add))
            s(dve.reciprocal(dtmp3, dtmp3))
            s(dve.tensor_tensor(dtmp2, dtmp2, dtmp3, ALU.mult))
            s(dve.tensor_tensor(dtmp2, dtmp2, dtmp, ALU.mult))
            s(dve.scalar_tensor_tensor(dt, dt, 0.0, dtmp2, ALU.max, ALU.add))
            s(dve.scalar_tensor_tensor(da, dt, -1.0, repeat(a_bc, 3), ALU.mult, ALU.mult), dve_done, "da")
            for n in range(4):
                for t in range(3):
                    zz = z[0:ROWS[t], t, n * 512:(n + 1) * 512]
                    dve.wait_ge(*act_done.at(("ztanh", n, t)))
                    s(dve.tensor_scalar(zz, zz, 0.5, 0.5, ALU.mult, ALU.add))
                    bank = filled(dve, ("z", n, t))
                    freeing(dve.tensor_tensor(zz, zz, bank[0:ROWS[t], :], ALU.mult), ("z", n, t))

            def conv(b):
                dve.wait_ge(*freed(("xbc", b)))
                if b >= 3:
                    dve.wait_ge(*act_done.at(("ctanh", b - 3)))
                p = raw[:, b % 4, 0:259]
                q = raw[:, b % 4, 259:347].rearrange("p (b w) -> p b w", b=8)
                outs = cacc[:, b % 3, 0:256], cacc[:, b % 3, 256:320].rearrange("p (b w) -> p b w", b=8)
                tap = lambda w: stT[:, b, 24 + w:25 + w]
                s(dve.tensor_scalar(outs[0], p[:, 0:256], tap(0), tap(4), ALU.mult, ALU.add))
                s(dve.tensor_scalar(outs[1], q[:, :, 0:8], tap(0), tap(4), ALU.mult, ALU.add))
                for w in range(1, CONV_W):
                    s(dve.scalar_tensor_tensor(outs[0], p[:, w:w + 256], tap(w), outs[0], ALU.mult, ALU.add))
                    s(dve.scalar_tensor_tensor(outs[1], q[:, :, w:w + 8], tap(w), outs[1], ALU.mult, ALU.add),
                      *((dve_done, ("conv", b)) if w == CONV_W - 1 else ()))

            def silu(b):
                dve.wait_ge(*act_done.at(("ctanh", b)))
                e = sg[:, b % 3, :]
                s(dve.tensor_scalar(e, e, 0.5, 0.5, ALU.mult, ALU.add))
                if 8 <= b < 16:
                    for t in range(3):
                        dve.wait_ge(*full_at(("tok", b // 4 - 2, t)))
                dst = xc[:, b % 8, :] if b < 16 else bcT[:, b - 16, :]
                s(dve.tensor_tensor(dst, e, cacc[:, b % 3, :], ALU.mult), dve_done, ("silu", b))

            for b in range(CONV_BLKS):
                conv(b)
                if b >= 1:
                    silu(b - 1)
            silu(CONV_BLKS - 1)

            def decays(n):
                t, g = divmod(n, GROUPS)
                R, x = ROWS[t], n % 2
                if n >= 2:
                    dve.wait_ge(*full_at(("seg", (n - 2) // 8, (n - 2) % 8)))
                s(dve.tensor_tensor(seg_l[0:R, x, :, 0:R], repeat(strict_of(t), 4), spread(da[0:R, t, 4 * g:4 * g + 4], R),
                                    ALU.mult), dve_done, ("seg", t, g))

            for q in range(8):
                dve.wait_ge(*full_at(("newst", q)))
            s(dve.memset(ctm[:, :, :, :], 0.0), dve_done, "scan_area")

            def mix(n):
                (t, g), x = divmod(n, GROUPS), n % 2
                R = ROWS[t]
                bank = filled(dve, ("cb", t, g))
                freeing(dve.tensor_tensor(cbm[0:R, x, 0:R], bank[0:R, 0:R], tri_of(t), ALU.mult), ("cb", t, g))
                dve.wait_ge(*freed(("seg", t, g)))
                d = dec[0:R, x, 0:4 * R].rearrange("p (j r) -> p j r", j=4)
                s(dve.tensor_tensor(d, d, repeat(cbm[0:R, x, 0:R], 4), ALU.mult), dve_done, ("m", t, g))

            def scale_rows(t):
                R = ROWS[t]
                dve.wait_ge(*act_done.at(("gsq", t, GROUPS - 1)))
                s(dve.tensor_scalar(gvar[0:R, t, :], gvar[0:R, t, :], 1.0 / 256, EPS, ALU.mult, ALU.add))
                rsqrt(grstd[0:R, t, :], gvar[0:R, t, :], gnwt[0:R, t, :])
                zg = z[0:R, t, :].rearrange("p (g d) -> p g d", g=GROUPS)
                s(dve.tensor_tensor(zg, zg, spread(grstd[0:R, t, :], 256), ALU.mult), dve_done, ("ynorm", t))

            def turn_rows(t):
                R = ROWS[t]
                dve.wait_ge(*newst_out.at("all"))
                for q in range(4):
                    bank = filled(dve, ("yT", t, q))
                    freeing(dve.tensor_tensor(uT[:, 4 * q:4 * q + 4, OFF[t]:OFF[t] + R],
                                              bank.rearrange("p (j r) -> p j r", j=4)[:, :, 0:R],
                                              spread(ngT[:, 4 * q:4 * q + 4], R), ALU.mult), ("yT", t, q))

            decays(0)
            decays(1)
            mix(0)
            for n in range(3 * GROUPS):
                t, g = divmod(n, GROUPS)
                R, x = ROWS[t], n % 2
                if n + 2 < 3 * GROUPS:
                    decays(n + 2)
                if n + 1 < 3 * GROUPS:
                    mix(n + 1)
                if t == 2:
                    if g >= 1:
                        dve.wait_ge(*full_at(("hupd", 2 * g - 1, 1)))
                    s(dve.tensor_tensor(bm[0:64, :, :], repeat(btok[0:64, 2, g * 128:(g + 1) * 128], 8),
                                        spread(cst[0:64, C_BM:C_BM + 8], 128), ALU.mult), dve_done, ("bm", g))
                    for i in range(2):
                        blk = 2 * g + i
                        dve.wait_ge(*pool_done.at(("h0s", blk)))
                        if blk >= 2:
                            dve.wait_ge(*hnew_out[blk % 2].at(blk - 2))
                        for q in range(2):
                            bank = filled(dve, ("hupd", blk, q))
                            freeing(dve.tensor_tensor(hnew[:, i, 4 * q:4 * q + 4, :], h0[:, blk % 3, 4 * q:4 * q + 4, :],
                                                      bank.rearrange("p (b n) -> p b n", b=4), ALU.add), ("hupd", blk, q))
                        tell(("hnew", blk))
                y = yt[0:R, x, :]
                if n >= 2:
                    dve.wait_ge(*act_done.at(("gsq", (n - 2) // 8, (n - 2) % 8)))
                dve.wait_ge(*pool_done.at(("dxs", t, g)))
                if t == 0:
                    bank = filled(dve, ("y", t, g))
                    freeing(dve.tensor_tensor(y, bank[0:R, 0:256], dxs[0:R, x, :], ALU.add), ("y", t, g))
                else:
                    bank = filled(dve, ("inter", t, g))
                    freeing(dve.tensor_tensor(heads(y), heads(bank[0:R, 0:256]), spread(ex[0:R, t, 4 * g:4 * g + 4], 64),
                                              ALU.mult), ("inter", t, g))
                    s(dve.tensor_tensor(y, y, dxs[0:R, x, :], ALU.add))
                    bank = filled(dve, ("y", t, g))
                    freeing(dve.tensor_tensor(y, y, bank[0:R, 0:256], ALU.add), ("y", t, g))
                zz = z[0:R, t, g * 256:(g + 1) * 256]
                s(dve.tensor_tensor(zz, zz, y, ALU.mult), dve_done, ("gated", t, g))
                if t == 0:
                    bank = filled(dve, ("state", t, g))
                    freeing(dve.tensor_copy(hT[:, g, :], bank[:, 0:256]), ("state", t, g))
                if t == 1:
                    s(dve.tensor_tensor(heads(hT[:, g, :]), heads(hT[:, g, :]), spread(ex[:, t, 64 + 4 * g:68 + 4 * g], 64), ALU.mult))
                    bank = filled(dve, ("state", t, g))
                    freeing(dve.tensor_tensor(hT[:, g, :], hT[:, g, :], bank[:, 0:256], ALU.add), ("state", t, g))
                if g == GROUPS - 1:
                    scale_rows(t)
                if g == 0 and t > 0:
                    turn_rows(t - 1)
            turn_rows(2)

            def add_to_h(key, l):
                for n in range(2):
                    for t in range(3):
                        hh = h[0:ROWS[t], t, n * 512:(n + 1) * 512]
                        bank = filled(dve, (key, n, t))
                        freeing(dve.tensor_tensor(hh, hh, bank[0:ROWS[t], :], ALU.add), (key, n, t))
                        if n == 1:
                            tell(("h", "mix", l, t))

            def top16(*jobs):
                ends = [0] * len(jobs)

                def step(j, ins):
                    ins.then_inc(*dve_order.mark())
                    ends[j] = dve_order.n

                for half in range(2):
                    o = slice(8 * half, 8 * half + 8)
                    for j, (values, out_v, _) in enumerate(jobs):
                        if half:
                            dve.wait_ge(dve_order.sem, ends[j])
                        step(j, dve.max(out_v[:, o], values))
                    for j, (values, out_v, out_i) in enumerate(jobs):
                        dve.wait_ge(dve_order.sem, ends[j])
                        step(j, dve.max_index(out_i[:, o], out_v[:, o], values))
                    if half == 0:
                        for j, (values, out_v, _) in enumerate(jobs):
                            dve.wait_ge(dve_order.sem, ends[j])
                            step(j, dve.match_replace(values, out_v[:, o], values, -3.0e38))
                dve.wait_ge(dve_order.sem, dve_order.n)

            def pick_quad(l, t, q):
                x, hs, hcs, n = t % 2, slice(2 * q, 2 * q + 2), slice(4 * q, 4 * q + 4), 2 * TOPK
                ks = slice(n * q, n * q + n)
                dve.wait_ge(*freed(("score", l, t, q)))
                for hc in range(4 * q, 4 * q + 4, 2):
                    top16(*((sc[:, x, i, :], top_v[:, i, :], top_i[:, i, :]) for i in (hc, hc + 1)))
                    yield
                pair = top_v[:, hcs, :].rearrange("p (h c) k -> p h c k", c=2)
                grid = cand[:, hs, :].rearrange("p h (a b) -> p h a b", a=TOPK)
                s(dve.tensor_tensor(grid, pair[:, :, 0, :].unsqueeze(3).to_broadcast([128, 2, TOPK, TOPK]),
                                    pair[:, :, 1, :].unsqueeze(2).to_broadcast([128, 2, TOPK, TOPK]), ALU.add))
                top16(*((cand[:, hd, :], best_v[:, hd, :], best_j[:, hd, :]) for hd in (2 * q, 2 * q + 1)))
                yield
                s(dve.tensor_copy(top_f[:, hcs, :], top_i[:, hcs, :]))
                for shift, dst in ((True, best_a), (False, best_b)):
                    j32 = ptmp.bitcast(U32)[:, 0:n].rearrange("p (h k) -> p h k", h=2)
                    s(dve.tensor_scalar(j32, best_j[:, hs, :], 4 if shift else 15, None,
                                        ALU.logical_shift_right if shift else ALU.bitwise_and))
                    s(dve.tensor_copy(dst[:, hs, :], j32))
                yield
                keys = top_f[:, hcs, :].rearrange("p (h c) k -> p h c k", c=2)
                for c, (pos, dst) in enumerate(((best_a, pick1), (best_b, pick2))):
                    hot = onehot[:, ks, :]
                    s(dve.tensor_tensor(hot, pos[:, hs, :].rearrange("p h k -> p (h k)").unsqueeze(2).to_broadcast([128, n, 16]),
                                        cst[:, C_IOTA:C_IOTA + 16].unsqueeze(1).to_broadcast([128, n, 16]), ALU.is_equal))
                    hot4 = hot.rearrange("p (h k) a -> p h k a", h=2)
                    s(dve.tensor_tensor(hot4, hot4, keys[:, :, c, :].unsqueeze(2).to_broadcast([128, 2, TOPK, 16]), ALU.mult))
                    s(dve.tensor_reduce(dst[:, ks], hot, AX.X, ALU.add))
                    yield
                s(dve.scalar_tensor_tensor(pick1[:, ks], pick1[:, ks], float(PK), pick2[:, ks], ALU.mult, ALU.add))
                s(dve.tensor_scalar(expert[:, x, ks], pick1[:, ks], float(l * EXPERTS), None, ALU.add), dve_done, ("expert", l, t, q))
                g = pgate[:, x, ks].rearrange("p (h k) -> p h k", h=2)
                s(dve.tensor_tensor(g, best_v[:, hs, :], best_v[:, hs, 0:1].to_broadcast([128, 2, TOPK]), ALU.subtract),
                  dve_done, ("gate_in", l, t, q))

            def pick(l, t):
                for q in range(HPT[t] // 2):
                    yield from pick_quad(l, t, q)

            def normalise_gates(l, t):
                H, x = HPT[t], t % 2
                g = pgate[:, x, 0:H * TOPK].rearrange("p (h k) -> p h k", h=H)
                dve.wait_ge(*act_done.at(("gate_exp", l, t)))
                s(dve.tensor_reduce(stt2[:, 0:H], g, AX.X, ALU.add))
                s(dve.reciprocal(stt2[:, 8:8 + H], stt2[:, 0:H]))
                s(dve.tensor_tensor(g, g, spread(stt2[:, 8:8 + H], TOPK), ALU.mult))

            def dots(l, t, first, last):
                cols, base = pact[:, t % 2, :].rearrange("p (n k) -> p n k", k=PSLOTS), u_base(l, t)
                with dve.Fori(first, last, 1) as i:
                    for k in range(PSLOTS):
                        dve.wait_ge(gathered[k].sem, i * 16 + (base * 16 + 16))
                        dve.scalar_tensor_tensor(rows_buf[:, k, :], rows_buf[:, k, :], 1.0, u[:, t, :], ALU.mult, ALU.mult,
                                                 accum_out=cols[:, bass.ds(i, 1), k]).then_inc(slot_free[k].sem, 1)

            def gelu(l, t):
                x, n = t % 2, HPT[t] * TOPK
                for k in range(PSLOTS):
                    dve.wait_ge(slot_free[k].sem, v_base(l, t) + 1)
                a, q = pact[:, x, 0:n], ptmp[:, 0:n]
                s(dve.tensor_tensor(q, a, a, ALU.mult))
                s(dve.tensor_scalar(q, q, 0.044715, 1.0, ALU.mult, ALU.add))
                s(dve.tensor_tensor(q, q, a, ALU.mult), dve_done, ("gelu_in", l, t))
                s(dve.tensor_scalar(ptmp2[:, 0:n], a, 0.5, None, ALU.mult))
                s(dve.tensor_tensor(ptmp2[:, 0:n], ptmp2[:, 0:n], pgate[:, x, 0:n], ALU.mult))
                dve.wait_ge(*act_done.at(("gelu_tanh", l, t)))
                s(dve.scalar_tensor_tensor(coef[:, x, 0:n], q, 1.0, ptmp2[:, 0:n], ALU.add, ALU.mult), dve_done, ("coef", l, t))

            def sum_rows(l, t, beside=None, pace=1):
                x, base, rounds = t % 2, v_base(l, t), peer_rounds(t)
                cols = coef[:, x, :].rearrange("p (n k) -> p n k", k=PSLOTS)
                s(dve.memset(u[:, t, :], 0.0))

                def slots(first, last):
                    with dve.Fori(first, last, 1) as i:
                        for j, k in enumerate(VDVE[t]):
                            before = VDVE[t][j - 1]
                            dve.wait_ge(slot_free[before].sem, i + (base + (2 if j else 1)))
                            dve.wait_ge(gathered[k].sem, i * 16 + (base * 16 + 16))
                            dve.scalar_tensor_tensor(u[:, t, :], rows_buf[:, k, :], cols[:, bass.ds(i, 1), k], u[:, t, :],
                                                     ALU.mult, ALU.add).then_inc(slot_free[k].sem, 1)

                in_rounds(t, slots, beside, pace)
                dve.wait_ge(slot_free[VDVE[t][-1]].sem, base + rounds + 1)
                tell(("vsum", l, t))

            def take_peer(l, t):
                for n in range(2):
                    bank = filled(dve, ("peer", l, t, n))
                    freeing(dve.tensor_copy(h[0:ROWS[t], t, n * 512:(n + 1) * 512], bank[0:ROWS[t], :]), ("peer", l, t, n))
                tell(("h", "peer", l, t))

            def ffn(l):
                norm(f"ffn{l}", FFN_GAIN)
                s(dve.tensor_copy(u[64:128, 2, :], u[0:64, 2, :]))
                per_quad = peer_rounds(0) // 4
                advance(pick_quad(l, 0, 0))
                advance(pick_quad(l, 0, 1))
                for q in range(4):
                    following = pick_quad(l, 0, q + 2) if q < 2 else iter(())
                    for r in range(q * per_quad, (q + 1) * per_quad):
                        dots(l, 0, r, r + 1)
                        advance(following, 3)
                    advance(following)
                normalise_gates(l, 0)
                gelu(l, 0)
                for t in range(2):
                    following = pick(l, t + 1)
                    sum_rows(l, t, following, 3)
                    advance(following)
                    normalise_gates(l, t + 1)
                    take_peer(l, t)
                    if t == 0:
                        dots(l, 1, 0, peer_rounds(1))
                        gelu(l, 1)
                prompt = middle("P") if l == 0 else embed(1, "P")
                for r in range(peer_rounds(2)):
                    dots(l, 2, r, r + 1)
                    advance(prompt, BESIDE_U * (r + 1) // peer_rounds(2) - BESIDE_U * r // peer_rounds(2))
                gelu(l, 2)
                sum_rows(l, 2, prompt)
                advance(prompt)
                take_peer(l, 2)
                if l == 1:
                    advance(embed(1, "S"))

            def embed(l, group):
                tiles = GROUP_TILES[group]
                norm(f"ple{l}{group}", PLE_GAIN[l, group], tiles)
                yield
                for n in range(2):
                    for t in tiles:
                        R = ROWS[t]
                        gt = sgate[0:R, t, :]
                        dve.wait_ge(*freed((f"pgate{l}{group}", n, t)))
                        s(dve.tensor_scalar(gt, gt, 0.5, 0.5, ALU.mult, ALU.add))
                        bank = filled(dve, (f"pproj{l}", n, t))
                        freeing(dve.tensor_tensor(gt, gt, bank[0:R, :], ALU.mult), (f"pproj{l}", n, t))
                        hh = h[0:R, t, n * 512:(n + 1) * 512]
                        s(dve.tensor_tensor(hh, hh, gt, ALU.add), dve_done, ("ple", l, n, t))
                    yield

            def middle(group):
                tiles = GROUP_TILES[group]
                yield from embed(0, group)
                norm(f"kv{group}", KV_GAIN[group], tiles)
                yield
                yield
                yield
                norm(f"mix1{group}", MIX1_GAIN[group], tiles)
                yield
                yield
                yield
                yield
                if group == "P":
                    dve.wait_ge(qk_gain_in.sem, 32)
                    s(dve.tensor_scalar(gq, gq, 0.125, None, ALU.mult))
                for t in tiles:
                    dve.wait_ge(*act_done.at(("qsq", t)))
                    R = ROWS[t]
                    s(dve.tensor_reduce(qvar[0:R, t, 0:NQH], sq_q[group][0:R], AX.X, ALU.add))
                    s(dve.tensor_reduce(qvar[0:R, t, NQH:], sq_k[group][0:R], AX.X, ALU.add), dve_done, ("qsum", t))
                if group == "S":
                    s(dve.memset(qst, 0.0), dve_done, "qst_zero")
                yield
                for t in tiles:
                    yield from normalise_heads(group, t)

            def normalise_heads(group, t):
                R = ROWS[t]
                v = qvar[0:R, t, :]
                s(dve.tensor_scalar(v, v, 1.0 / 64, EPS, ALU.mult, ALU.add))
                rsqrt(qrstd[0:R, t, :], v, qtmp[0:R, t, :])
                for g in range(3):
                    src = q_raw[t][0:R, g * 512:(g + 1) * 512].rearrange("p (r j d) -> p r j d", r=2, j=4)
                    dst = qkn[t][0:R, 8 * g:8 * g + 8, :].rearrange("p (j r) d -> p r j d", r=2)
                    by = qrstd[0:R, t, 8 * g:8 * g + 8].rearrange("p (r j) -> p r j", r=2).unsqueeze(3).to_broadcast([R, 2, 4, 64])
                    s(dve.tensor_tensor(dst, src, by, ALU.mult))
                kk, qq = qkn[t][0:R, NQH:, :], qkn[t][0:R, 0:NQH, :]
                s(dve.tensor_tensor(kk, heads(kvs[0:R, t, 0:384]), spread(qrstd[0:R, t, NQH:], 64), ALU.mult))
                yield
                s(dve.tensor_tensor(qq, qq, repeat(gq[0:R, :], NQH), ALU.mult))
                s(dve.tensor_tensor(kk, kk, repeat(gk[0:R, :], NKH), ALU.mult))
                dve.wait_ge(angles_in.sem, 16)
                x1, x2 = qkn[t][0:R, :, 0:8], qkn[t][0:R, :, 8:16]
                cos, sin = repeat(angles[0:R, t, 0, :], 30), repeat(angles[0:R, t, 1, :], 30)
                at = rotary[group]
                r4 = [arena[0:R, at + 240 * i:at + 240 + 240 * i].rearrange("p (h f) -> p h f", h=30) for i in range(4)]
                s(dve.tensor_tensor(r4[0], x1, cos, ALU.mult))
                s(dve.tensor_tensor(r4[1], x2, sin, ALU.mult))
                s(dve.tensor_tensor(r4[2], x2, cos, ALU.mult))
                s(dve.tensor_tensor(r4[3], x1, sin, ALU.mult))
                s(dve.tensor_tensor(x1, r4[0], r4[1], ALU.subtract))
                s(dve.tensor_tensor(x2, r4[2], r4[3], ALU.add), dve_done, ("rope", t))
                yield

            for k in range(PSLOTS):
                dve.sem_inc(slot_free[k].sem, 1)
            add_to_h("out", 0)
            ffn(0)

            def prompt_max(t, hd):
                x, n = hd % 2, 384 * (t + 1)
                dve.wait_ge(*masks_in.at("P"))
                if hd >= 2:
                    for c in range(t + 1):
                        dve.wait_ge(*full_at(("pt", t, hd - 2, c)))
                at = 0
                for c in range(t + 1):
                    m = 384 if t == 0 else (512, 256)[c]
                    bank = filled(dve, ("s", t, hd, c))
                    freeing(dve.tensor_tensor(sm[:, x, at:at + m], bank[:, 0:m], pmask[t][:, at:at + m], ALU.add), ("s", t, hd, c))
                    at += m
                s(dve.tensor_reduce(negmax[:, x:x + 1], sm[:, x, 0:n], AX.X, ALU.max, negate=True), dve_done, ("max", t, hd))

            def prompt_out(t, hd):
                x = hd % 2
                dve.wait_ge(*act_done.at(("p", t, hd)))
                s(dve.reciprocal(rz[:, x:x + 1], zsum[:, hd % 4:hd % 4 + 1]))
                bank = filled(dve, ("o", t, hd))
                freeing(dve.tensor_scalar(osb[:, hd * 64:(hd + 1) * 64], bank[:, 0:64], rz[:, x:x + 1], None, ALU.mult), ("o", t, hd))

            samples = middle("S")
            for t in range(2):
                if t == 1:
                    dve.wait_ge(*full_at(("oT", 0)))
                for hd in range(10):
                    if hd < 8:
                        prompt_max(t, hd)
                    if hd >= 2:
                        prompt_out(t, hd - 2)
                    advance(samples, 1)
                tell(("osb", t))
            advance(samples)

            def sample_max(p):
                dve.wait_ge(*masks_in.at("S"))
                if p >= 1:
                    for c in range(4):
                        dve.wait_ge(*full_at(("spt", p - 1, c)))
                for c in range(4):
                    at, m = 512 * c, 512 if c < 3 else SCOLS - 1536
                    bank = filled(dve, ("ss", p, c))
                    freeing(dve.tensor_tensor(ssm[:, at:at + m], bank[:, 0:m], smask[:, at:at + m], ALU.add), ("ss", p, c))
                s(dve.tensor_reduce(negmax[:, 0:1], ssm, AX.X, ALU.max, negate=True), dve_done, ("smax", p))

            def sample_out(p):
                dve.wait_ge(*act_done.at(("sp", p)))
                s(dve.reciprocal(rz[:, 0:1], zsum[:, p % 4:p % 4 + 1]))
                bank = filled(dve, ("so", p))
                if p >= 1:
                    dve.wait_ge(*full_at(("soT", p - 1)))
                freeing(dve.tensor_scalar(so, bank[:, 0:128], rz[:, 0:1], None, ALU.mult), ("so", p))
                tell(("so", p))

            def sample_back(p):
                bank = filled(dve, ("soT", p))[:, 0:128].rearrange("p (b r c f i) -> p b r c f i", b=2, r=2, c=2, f=2)
                for r in range(2):
                    for f in range(2):
                        for c in range(2):
                            src = bank[64 * r:64 * r + 64, :, r, c, f, :]
                            dst = uT[64 * f:64 * f + 64, 2 * r + c, 256 + 16 * p:272 + 16 * p].rearrange("p (b i) -> p b i", b=2)
                            ins = dve.tensor_copy(dst, src)
                            if (r, f, c) == (1, 1, 1):
                                freeing(ins, ("soT", p))
                            else:
                                s(ins)
                tell(("oT", p))

            sample_max(0)
            for p in range(4):
                sample_out(p)
                if p + 1 < 4:
                    sample_max(p + 1)
                sample_back(p)
            add_to_h("wo", 1)
            ffn(1)

        @block.gpsimd
        def _(pool):
            s, freeing = stepper(pool, pool_order)
            for slot in range(4):
                s(pool.memset(raw[:, slot, 0:3], 0.0))
            for half in range(2):
                pool.wait_ge(*freed(("rows", half)))
            for b in range(CONV_BLKS):
                if b >= 4:
                    pool.wait_ge(*dve_done.at(("conv", b - 4)))
                q = raw[:, b % 4, 259:347].rearrange("p (b w) -> p b w", b=8)
                s(pool.tensor_copy(q[:, :, 0:3], stT[:, b, 0:24].rearrange("p (b w) -> p b w", b=8)), pool_done, ("rawstate", b))
                pool.wait_ge(*freed(("xbc", b)))
                s(pool.tensor_copy(newT[:, b, 0:3], raw[:, b % 4, 256:259]))
                s(pool.tensor_copy(newT[:, b, 3:27].rearrange("p (b w) -> p b w", b=8), q[:, :, 8:11]), pool_done, ("newrow", b))
            pool.wait_ge(*dve_done.at("scan_area"))
            pool.wait_ge(vec_in.sem, 48)
            for n in range(3 * GROUPS):
                t, g = divmod(n, GROUPS)
                R, x = ROWS[t], n % 2
                pool.wait_ge(*freed(("cum", t)))
                pool.wait_ge(*freed(("tok", g // 2, t)))
                if n >= 2:
                    tp, gp = divmod(n - 2, GROUPS)
                    pool.wait_ge(*full_at(("y", tp, gp)))
                    pool.wait_ge(*full_at(("state", tp, gp) if tp < 2 else ("hupd", 2 * gp + 1, 1)))
                    pool.wait_ge(*dve_done.at(("gated", tp, gp)))
                xg = heads(xs[0:R, t, g * 256:(g + 1) * 256])
                s(pool.tensor_tensor(heads(xdt[0:R, x, :]), xg, spread(dt[0:R, t, 4 * g:4 * g + 4], 64), ALU.mult))
                s(pool.tensor_tensor(heads(xdtt[0:R, x, :]), heads(xdt[0:R, x, :]),
                                     spread(ex[0:R, t, 32 + 4 * g:36 + 4 * g], 64), ALU.mult), pool_done, ("xdt", t, g))
                s(pool.tensor_tensor(heads(dxs[0:R, x, :]), xg, spread(d_bc[0:R, 4 * g:4 * g + 4], 64), ALU.mult),
                  pool_done, ("dxs", t, g))
                if t == 2:
                    if g >= 2:
                        pool.wait_ge(*full_at(("inter", 2, g - 2)))
                    c = ctm[:, g % 2, :, :]
                    diag = bass.AP(c.tensor, c.offset, [list(c.ap[0]), [72, 8], [1, 8]])
                    s(pool.tensor_copy(diag, bcT[:, 8 + g, 256:320].rearrange("p (b w) -> p b w", b=8)), pool_done, ("ctm", g))
                    pool.wait_ge(*freed("ec"))
                    for i in range(2):
                        blk = 2 * g + i
                        for q in range(2):
                            pool.wait_ge(*full_at(("h0T", blk, q)))
                        hh = h0[:, blk % 3, :, :]
                        s(pool.tensor_tensor(hh, hh, spread(ec[:, blk, :], 128), ALU.mult), pool_done, ("h0s", blk))

            tables = {which: I["peer_" + which].rearrange("l e d -> (l e) d") for which in "uv"}

            def gather(l, t, which, first=0, last=None):
                base = (u_base if which == "u" else v_base)(l, t)
                cols = expert[:, t % 2, :].rearrange("p (n k) -> p n k", k=PSLOTS)
                with pool.Fori(first, peer_rounds(t) if last is None else last, 1) as i:
                    for k in range(PSLOTS):
                        pool.wait_ge(slot_free[k].sem, i + (base + 1))
                        pool.tensor_copy(islot[:, k:k + 1], cols[:, bass.ds(i, 1), k]).then_inc(index_copied.sem, 1)
                        pool.wait_ge(index_copied.sem, i * PSLOTS + (base * PSLOTS + k + 1))
                        pool.nop(nofuse=True)
                        pool.indirect_dma_start(rows_buf[:, k, :], None, tables[which],
                                                bass.IndirectOffsetOnAxis(ap=islot[:, k:k + 1], axis=0))\
                            .then_inc(gathered[k].sem, 16)

            def ffn(l):
                for t in range(3):
                    quads = HPT[t] // 2
                    if t == 0:
                        for q in range(quads):
                            pool.wait_ge(*dve_done.at(("expert", l, t, q)))
                            gather(l, t, "u", q * peer_rounds(t) // quads, (q + 1) * peer_rounds(t) // quads)
                    else:
                        pool.wait_ge(*dve_done.at(("expert", l, t, quads - 1)))
                        gather(l, t, "u")
                    gather(l, t, "v")

            ffn(0)
            ffn(1)
    return counts


INPUTS = ["x_prompt", "x_sample", "state_conv", "state_ssm", "cache_k", "cache_v", "p_prompt", "p_sample",
          "norm_mix", "norm_ffn", "norm_ple", "ssm_w_in", "ssm_conv_w", "ssm_conv_b", "ssm_dt_bias", "ssm_a_log",
          "ssm_d", "ssm_norm", "ssm_w_out", "kv_norm", "w_kv", "k_norm", "w_q", "q_norm", "w_o",
          "peer_w_query", "peer_sub_keys", "peer_u", "peer_v", "ple_w_proj", "ple_w_gate"]
OUTPUTS = [("y_prompt", (1, 256, 1024)), ("y_sample", (8, 8, 1024)), ("prompt_conv", (1, 1, 3, 4096)),
           ("prompt_ssm", (1, 1, 32, 64, 128)), ("prompt_k", (1, 256, 6, 64)), ("prompt_v", (1, 256, 6, 64)),
           ("sample_conv", (1, 8, 3, 4096)), ("sample_ssm", (1, 8, 32, 64, 128)),
           ("sample_k", (8, 8, 6, 64)), ("sample_v", (8, 8, 6, 64))]


def kernel(**inputs):
    import concourse.bacc as bacc
    from concourse.bass_utils import run_bass_kernel_spmd

    arrays = {name: np.ascontiguousarray(inputs[name]) for name in INPUTS}
    arrays["constants"] = shape_constants()
    arrays["masks"] = attention_masks()
    arrays["angles"] = rotary_angles()

    def program(counts):
        nc = bacc.Bacc("TRN2", target_bir_lowering=False, num_devices=1)
        I = {n: nc.dram_tensor(n, a.shape, F32, kind="ExternalInput").ap() for n, a in arrays.items()}
        O = {n: nc.dram_tensor("out_" + n, shape, F32, kind="ExternalOutput").ap() for n, shape in OUTPUTS}
        I["w_in"], I["w_out"] = I["ssm_w_in"][0], I["ssm_w_out"][0]
        return nc, build(nc, I, O, counts)

    counts = program(None)[1]
    nc = program({k: dict(v) for k, v in counts.items()})[0]
    r = run_bass_kernel_spmd(nc, [arrays], core_ids=[0]).results[0]
    return tuple(r["out_" + n] for n, _ in OUTPUTS)
```
